# Optimizing a Trainium2 kernel written in Bass

```python
import math
import jax, jax.numpy as jnp
from jax import lax
import numpy as np

D_MODEL = 1024
BATCH = 1
SEQ = 512
DEPTH = 1

N_META = 16
RWKV_HEAD_DIM = 64
RWKV_HEADS = D_MODEL // RWKV_HEAD_DIM
RWKV_WIDTH = RWKV_HEADS * RWKV_HEAD_DIM
DECAY_LORA = 64
AAA_LORA = 64
GATE_LORA = 160
RWKV_LN_EPS = 64e-5
DIFF_HEAD_DIM = 64
DIFF_HEADS = D_MODEL // (2 * DIFF_HEAD_DIM)
DIFF_V_DIM = 2 * DIFF_HEAD_DIM
DIFF_QK_WIDTH = 2 * DIFF_HEADS * DIFF_HEAD_DIM
DIFF_V_WIDTH = DIFF_HEADS * DIFF_V_DIM
ROPE_THETA = 500000.0
ROPE_DIM = DIFF_HEAD_DIM // 4
D_FF = 4 * D_MODEL
N_BRANCH = 2
Q_BLOCK = 128
NORM_EPS = 1e-5
SUBLN_EPS = 1e-5

RWKV_COLS = 3 * RWKV_WIDTH + DECAY_LORA + AAA_LORA + GATE_LORA
DIFF_COLS = 2 * DIFF_QK_WIDTH + DIFF_V_WIDTH
GATE_COLS = N_BRANCH * D_MODEL
N_IN = RWKV_COLS + DIFF_COLS + GATE_COLS


def rms_norm(x, w, eps=NORM_EPS):
    xf = x.astype(jnp.float32)
    y = xf * lax.rsqrt(jnp.mean(xf * xf, axis=-1, keepdims=True) + eps)
    return (y * w.astype(jnp.float32)).astype(x.dtype)

def token_shift(p):
    return jnp.pad(p, ((0, 0), (1, 0), (0, 0)))[:, :-1]

def rwkv7_mix(p, mu, w0, w2, a0, a2, g2, k_k, k_a, r_k, ln_w, ln_b):
    f32 = jnp.float32
    bsz, seqlen, _ = p.shape
    p = p + (token_shift(p) - p) * mu
    c1 = RWKV_WIDTH
    c2 = 2 * RWKV_WIDTH
    c3 = 3 * RWKV_WIDTH
    c4 = c3 + DECAY_LORA
    c5 = c4 + AAA_LORA
    r, k, v, wd, ad, gd = jnp.split(p, [c1, c2, c3, c4, c5], axis=-1)
    w = -jax.nn.softplus(-(w0 + jnp.tanh(wd) @ w2).astype(f32)) - 0.5
    decay = jnp.exp(-jnp.exp(w))
    a = jax.nn.sigmoid((a0 + ad @ a2).astype(f32))
    g = jax.nn.sigmoid(gd) @ g2

    def heads(t):
        return t.astype(f32).reshape(bsz, seqlen, RWKV_HEADS, RWKV_HEAD_DIM)

    kk = heads(k * k_k)
    kk = kk / jnp.maximum(jnp.sqrt(jnp.sum(kk * kk, axis=-1, keepdims=True)), 1e-12)
    k = k.astype(f32) * (1.0 + (a - 1.0) * k_a.astype(f32))
    r_h, k_h, v_h, a_h, w_h = heads(r), heads(k), heads(v), heads(a), heads(decay)

    def tm(t):
        return jnp.moveaxis(t, 1, 0)

    xs = (tm(r_h), tm(w_h), tm(k_h), tm(v_h), tm(-kk), tm(kk * a_h))

    def step(S, inp):
        rt, wt, kt, vt, at, bt = inp
        sa = jnp.einsum('bhvk,bhk->bhv', S, at)
        S = S * wt[:, :, None, :] + sa[..., None] * bt[:, :, None, :] + vt[..., None] * kt[:, :, None, :]
        y = jnp.einsum('bhvk,bhk->bhv', S, rt)
        return S, y

    S0 = jnp.zeros((bsz, RWKV_HEADS, RWKV_HEAD_DIM, RWKV_HEAD_DIM), f32)
    _, ys = lax.scan(step, S0, xs)
    y = jnp.moveaxis(ys, 0, 1)
    mean = jnp.mean(y, axis=-1, keepdims=True)
    var = jnp.mean(jnp.square(y - mean), axis=-1, keepdims=True)
    y = (y - mean) * lax.rsqrt(var + RWKV_LN_EPS)
    y = y.reshape(bsz, seqlen, RWKV_WIDTH) * ln_w.astype(f32) + ln_b.astype(f32)
    bonus = jnp.sum(r_h * k_h * r_k.astype(f32), axis=-1, keepdims=True) * v_h
    y = y + bonus.reshape(bsz, seqlen, RWKV_WIDTH)
    return (y * g.astype(f32)).astype(p.dtype)

def partial_rope(x, pos):
    half = ROPE_DIM // 2
    inv = ROPE_THETA ** (-jnp.arange(0, ROPE_DIM, 2, dtype=jnp.float32) / ROPE_DIM)
    ang = pos.astype(jnp.float32)[:, None] * inv[None, :]
    cos = jnp.cos(ang)[None, :, None, :]
    sin = jnp.sin(ang)[None, :, None, :]
    x1 = x[..., :half].astype(jnp.float32)
    x2 = x[..., half:ROPE_DIM].astype(jnp.float32)
    rot = jnp.concatenate([x1 * cos - x2 * sin, x2 * cos + x1 * sin], axis=-1).astype(x.dtype)
    return jnp.concatenate([rot, x[..., ROPE_DIM:]], axis=-1)

def diff_attention(p, lq1, lk1, lq2, lk2, subln_w, lambda_init):
    f32 = jnp.float32
    bsz, seqlen, _ = p.shape
    q, k, v = jnp.split(p, [DIFF_QK_WIDTH, 2 * DIFF_QK_WIDTH], axis=-1)
    pos = jnp.arange(seqlen)
    q = partial_rope(q.reshape(bsz, seqlen, 2 * DIFF_HEADS, DIFF_HEAD_DIM), pos)
    k = partial_rope(k.reshape(bsz, seqlen, 2 * DIFF_HEADS, DIFF_HEAD_DIM), pos)
    q = jnp.transpose(q, (0, 2, 1, 3)) * (DIFF_HEAD_DIM ** -0.5)
    k = jnp.transpose(k, (0, 2, 1, 3))
    v = jnp.transpose(v.reshape(bsz, seqlen, DIFF_HEADS, DIFF_V_DIM), (0, 2, 1, 3))
    lam = (jnp.exp(jnp.sum(lq1.astype(f32) * lk1.astype(f32)))
           - jnp.exp(jnp.sum(lq2.astype(f32) * lk2.astype(f32))) + lambda_init)
    neg = jnp.finfo(f32).min

    def attend(qb, qpos):
        nq = qb.shape[2]
        s = jnp.einsum('bhqd,bhkd->bhqk', qb, k, preferred_element_type=f32)
        s = jnp.where(pos[None, :] <= qpos[:, None], s, neg)
        pr = jax.nn.softmax(s, axis=-1).reshape(bsz, DIFF_HEADS, 2, nq, seqlen)
        attn_w = pr[:, :, 0] - lam * pr[:, :, 1]
        return jnp.einsum('bhqk,bhkd->bhqd', attn_w.astype(v.dtype), v)

    meta_out = attend(q[:, :, :N_META], pos[:N_META])
    n_blk = (seqlen - N_META) // Q_BLOCK

    def blk(i):
        start = N_META + i * Q_BLOCK
        qb = lax.dynamic_slice_in_dim(q, start, Q_BLOCK, axis=2)
        return attend(qb, start + jnp.arange(Q_BLOCK))

    outs = lax.map(blk, jnp.arange(n_blk))
    outs = jnp.transpose(outs, (1, 2, 0, 3, 4)).reshape(bsz, DIFF_HEADS, n_blk * Q_BLOCK, DIFF_V_DIM)
    o = jnp.concatenate([meta_out, outs], axis=2)
    o = rms_norm(o, subln_w, SUBLN_EPS) * (1.0 - lambda_init)
    return jnp.transpose(o, (0, 2, 1, 3)).reshape(bsz, seqlen, DIFF_V_WIDTH)

def first_inputs(seed: int = 0) -> dict:
    key = jax.random.key(seed)
    ks = jax.random.split(key, 32)
    f32 = jnp.float32

    def nrm(k, shape, scale):
        return jax.random.normal(k, shape, f32) * scale

    L = DEPTH
    return {
        "x": nrm(ks[0], (BATCH, SEQ, D_MODEL), 1.0),
        "meta_tokens": nrm(ks[1], (N_META, D_MODEL), 1.0),
        "norm_mix_w": 1.0 + nrm(ks[2], (L, D_MODEL), 0.02),
        "w_in": nrm(ks[3], (L, D_MODEL, N_IN), D_MODEL ** -0.5),
        "rwkv_mu": jax.random.uniform(ks[4], (L, RWKV_COLS), f32, 0.0, 1.0),
        "rwkv_w0": jax.random.uniform(ks[5], (L, RWKV_WIDTH), f32, -6.5, -1.5),
        "rwkv_w2": nrm(ks[6], (L, DECAY_LORA, RWKV_WIDTH), 0.1 * DECAY_LORA ** -0.5),
        "rwkv_a0": nrm(ks[7], (L, RWKV_WIDTH), 0.01),
        "rwkv_a2": nrm(ks[8], (L, AAA_LORA, RWKV_WIDTH), 0.5 * AAA_LORA ** -0.5),
        "rwkv_g2": nrm(ks[9], (L, GATE_LORA, RWKV_WIDTH), GATE_LORA ** -0.5),
        "rwkv_k_k": 0.85 + nrm(ks[10], (L, RWKV_WIDTH), 0.02),
        "rwkv_k_a": 1.0 + nrm(ks[11], (L, RWKV_WIDTH), 0.02),
        "rwkv_r_k": nrm(ks[12], (L, RWKV_HEADS, RWKV_HEAD_DIM), 0.1),
        "rwkv_ln_w": 1.0 + nrm(ks[13], (L, RWKV_WIDTH), 0.02),
        "rwkv_ln_b": nrm(ks[14], (L, RWKV_WIDTH), 0.01),
        "rwkv_w_o": nrm(ks[15], (L, RWKV_WIDTH, D_MODEL), RWKV_WIDTH ** -0.5),
        "diff_lq1": nrm(ks[16], (L, DIFF_HEAD_DIM), 0.1),
        "diff_lk1": nrm(ks[17], (L, DIFF_HEAD_DIM), 0.1),
        "diff_lq2": nrm(ks[18], (L, DIFF_HEAD_DIM), 0.1),
        "diff_lk2": nrm(ks[19], (L, DIFF_HEAD_DIM), 0.1),
        "diff_subln_w": 1.0 + nrm(ks[20], (L, DIFF_V_DIM), 0.02),
        "diff_w_o": nrm(ks[21], (L, DIFF_V_WIDTH, D_MODEL), DIFF_V_WIDTH ** -0.5),
        "w_out": nrm(ks[22], (L, D_MODEL, D_MODEL), D_MODEL ** -0.5),
        "norm_mlp_w": 1.0 + nrm(ks[23], (L, D_MODEL), 0.02),
        "mlp_w1": nrm(ks[24], (L, D_MODEL, D_FF), D_MODEL ** -0.5),
        "mlp_w2": nrm(ks[25], (L, D_FF, D_MODEL), D_FF ** -0.5),
        "final_norm_w": 1.0 + nrm(ks[26], (D_MODEL,), 0.02),
    }

def first_block(x, meta_tokens, norm_mix_w, w_in, rwkv_mu, rwkv_w0, rwkv_w2, rwkv_a0, rwkv_a2, rwkv_g2,
              rwkv_k_k, rwkv_k_a, rwkv_r_k, rwkv_ln_w, rwkv_ln_b, rwkv_w_o, diff_lq1, diff_lk1, diff_lq2,
              diff_lk2, diff_subln_w, diff_w_o, w_out, norm_mlp_w, mlp_w1, mlp_w2, final_norm_w):
    bsz = x.shape[0]
    meta = jnp.broadcast_to(meta_tokens[None].astype(x.dtype), (bsz, N_META, D_MODEL))
    h_res = jnp.concatenate([meta, x], axis=1)
    seqlen = h_res.shape[1]
    for layer in range(DEPTH):
        lambda_init = 0.8 - 0.6 * math.exp(-0.3 * layer)
        h = rms_norm(h_res, norm_mix_w[layer])
        proj = h @ w_in[layer]
        p_rwkv, p_diff, p_gate = jnp.split(proj, [RWKV_COLS, RWKV_COLS + DIFF_COLS], axis=-1)
        o_rwkv = rwkv7_mix(p_rwkv, rwkv_mu[layer], rwkv_w0[layer], rwkv_w2[layer], rwkv_a0[layer],
                           rwkv_a2[layer], rwkv_g2[layer], rwkv_k_k[layer], rwkv_k_a[layer],
                           rwkv_r_k[layer], rwkv_ln_w[layer], rwkv_ln_b[layer]) @ rwkv_w_o[layer]
        o_diff = diff_attention(p_diff, diff_lq1[layer], diff_lk1[layer], diff_lq2[layer],
                                diff_lk2[layer], diff_subln_w[layer], lambda_init) @ diff_w_o[layer]
        gates = jax.nn.sigmoid(p_gate).reshape(bsz, seqlen, N_BRANCH, D_MODEL)
        merged = gates[:, :, 0] * o_rwkv + gates[:, :, 1] * o_diff
        h_res = h_res + merged @ w_out[layer]
        h = rms_norm(h_res, norm_mlp_w[layer])
        h_res = h_res + jnp.square(jax.nn.relu(h @ mlp_w1[layer])) @ mlp_w2[layer]
    out = rms_norm(h_res, final_norm_w)
    return out[:, N_META:]


_first_inputs = first_inputs


def first_inputs(seed=0):
    import zlib

    import numpy as np

    out = dict(_first_inputs(seed))
    spreads = {}
    factors = {'norm_mix_w': 2.945,
     'rwkv_w2': 37.606,
     'rwkv_a0': 8.0,
     'rwkv_k_k': 64.0,
     'rwkv_k_a': 8.0,
     'rwkv_ln_w': 64.0,
     'rwkv_ln_b': 64.0,
     'diff_subln_w': 56.6,
     'norm_mlp_w': 12.365,
     'final_norm_w': 7.86}
    for name, (base, spread) in spreads.items():
        noise = np.random.default_rng([zlib.crc32(name.encode()), seed]).standard_normal(out[name].shape)
        drawn = base * np.exp(spread * noise) if base else spread * noise
        out[name] = __import__('jax').numpy.asarray(drawn.astype(out[name].dtype))
    for name, factor in factors.items():
        out[name] = (out[name] * factor).astype(out[name].dtype)
    return out


_narrow_inputs = first_inputs


def first_inputs(seed=0):

    out = dict(_narrow_inputs(seed))
    wider = {'rwkv_k_k': 10.01,
     'rwkv_k_a': 3.04,
     'rwkv_ln_w': 4.31,
     'rwkv_ln_b': 9.11,
     'diff_subln_w': 4.1,
     'final_norm_w': 3.15}
    for name, times in wider.items():
        mean = out[name].mean()
        out[name] = (mean + times * (out[name] - mean)).astype(out[name].dtype)
    return out


PLE_DIM = 256
N_HEADS = 8
HEAD_DIM = 64
N_KV_HEADS = 2
HEADS_PER_GROUP = N_HEADS // N_KV_HEADS
L_CMP = 32
D_STRIDE = 16
CMP_HIDDEN = 256
L_SLC = 64
N_SEL = 16
WINDOW = 512
N_BUCKETS = 32
MAX_EXACT = N_BUCKETS // 2
MAX_DISTANCE = 128
D_CONV = D_MODEL // 2
CONV_WIDTH = 31
D_FF_2 = 2816
FFN_CONV_WIDTH = 3

EPS = 1e-6
NEG = -1e30
FORCE = 1e4

N_CONV_IN = 2 * D_CONV
N_Q = N_HEADS * HEAD_DIM
N_KV = 6 * N_KV_HEADS * HEAD_DIM
N_NSA_GATE = 3 * N_HEADS
N_MERGE = 2 * D_MODEL
N_IN_2 = N_CONV_IN + N_Q + N_KV + N_NSA_GATE + N_MERGE


def rmsnorm(x, g):
    xf = x.astype(jnp.float32)
    y = xf * lax.rsqrt(jnp.mean(xf * xf, axis=-1, keepdims=True) + EPS)
    return (y * g.astype(jnp.float32)).astype(x.dtype)

def layernorm(x, g, b):
    xf = x.astype(jnp.float32)
    mu = jnp.mean(xf, axis=-1, keepdims=True)
    var = jnp.mean(jnp.square(xf - mu), axis=-1, keepdims=True)
    y = (xf - mu) * lax.rsqrt(var + EPS)
    return (y * g.astype(jnp.float32) + b.astype(jnp.float32)).astype(x.dtype)

def causal_dwconv(x, w, b):
    k, c = w.shape
    y = lax.conv_general_dilated(x, w[:, None, :].astype(x.dtype), (1,), [(k - 1, 0)],
                                 dimension_numbers=('NWC', 'WIO', 'NWC'),
                                 feature_group_count=c)
    return y + b.astype(x.dtype)

def t5_bucket(dist):
    n = jnp.maximum(dist, 0)
    nf = jnp.maximum(n, MAX_EXACT).astype(jnp.float32)
    large = MAX_EXACT + (jnp.log(nf / MAX_EXACT) / math.log(MAX_DISTANCE / MAX_EXACT)
                         * (N_BUCKETS - MAX_EXACT)).astype(jnp.int32)
    large = jnp.minimum(large, N_BUCKETS - 1)
    return jnp.where(n < MAX_EXACT, n, large)

def masked_softmax(s, mask):
    p = jax.nn.softmax(jnp.where(mask, s, NEG), axis=-1)
    return jnp.where(mask, p, 0.0)

def compress(kv, pe, w1, w2):
    b, s, g, dh = kv.shape
    nc = (s - L_CMP) // D_STRIDE + 1
    idx = jnp.arange(nc)[:, None] * D_STRIDE + jnp.arange(L_CMP)[None, :]
    blocks = kv[:, idx] + pe[None, None, :, None, :]
    blocks = blocks.transpose(0, 1, 3, 2, 4).reshape(b, nc, g, L_CMP * dh)
    return jax.nn.gelu(blocks @ w1) @ w2

def nsa_attention(q, k_cmp, v_cmp, k_slc, v_slc, k_win, v_win, gates, rel_bias):
    b, s, g, hpg, dh = q.shape
    nc = k_cmp.shape[1]
    ns = s // L_SLC
    n_sel = min(N_SEL, ns)
    nqb = s // Q_BLOCK
    scale = 1.0 / math.sqrt(dh)

    c_start = jnp.arange(nc) * D_STRIDE
    c_end = c_start + L_CMP - 1
    s_start = jnp.arange(ns) * L_SLC
    agg = ((c_end[:, None] >= s_start[None, :]) &
           (c_start[:, None] <= s_start[None, :] + L_SLC - 1)).astype(jnp.float32)

    k_blocks = k_slc.reshape(b, ns, L_SLC, g, dh).transpose(0, 3, 1, 2, 4)
    v_blocks = v_slc.reshape(b, ns, L_SLC, g, dh).transpose(0, 3, 1, 2, 4)
    k_pad = jnp.pad(k_win, ((0, 0), (WINDOW, 0), (0, 0), (0, 0)))
    v_pad = jnp.pad(v_win, ((0, 0), (WINDOW, 0), (0, 0), (0, 0)))
    bias_grouped = rel_bias.reshape(N_BUCKETS, g, hpg).transpose(1, 0, 2)
    bi = jnp.arange(b)[:, None, None, None]
    gi = jnp.arange(g)[None, :, None, None]

    def head_bias(dist):
        bb = rel_bias[t5_bucket(dist)].astype(jnp.float32)
        return bb.reshape(dist.shape + (g, hpg)).transpose(2, 3, 0, 1)

    def block(qi):
        t0 = qi * Q_BLOCK
        qb = lax.dynamic_slice_in_dim(q, t0, Q_BLOCK, axis=1)
        gb = lax.dynamic_slice_in_dim(gates, t0, Q_BLOCK, axis=1)
        tpos = t0 + jnp.arange(Q_BLOCK)

        dist_c = tpos[:, None] - c_end[None, :]
        s_c = jnp.einsum('bqghd,bcgd->bghqc', qb, k_cmp).astype(jnp.float32) * scale
        p_c = masked_softmax(s_c + head_bias(dist_c), dist_c >= 0)
        o_c = jnp.einsum('bghqc,bcgd->bqghd', p_c.astype(v_cmp.dtype), v_cmp)

        imp = jnp.einsum('bghqc,cs->bgqs', p_c, agg)
        blk = jnp.arange(ns)[None, :]
        cur = (tpos // L_SLC)[:, None]
        valid = blk * L_SLC <= tpos[:, None]
        forced = (blk == 0) | (blk == cur) | (blk == cur - 1)
        imp = jnp.where(forced, FORCE, jnp.where(valid, imp, -FORCE))
        _, idx = lax.top_k(imp, n_sel)
        kb = k_blocks[bi, gi, idx].reshape(b, g, Q_BLOCK, n_sel * L_SLC, dh)
        vb = v_blocks[bi, gi, idx].reshape(b, g, Q_BLOCK, n_sel * L_SLC, dh)
        kpos = (idx[..., None] * L_SLC + jnp.arange(L_SLC)).reshape(b, g, Q_BLOCK, n_sel * L_SLC)
        dist_s = tpos[None, None, :, None] - kpos
        bias_s = bias_grouped[gi, t5_bucket(dist_s)].astype(jnp.float32).transpose(0, 1, 4, 2, 3)
        s_s = jnp.einsum('bqghd,bgqkd->bghqk', qb, kb).astype(jnp.float32) * scale + bias_s
        p_s = masked_softmax(s_s, (dist_s >= 0)[:, :, None])
        o_s = jnp.einsum('bghqk,bgqkd->bqghd', p_s.astype(vb.dtype), vb)

        kw = lax.dynamic_slice_in_dim(k_pad, t0, Q_BLOCK + WINDOW, axis=1)
        vw = lax.dynamic_slice_in_dim(v_pad, t0, Q_BLOCK + WINDOW, axis=1)
        kwpos = t0 - WINDOW + jnp.arange(Q_BLOCK + WINDOW)
        dist_w = tpos[:, None] - kwpos[None, :]
        mask_w = (dist_w >= 0) & (dist_w < WINDOW) & (kwpos[None, :] >= 0)
        s_w = jnp.einsum('bqghd,bkgd->bghqk', qb, kw).astype(jnp.float32) * scale
        p_w = masked_softmax(s_w + head_bias(dist_w), mask_w)
        o_w = jnp.einsum('bghqk,bkgd->bqghd', p_w.astype(vw.dtype), vw)

        return gb[..., 0:1] * o_c + gb[..., 1:2] * o_s + gb[..., 2:3] * o_w

    out = lax.map(block, jnp.arange(nqb))
    return jnp.moveaxis(out, 0, 1).reshape(b, s, g * hpg * dh)

def second_inputs(seed: int = 0) -> dict:
    key = jax.random.key(seed)
    ks = jax.random.split(key, 27)
    f32 = jnp.float32

    def nrm(k, shape, scale):
        return jax.random.normal(k, shape, f32) * scale

    def gain(k, shape):
        return 1.0 + 0.01 * jax.random.normal(k, shape, f32)

    L = DEPTH
    return {
        "x": nrm(ks[0], (BATCH, SEQ, D_MODEL), 1.0),
        "p": nrm(ks[1], (DEPTH, BATCH, SEQ, PLE_DIM), 1.0),
        "rel_bias": nrm(ks[2], (N_BUCKETS, N_HEADS), 0.1),
        "norm_mix": gain(ks[3], (L, D_MODEL)),
        "w_in": nrm(ks[4], (L, D_MODEL, N_IN_2), D_MODEL ** -0.5),
        "conv_dw_w": nrm(ks[5], (L, CONV_WIDTH, D_CONV), CONV_WIDTH ** -0.5),
        "conv_dw_b": nrm(ks[6], (L, D_CONV), 0.01),
        "conv_ln_g": gain(ks[7], (L, D_CONV)),
        "conv_ln_b": nrm(ks[8], (L, D_CONV), 0.01),
        "w_conv_out": nrm(ks[9], (L, D_CONV, D_MODEL), D_CONV ** -0.5),
        "cmp_pe_k": nrm(ks[10], (L, L_CMP, HEAD_DIM), 0.1),
        "cmp_pe_v": nrm(ks[11], (L, L_CMP, HEAD_DIM), 0.1),
        "w_ck1": nrm(ks[12], (L, L_CMP * HEAD_DIM, CMP_HIDDEN), (L_CMP * HEAD_DIM) ** -0.5),
        "w_ck2": nrm(ks[13], (L, CMP_HIDDEN, HEAD_DIM), CMP_HIDDEN ** -0.5),
        "w_cv1": nrm(ks[14], (L, L_CMP * HEAD_DIM, CMP_HIDDEN), (L_CMP * HEAD_DIM) ** -0.5),
        "w_cv2": nrm(ks[15], (L, CMP_HIDDEN, HEAD_DIM), CMP_HIDDEN ** -0.5),
        "w_attn_out": nrm(ks[16], (L, N_HEADS * HEAD_DIM, D_MODEL), (N_HEADS * HEAD_DIM) ** -0.5),
        "w_out": nrm(ks[17], (L, D_MODEL, D_MODEL), D_MODEL ** -0.5),
        "norm_ffn": gain(ks[18], (L, D_MODEL)),
        "w_up": nrm(ks[19], (L, D_MODEL, 2 * D_FF_2), D_MODEL ** -0.5),
        "ffn_dw_w": nrm(ks[20], (L, FFN_CONV_WIDTH, 2 * D_FF_2), FFN_CONV_WIDTH ** -0.5),
        "ffn_dw_b": nrm(ks[21], (L, 2 * D_FF_2), 0.01),
        "w_down": nrm(ks[22], (L, D_FF_2, D_MODEL), D_FF_2 ** -0.5),
        "norm_ple": gain(ks[23], (L, D_MODEL)),
        "w_ple_gate": nrm(ks[24], (L, D_MODEL, D_MODEL), D_MODEL ** -0.5),
        "w_ple": nrm(ks[25], (L, PLE_DIM, D_MODEL), PLE_DIM ** -0.5),
        "norm_final": gain(ks[26], (D_MODEL,)),
    }

def second_block(x, p, rel_bias, norm_mix, w_in, conv_dw_w, conv_dw_b, conv_ln_g, conv_ln_b,
              w_conv_out, cmp_pe_k, cmp_pe_v, w_ck1, w_ck2, w_cv1, w_cv2, w_attn_out, w_out,
              norm_ffn, w_up, ffn_dw_w, ffn_dw_b, w_down, norm_ple, w_ple_gate, w_ple, norm_final):
    b, s, d = x.shape
    g, hpg, dh = N_KV_HEADS, HEADS_PER_GROUP, HEAD_DIM
    splits = [N_CONV_IN, N_CONV_IN + N_Q, N_CONV_IN + N_Q + N_KV,
              N_CONV_IN + N_Q + N_KV + N_NSA_GATE]
    for i in range(DEPTH):
        h = rmsnorm(x, norm_mix[i])
        z = h @ w_in[i]
        u, qf, kvf, ng, mg = jnp.split(z, splits, axis=-1)

        a = u[..., :D_CONV] * jax.nn.sigmoid(u[..., D_CONV:])
        a = causal_dwconv(a, conv_dw_w[i], conv_dw_b[i])
        a = jax.nn.silu(layernorm(a, conv_ln_g[i], conv_ln_b[i]))
        y_conv = a @ w_conv_out[i]

        q = qf.reshape(b, s, g, hpg, dh)
        kv = kvf.reshape(b, s, 6, g, dh)
        k_c, v_c, k_s, v_s, k_w, v_w = (kv[:, :, 0], kv[:, :, 1], kv[:, :, 2],
                                        kv[:, :, 3], kv[:, :, 4], kv[:, :, 5])
        k_cmp = compress(k_c, cmp_pe_k[i], w_ck1[i], w_ck2[i])
        v_cmp = compress(v_c, cmp_pe_v[i], w_cv1[i], w_cv2[i])
        nsa_gates = jax.nn.sigmoid(ng).reshape(b, s, g, hpg, 3)
        o = nsa_attention(q, k_cmp, v_cmp, k_s, v_s, k_w, v_w, nsa_gates, rel_bias)
        y_attn = o @ w_attn_out[i]

        y = jax.nn.sigmoid(mg[..., :d]) * y_conv + jax.nn.sigmoid(mg[..., d:]) * y_attn
        x = x + y @ w_out[i]

        hf = rmsnorm(x, norm_ffn[i])
        up = causal_dwconv(hf @ w_up[i], ffn_dw_w[i], ffn_dw_b[i])
        gate, val = jnp.split(up, 2, axis=-1)
        x = x + (jax.nn.gelu(gate) * val) @ w_down[i]

        pg = jax.nn.sigmoid(rmsnorm(x, norm_ple[i]) @ w_ple_gate[i])
        x = x + pg * (p[i] @ w_ple[i])
    return rmsnorm(x, norm_final)


_first_inputs_2 = second_inputs


def second_inputs(seed=0):
    import zlib

    import numpy as np

    out = dict(_first_inputs_2(seed))
    spreads = {}
    factors = {'rel_bias': 8.0,
     'norm_mix': 8.0,
     'conv_dw_b': 8.0,
     'conv_ln_g': 8.0,
     'conv_ln_b': 8.0,
     'cmp_pe_k': 8.0,
     'cmp_pe_v': 3.595,
     'norm_ffn': 8.0,
     'ffn_dw_b': 7.92,
     'norm_ple': 8.0,
     'norm_final': 5.586}
    for name, (base, spread) in spreads.items():
        noise = np.random.default_rng([zlib.crc32(name.encode()), seed]).standard_normal(out[name].shape)
        drawn = base * np.exp(spread * noise) if base else spread * noise
        out[name] = __import__('jax').numpy.asarray(drawn.astype(out[name].dtype))
    for name, factor in factors.items():
        out[name] = (out[name] * factor).astype(out[name].dtype)
    return out


_narrow_inputs_2 = second_inputs


def second_inputs(seed=0):

    out = dict(_narrow_inputs_2(seed))
    wider = {'p': 4.25,
     'conv_dw_b': 4.59,
     'conv_ln_g': 7.93,
     'conv_ln_b': 8.03,
     'norm_ffn': 4.68,
     'ffn_dw_b': 4.41,
     'norm_ple': 12.0,
     'w_ple_gate': 6.38,
     'w_ple': 4.24,
     'norm_final': 6.3}
    for name, times in wider.items():
        mean = out[name].mean()
        out[name] = (mean + times * (out[name] - mean)).astype(out[name].dtype)
    return out


N_HEADS_3 = 4
HEAD_DIM_3 = D_MODEL // 8
MIX_W = N_HEADS_3 * HEAD_DIM_3
N_BRANCH_3 = 3
CHUNK = 64
GLA_RANK = 16
GLA_TAU = 16
CONV_K = 4
D_FF_3 = 4 * D_MODEL


def _in_sizes():
    H, W = N_HEADS_3, MIX_W
    return [W, W, W, W, H, H,
            W, W, W, W, GLA_RANK,
            W, W, W, W, H, H,
            N_BRANCH_3 * D_MODEL]

def rmsnorm_3(x, g):
    x32 = x.astype(jnp.float32)
    y = x32 * lax.rsqrt(jnp.mean(x32 * x32, axis=-1, keepdims=True) + EPS)
    return (y * g.astype(jnp.float32)).astype(x.dtype)

def head_rmsnorm(h, g):
    B_, S_, _ = h.shape
    hh = h.reshape(B_, S_, N_HEADS_3, HEAD_DIM_3)
    hh = hh * lax.rsqrt(jnp.mean(hh * hh, axis=-1, keepdims=True) + EPS)
    return hh.reshape(B_, S_, MIX_W) * g.astype(jnp.float32)

def l2norm_heads(h):
    B_, S_, _ = h.shape
    hh = h.reshape(B_, S_, N_HEADS_3, HEAD_DIM_3)
    hh = hh * lax.rsqrt(jnp.sum(hh * hh, axis=-1, keepdims=True) + EPS)
    return hh.reshape(B_, S_, MIX_W)

def to_chunks(t):
    B_, S_, HD = t.shape
    t = t.reshape(B_, S_ // CHUNK, CHUNK, N_HEADS_3, HD // N_HEADS_3)
    return t.transpose(1, 0, 3, 2, 4)

def scalar_chunks(t):
    B_, S_, H_ = t.shape
    return t.reshape(B_, S_ // CHUNK, CHUNK, H_).transpose(1, 0, 3, 2)

def from_chunks(t):
    NC, B_, H_, L_, d = t.shape
    return t.transpose(1, 0, 3, 2, 4).reshape(B_, NC * L_, H_ * d)

def causal_conv(x, w):
    K = w.shape[0]
    xp = jnp.pad(x, ((0, 0), (K - 1, 0), (0, 0)))
    return lax.conv_general_dilated(xp, w[:, None, :], window_strides=(1,), padding='VALID',
                                    dimension_numbers=('NWC', 'WIO', 'NWC'),
                                    feature_group_count=x.shape[-1])

def mlstm_chunk(carry, xs):
    C, n, m = carry
    q, k, v, li, lf = xs
    causal = jnp.tril(jnp.ones((CHUNK, CHUNK), dtype=bool))
    b = jnp.cumsum(lf, axis=-1)
    D = jnp.where(causal, b[..., :, None] - b[..., None, :] + li[..., None, :], -jnp.inf)
    inter = b + m[..., None]
    m_t = jnp.maximum(inter, jnp.max(D, axis=-1))
    P = jnp.exp(D - m_t[..., None]) * jnp.einsum('bhtk,bhsk->bhts', q, k)
    w_inter = jnp.exp(inter - m_t)
    num = jnp.einsum('bhts,bhsv->bhtv', P, v) + w_inter[..., None] * jnp.einsum('bhtk,bhkv->bhtv', q, C)
    den = jnp.sum(P, axis=-1) + w_inter * jnp.einsum('bhtk,bhk->bht', q, n)
    h = num / jnp.maximum(jnp.abs(den), jnp.exp(-m_t))[..., None]
    bL = b[..., -1]
    g_s = bL[..., None] - b + li
    m_new = jnp.maximum(bL + m, jnp.max(g_s, axis=-1))
    w_s = jnp.exp(g_s - m_new[..., None])
    w_old = jnp.exp(bL + m - m_new)
    C = w_old[..., None, None] * C + jnp.einsum('bhsk,bhsv->bhkv', k * w_s[..., None], v)
    n = w_old[..., None] * n + jnp.einsum('bhs,bhsk->bhk', w_s, k)
    return (C, n, m_new), h

def mlstm(q, k, v, li, lf):
    B_ = q.shape[0]
    init = (jnp.zeros((B_, N_HEADS_3, HEAD_DIM_3, HEAD_DIM_3), jnp.float32),
            jnp.zeros((B_, N_HEADS_3, HEAD_DIM_3), jnp.float32),
            jnp.zeros((B_, N_HEADS_3), jnp.float32))
    xs = (to_chunks(q * HEAD_DIM_3 ** -0.5), to_chunks(k), to_chunks(v), scalar_chunks(li), scalar_chunks(lf))
    _, hs = lax.scan(mlstm_chunk, init, xs)
    return from_chunks(hs)

def gla_chunk(S, xs):
    q, k, v, g = xs
    causal = jnp.tril(jnp.ones((CHUNK, CHUNK), dtype=bool))
    b = jnp.cumsum(g, axis=2)
    diff = b[:, :, :, None, :] - b[:, :, None, :, :]
    decay = jnp.exp(jnp.where(causal[:, :, None], diff, -jnp.inf))
    A = jnp.einsum('bhtsk,bhsk->bhts', q[:, :, :, None, :] * decay, k)
    o = jnp.einsum('bhts,bhsv->bhtv', A, v) + jnp.einsum('bhtk,bhkv->bhtv', q * jnp.exp(b), S)
    bL = b[:, :, -1:, :]
    S = jnp.exp(bL[:, :, 0, :])[..., None] * S + jnp.einsum('bhsk,bhsv->bhkv', k * jnp.exp(bL - b), v)
    return S, o

def gla(q, k, v, g):
    B_ = q.shape[0]
    init = jnp.zeros((B_, N_HEADS_3, HEAD_DIM_3, HEAD_DIM_3), jnp.float32)
    xs = (to_chunks(q * HEAD_DIM_3 ** -0.5), to_chunks(k), to_chunks(v), to_chunks(g))
    _, os_ = lax.scan(gla_chunk, init, xs)
    return from_chunks(os_)

def gdn_chunk(S, xs):
    q, k, v, g, beta = xs
    causal = jnp.tril(jnp.ones((CHUNK, CHUNK), dtype=bool))
    strict = jnp.tril(jnp.ones((CHUNK, CHUNK), dtype=bool), -1)
    b = jnp.cumsum(g, axis=-1)
    decay = jnp.exp(jnp.where(causal, b[..., :, None] - b[..., None, :], -jnp.inf))
    kk = jnp.einsum('bhtk,bhsk->bhts', k, k)
    A = jnp.where(strict, beta[..., None] * kk * decay, 0.0)
    eye = jnp.eye(CHUNK, dtype=A.dtype)
    rhs = jnp.concatenate([beta[..., None] * k * jnp.exp(b)[..., None], beta[..., None] * v], axis=-1)
    sol = lax.linalg.triangular_solve(eye + A, rhs, left_side=True, lower=True, unit_diagonal=True)
    w, u = sol[..., :HEAD_DIM_3], sol[..., HEAD_DIM_3:]
    v_new = u - jnp.einsum('bhtk,bhkv->bhtv', w, S)
    qk = jnp.einsum('bhtk,bhsk->bhts', q, k) * decay
    o = jnp.einsum('bhtk,bhkv->bhtv', q * jnp.exp(b)[..., None], S) + jnp.einsum('bhts,bhsv->bhtv', qk, v_new)
    bL = b[..., -1]
    S = jnp.exp(bL)[..., None, None] * S + jnp.einsum('bhsk,bhsv->bhkv', k * jnp.exp(bL[..., None] - b)[..., None], v_new)
    return S, o

def gated_deltanet(q, k, v, g, beta):
    B_ = q.shape[0]
    init = jnp.zeros((B_, N_HEADS_3, HEAD_DIM_3, HEAD_DIM_3), jnp.float32)
    xs = (to_chunks(q), to_chunks(k), to_chunks(v), scalar_chunks(g), scalar_chunks(beta))
    _, os_ = lax.scan(gdn_chunk, init, xs)
    return from_chunks(os_)

def mixer_block(u, w_in, b_if, w_gla_lr, b_gla, conv_w, a_log, dt_bias, g_hm, g_hl, g_hd, w_up, w_out):
    f32 = jnp.float32
    proj = u @ w_in
    idx = [int(i) for i in np.cumsum(_in_sizes())[:-1]]
    (mq, mk, mv, mo, mi, mf, lq, lk, lv, lr, llr, dq, dk, dv, dz, dbeta, da, gates) = jnp.split(proj, idx, axis=-1)
    B_, S_, _ = u.shape
    b_if = b_if.astype(f32)
    li = mi.astype(f32) + b_if[:N_HEADS_3]
    lf = jax.nn.log_sigmoid(mf.astype(f32) + b_if[N_HEADS_3:])
    h_m = mlstm(mq.astype(f32), mk.astype(f32), mv.astype(f32), li, lf)
    h_m = head_rmsnorm(jax.nn.sigmoid(mo.astype(f32)) * h_m, g_hm)
    lg = jax.nn.log_sigmoid(llr.astype(f32) @ w_gla_lr.astype(f32) + b_gla.astype(f32)) / GLA_TAU
    h_l = gla(lq.astype(f32), lk.astype(f32), lv.astype(f32), lg)
    h_l = head_rmsnorm(h_l, g_hl) * jax.nn.silu(lr.astype(f32))
    qkv = jax.nn.silu(causal_conv(jnp.concatenate([dq, dk, dv], axis=-1).astype(f32), conv_w.astype(f32)))
    gq, gk, gv = jnp.split(qkv, 3, axis=-1)
    gq = l2norm_heads(gq) * HEAD_DIM_3 ** -0.5
    gk = l2norm_heads(gk)
    g_dec = -jnp.exp(a_log.astype(f32)) * jax.nn.softplus(da.astype(f32) + dt_bias.astype(f32))
    beta = jax.nn.sigmoid(dbeta.astype(f32))
    h_d = gated_deltanet(gq, gk, gv, g_dec, beta)
    h_d = head_rmsnorm(h_d, g_hd) * jax.nn.silu(dz.astype(f32))
    branches = jnp.stack([h_m, h_l, h_d], axis=2).astype(u.dtype)
    up = jnp.einsum('bsnc,ncd->bsnd', branches, w_up)
    gate = jax.nn.sigmoid(gates.reshape(B_, S_, N_BRANCH_3, D_MODEL))
    return jnp.sum(gate * up, axis=2) @ w_out

def third_inputs(seed: int = 0) -> dict:
    key = jax.random.key(seed)
    ks = jax.random.split(key, 20)
    n_in = sum(_in_sizes())

    def nrm(k, shape, scale):
        return jax.random.normal(k, shape, jnp.float32) * scale

    x = nrm(ks[0], (BATCH, SEQ, D_MODEL), 1.0)
    w_in = nrm(ks[1], (DEPTH, D_MODEL, n_in), D_MODEL ** -0.5)
    f_bias = jnp.linspace(3.0, 6.0, N_HEADS_3, dtype=jnp.float32)
    b_if = jnp.concatenate([nrm(ks[2], (DEPTH, N_HEADS_3), 0.1),
                            f_bias + nrm(ks[3], (DEPTH, N_HEADS_3), 0.1)], axis=-1)
    w_gla_lr = nrm(ks[4], (DEPTH, GLA_RANK, MIX_W), GLA_RANK ** -0.5)
    b_gla = nrm(ks[5], (DEPTH, MIX_W), 0.1)
    conv_gdn = nrm(ks[6], (DEPTH, CONV_K, 3 * MIX_W), CONV_K ** -0.5)
    a_log = jnp.log(jax.random.uniform(ks[7], (DEPTH, N_HEADS_3), jnp.float32, 1.0, 16.0))
    dt = jnp.exp(jax.random.uniform(ks[8], (DEPTH, N_HEADS_3), jnp.float32, np.log(1e-3), np.log(1e-1)))
    dt_bias = dt + jnp.log(-jnp.expm1(-dt))
    g_norm_mix = 1.0 + nrm(ks[9], (DEPTH, D_MODEL), 0.02)
    g_norm_mlp = 1.0 + nrm(ks[10], (DEPTH, D_MODEL), 0.02)
    g_head_mlstm = 1.0 + nrm(ks[11], (DEPTH, MIX_W), 0.02)
    g_head_gla = 1.0 + nrm(ks[12], (DEPTH, MIX_W), 0.02)
    g_head_gdn = 1.0 + nrm(ks[13], (DEPTH, MIX_W), 0.02)
    w_up = nrm(ks[14], (DEPTH, N_BRANCH_3, MIX_W, D_MODEL), MIX_W ** -0.5)
    w_out = nrm(ks[15], (DEPTH, D_MODEL, D_MODEL), D_MODEL ** -0.5)
    w_mlp_in = nrm(ks[16], (DEPTH, D_MODEL, D_FF_3), D_MODEL ** -0.5)
    w_mlp_out = nrm(ks[17], (DEPTH, D_FF_3, D_MODEL), D_FF_3 ** -0.5)
    g_final = 1.0 + nrm(ks[18], (D_MODEL,), 0.02)
    return {'x': x, 'w_in': w_in, 'b_if': b_if, 'w_gla_lr': w_gla_lr, 'b_gla': b_gla,
            'conv_gdn': conv_gdn, 'a_log': a_log, 'dt_bias': dt_bias,
            'g_norm_mix': g_norm_mix, 'g_norm_mlp': g_norm_mlp,
            'g_head_mlstm': g_head_mlstm, 'g_head_gla': g_head_gla, 'g_head_gdn': g_head_gdn,
            'w_up': w_up, 'w_out': w_out, 'w_mlp_in': w_mlp_in, 'w_mlp_out': w_mlp_out,
            'g_final': g_final}

def third_block(x, w_in, b_if, w_gla_lr, b_gla, conv_gdn, a_log, dt_bias, g_norm_mix, g_norm_mlp,
              g_head_mlstm, g_head_gla, g_head_gdn, w_up, w_out, w_mlp_in, w_mlp_out, g_final):
    for l in range(DEPTH):
        u = rmsnorm_3(x, g_norm_mix[l])
        x = x + mixer_block(u, w_in[l], b_if[l], w_gla_lr[l], b_gla[l], conv_gdn[l], a_log[l], dt_bias[l],
                            g_head_mlstm[l], g_head_gla[l], g_head_gdn[l], w_up[l], w_out[l]).astype(x.dtype)
        u = rmsnorm_3(x, g_norm_mlp[l])
        x = x + jnp.square(jax.nn.relu(u @ w_mlp_in[l])) @ w_mlp_out[l]
    return rmsnorm_3(x, g_final)


_first_inputs_3 = third_inputs


def third_inputs(seed=0):
    import zlib

    import numpy as np

    out = dict(_first_inputs_3(seed))
    spreads = {}
    factors = {'b_gla': 4.439,
     'g_norm_mlp': 3.593,
     'g_head_mlstm': 5.775,
     'g_head_gla': 8.0,
     'g_head_gdn': 8.0,
     'g_final': 2.918}
    for name, (base, spread) in spreads.items():
        noise = np.random.default_rng([zlib.crc32(name.encode()), seed]).standard_normal(out[name].shape)
        drawn = base * np.exp(spread * noise) if base else spread * noise
        out[name] = __import__('jax').numpy.asarray(drawn.astype(out[name].dtype))
    for name, factor in factors.items():
        out[name] = (out[name] * factor).astype(out[name].dtype)
    return out


_narrow_inputs_3 = third_inputs


def third_inputs(seed=0):

    out = dict(_narrow_inputs_3(seed))
    wider = {'g_head_mlstm': 4.25, 'g_head_gla': 5.44, 'g_head_gdn': 5.16, 'g_final': 3.28}
    for name, times in wider.items():
        mean = out[name].mean()
        out[name] = (mean + times * (out[name] - mean)).astype(out[name].dtype)
    return out


def setup_inputs(seed=0):
    out = dict(first_inputs(seed))
    for name, value in second_inputs(seed + 1).items():
        if name != "x":
            out[name + "_2"] = value
    for name, value in third_inputs(seed + 2).items():
        if name != "x":
            out[name + "_3"] = value
    return out


def reference(
    x, meta_tokens, norm_mix_w, w_in, rwkv_mu, rwkv_w0, rwkv_w2, rwkv_a0, rwkv_a2, rwkv_g2,
    rwkv_k_k, rwkv_k_a, rwkv_r_k, rwkv_ln_w, rwkv_ln_b, rwkv_w_o, diff_lq1, diff_lk1, diff_lq2,
    diff_lk2, diff_subln_w, diff_w_o, w_out, norm_mlp_w, mlp_w1, mlp_w2, final_norm_w, p_2,
    rel_bias_2, norm_mix_2, w_in_2, conv_dw_w_2, conv_dw_b_2, conv_ln_g_2, conv_ln_b_2,
    w_conv_out_2, cmp_pe_k_2, cmp_pe_v_2, w_ck1_2, w_ck2_2, w_cv1_2, w_cv2_2, w_attn_out_2,
    w_out_2, norm_ffn_2, w_up_2, ffn_dw_w_2, ffn_dw_b_2, w_down_2, norm_ple_2, w_ple_gate_2,
    w_ple_2, norm_final_2, w_in_3, b_if_3, w_gla_lr_3, b_gla_3, conv_gdn_3, a_log_3, dt_bias_3,
    g_norm_mix_3, g_norm_mlp_3, g_head_mlstm_3, g_head_gla_3, g_head_gdn_3, w_up_3, w_out_3,
    w_mlp_in_3, w_mlp_out_3, g_final_3,
):
    x = first_block(
        x, meta_tokens, norm_mix_w, w_in, rwkv_mu, rwkv_w0, rwkv_w2, rwkv_a0, rwkv_a2, rwkv_g2,
        rwkv_k_k, rwkv_k_a, rwkv_r_k, rwkv_ln_w, rwkv_ln_b, rwkv_w_o, diff_lq1, diff_lk1,
        diff_lq2, diff_lk2, diff_subln_w, diff_w_o, w_out, norm_mlp_w, mlp_w1, mlp_w2,
        final_norm_w,
    )
    x = second_block(
        x, p_2, rel_bias_2, norm_mix_2, w_in_2, conv_dw_w_2, conv_dw_b_2, conv_ln_g_2,
        conv_ln_b_2, w_conv_out_2, cmp_pe_k_2, cmp_pe_v_2, w_ck1_2, w_ck2_2, w_cv1_2, w_cv2_2,
        w_attn_out_2, w_out_2, norm_ffn_2, w_up_2, ffn_dw_w_2, ffn_dw_b_2, w_down_2, norm_ple_2,
        w_ple_gate_2, w_ple_2, norm_final_2,
    )
    return third_block(
        x, w_in_3, b_if_3, w_gla_lr_3, b_gla_3, conv_gdn_3, a_log_3, dt_bias_3, g_norm_mix_3,
        g_norm_mlp_3, g_head_mlstm_3, g_head_gla_3, g_head_gdn_3, w_up_3, w_out_3, w_mlp_in_3,
        w_mlp_out_3, g_final_3,
    )


_drawn_inputs = setup_inputs


def setup_inputs(seed=0):
    import zlib

    import numpy as np

    out = dict(_drawn_inputs(seed))
    spreads = {}
    factors = {'g_norm_mlp_3': 2.698}
    for name, (base, spread) in spreads.items():
        noise = np.random.default_rng([zlib.crc32(name.encode()), seed]).standard_normal(out[name].shape)
        drawn = base * np.exp(spread * noise) if base else spread * noise
        out[name] = __import__('jax').numpy.asarray(drawn.astype(out[name].dtype))
    for name, factor in factors.items():
        out[name] = (out[name] * factor).astype(out[name].dtype)
    return out
```

```python
import math
from contextlib import ExitStack, contextmanager

import numpy as np
import concourse.bass as bass
from concourse import mybir

F32 = mybir.dt.float32
ALU = mybir.AluOpType
ACT = mybir.ActivationFunctionType
AX_X = mybir.AxisListType.X
P = 128
BANK = 512


class Stage:

    def __init__(self, nc, memory):
        self.nc, self.memory, self.sems = nc, memory, []

    def sb(self, name, shape, dtype=F32):
        return self.memory.enter_context(self.nc.sbuf_tensor(f"{name}_{self.nc.next_id()}", shape, dtype))

    def ps(self, name, shape):
        return self.memory.enter_context(self.nc.psum_tensor(f"{name}_{self.nc.next_id()}", shape, F32))

    def sem(self, name):
        s = self.nc.alloc_semaphore(f"{name}_{self.nc.next_id()}")
        self.sems.append(s)
        return s


@contextmanager
def stage(nc):
    with ExitStack() as memory:
        s = Stage(nc, memory)
        yield s
    nc.clear_and_free_semaphores(s.sems)
    nc.all_engine_barrier()


def halves(T):
    n = -(-T // BANK)
    assert T % n == 0
    return n, T // n


def dense(nc, w, x, dst, T, func=None, residual=None, n_body=2):
    N, KG, _, KP, _ = w.shape
    assert N % n_body == 0
    ring = n_body * KG
    nh, th = halves(T)
    assert n_body * nh <= 8
    with stage(nc) as s:
        wbuf = [s.sb("wbuf", [P, KP, P]) for _ in range(ring)]
        acc = [s.ps("acc", [P, nh, BANK]) for _ in range(n_body)]
        rect = [s.sb("rect", [P, nh, th]) for _ in range(n_body)] if func == "relu2" else None
        w_loaded = [s.sem("w_loaded") for _ in range(ring)]
        w_used = [s.sem("w_used") for _ in range(ring)]
        acc_ready = [s.sem("acc_ready") for _ in range(n_body)]
        acc_free = [s.sem("acc_free") for _ in range(n_body)]
        rect_ready = [s.sem("rect_ready") for _ in range(n_body)]

        def token_view(ap):
            return ap.rearrange("p (h t) -> p h t", h=nh)

        with nc.Block() as block:
            @block.sync
            def _(sp):
                with sp.Fori(0, N // n_body) as it:
                    for b in range(n_body):
                        for g in range(KG):
                            j = b * KG + g
                            sp.wait_ge(w_used[j] if g < KG - 1 else acc_ready[b], it)
                            sp.dma_start(wbuf[j][:], w[it * n_body + b, g]).then_inc(w_loaded[j], 16)

            @block.tensor
            def _(pe):
                with pe.Fori(0, N // n_body) as it:
                    for b in range(n_body):
                        pe.wait_ge(acc_free[b], it)
                        for g in range(KG):
                            j = b * KG + g
                            pe.wait_ge(w_loaded[j], it * 16 + 16)
                            for k in range(KP):
                                for h in range(nh):
                                    mm = nc.tensor.matmul(
                                        acc[b][:, h, 0:th], wbuf[j][:, k, :],
                                        x[:, g * KP + k, h * th:(h + 1) * th],
                                        start=(g == 0 and k == 0), stop=(g == KG - 1 and k == KP - 1))
                            mm.then_inc(w_used[j] if g < KG - 1 else acc_ready[b], 1)

            if residual is None:
                @block.scalar
                def _(act):
                    with act.Fori(0, N // n_body) as it:
                        for b in range(n_body):
                            act.wait_ge(acc_ready[b], it + 1)
                            if func == "relu2":
                                act.wait_ge(acc_free[b], it)
                                nc.scalar.activation(rect[b][:], acc[b][:, :, 0:th], ACT.Relu).then_inc(rect_ready[b], 1)
                            else:
                                nc.scalar.activation(token_view(dst[:, it * n_body + b, :]), acc[b][:, :, 0:th],
                                                     func).then_inc(acc_free[b], 1)

            if func == "relu2":
                @block.vector
                def _(dve):
                    with dve.Fori(0, N // n_body) as it:
                        for b in range(n_body):
                            dve.wait_ge(rect_ready[b], it + 1)
                            nc.vector.tensor_tensor(token_view(dst[:, it * n_body + b, :]), rect[b][:], rect[b][:],
                                                    ALU.mult).then_inc(acc_free[b], 1)

            if residual is not None:
                @block.vector
                def _(dve):
                    with dve.Fori(0, N // n_body) as it:
                        for b in range(n_body):
                            dve.wait_ge(acc_ready[b], it + 1)
                            nc.vector.tensor_tensor(token_view(dst[:, it * n_body + b, :]), acc[b][:, :, 0:th],
                                                    token_view(residual[:, it * n_body + b, :]),
                                                    ALU.add).then_inc(acc_free[b], 1)


def settle(eng, sem):
    eng.wait_ge(sem, 1)


class Chain:

    def __init__(self, eng, sem, round_no=0, per_round=0):
        self.eng, self.sem, self.n, self.round_no, self.per_round = eng, sem, 0, round_no, per_round

    def __call__(self, ins):
        self.n += 1
        ins.then_inc(self.sem, 1)
        self.eng.wait_ge(self.sem, self.round_no * self.per_round + self.n)

    def close(self):
        assert self.n == self.per_round, self.n


def load(nc, pairs):
    with stage(nc) as s:
        arrived = s.sem("arrived")
        with nc.Block() as block:
            @block.sync
            def _(sp):
                for dst, src in pairs:
                    sp.dma_start(dst, src).then_inc(arrived, 16)
                sp.wait_ge(arrived, 16 * len(pairs))


def rmsnorm(nc, ones, x, weight, out, T, eps, src=None, dst=None):
    K = x.shape[1]
    nh, th = halves(T)
    with stage(nc) as s:
        w = s.sb("norm_w", [P, K])
        sq = s.sb("squares", [P, K, T])
        rstd = s.sb("rstd", [P, T])
        acc = s.ps("sum_squares", [P, nh, BANK])
        loaded, squared, summed = s.sem("loaded"), s.sem("squared"), s.sem("summed")
        mean_ready, root_ready, order, stored = s.sem("mean_ready"), s.sem("root_ready"), s.sem("order"), s.sem("stored")
        ready = s.sem("normed")
        acc_v = acc[:, :, 0:th]
        rstd_v = rstd[:].rearrange("p (h t) -> p h t", h=nh)
        with nc.Block() as block:
            @block.sync
            def _(sp):
                sp.dma_start(w[:], weight).then_inc(loaded, 16)
                if src is not None:
                    for k in range(K):
                        sp.dma_start(x[:, k, :], src[:, k, :]).then_inc(loaded, 16)
                if dst is not None:
                    for k in range(K):
                        sp.wait_ge(ready, k + 1)
                        sp.dma_start(dst[:, k, :], out[:, k, :]).then_inc(stored, 16)
                    sp.wait_ge(stored, 16 * K)

            @block.scalar
            def _(act):
                for k in range(K):
                    if src is not None and k == 0:
                        act.wait_ge(loaded, 16 + 16 * K)
                    nc.scalar.activation(sq[:, k, :], x[:, k, :], ACT.Square).then_inc(squared, 1)
                act.wait_ge(mean_ready, 1)
                nc.scalar.activation(rstd[:], rstd[:], ACT.Sqrt).then_inc(root_ready, 1)

            @block.tensor
            def _(pe):
                for k in range(K):
                    pe.wait_ge(squared, k + 1)
                    for h in range(nh):
                        mm = nc.tensor.matmul(acc[:, h, 0:th], ones[:], sq[:, k, h * th:(h + 1) * th],
                                              start=(k == 0), stop=(k == K - 1))
                mm.then_inc(summed, 1)

            @block.vector
            def _(dve):
                chain = Chain(dve, order)
                dve.wait_ge(summed, 1)
                nc.vector.tensor_scalar(rstd_v, acc_v, 1.0 / (K * P), eps, ALU.mult, ALU.add).then_inc(mean_ready, 1)
                dve.wait_ge(root_ready, 1)
                chain(nc.vector.reciprocal(rstd[:], rstd[:]))
                dve.wait_ge(loaded, 16 if src is None else 16 + 16 * K)
                for k in range(K):
                    nc.vector.scalar_tensor_tensor(out=out[:, k, :], in0=x[:, k, :], scalar=w[:, k:k + 1], in1=rstd[:],
                                                   op0=ALU.mult, op1=ALU.mult).then_inc(ready, 1)


T1 = 528
RC = 66
RN = T1 // RC
QT = 88
QN = T1 // QT
EXP_HALF = math.exp(-0.5)
LEVELS1 = math.ceil(math.log2(RC))


def rwkv_lora_inputs(nc, c, p):
    with stage(nc) as s:
        mu = s.sb("mu", [P, 3])
        diff = s.sb("diff", [P, 3, T1])
        loaded, order, mixed = s.sem("loaded"), s.sem("order"), s.sem("mixed")
        with nc.Block() as block:
            @block.sync
            def _(sp):
                sp.dma_start(mu[:], c["lora_mu"]).then_inc(loaded, 16)

            @block.vector
            def _(dve):
                chain = Chain(dve, order)
                chain(nc.vector.tensor_tensor(diff[:], p[:, 24:27, 0:T1], p[:, 24:27, 1:T1 + 1], ALU.subtract))
                dve.wait_ge(loaded, 16)
                for i in range(3):
                    nc.vector.scalar_tensor_tensor(out=p[:, 24 + i, 1:T1 + 1], in0=diff[:, i, :], scalar=mu[:, i:i + 1],
                                                   in1=p[:, 24 + i, 1:T1 + 1], op0=ALU.mult, op1=ALU.add).then_inc(mixed, 1)

            @block.scalar
            def _(act):
                act.wait_ge(mixed, 3)
                nc.scalar.activation(p[0:64, 24, 1:T1 + 1], p[0:64, 24, 1:T1 + 1], ACT.Tanh)
                nc.scalar.activation(p[:, 25:27, 1:T1 + 1], p[:, 25:27, 1:T1 + 1], ACT.Sigmoid)


def rwkv_prepare(nc, c, p, chunks, chunk_decay, bonus_scr, gate_scr):
    with stage(nc) as s:
        vec = s.sb("vec", [P, 8])
        lora_w = s.sb("lora_w", [P, 3, P])
        fac = s.sb("factors", [P, 5, T1])
        r, k, kk, kn, a, lw, cum, ecum, eneg, eprev, tmp, sq, bonus, gate = (
            s.sb(n, [P, T1]) for n in
            "r k kk kn a lw cum ecum eneg eprev tmp sq bonus gate".split())
        dif = s.sb("dif", [P, T1])
        za, zw, zg, zs = (s.ps(n, [P, 2, BANK]) for n in ("za", "zw", "zg", "zs"))
        loaded, z_ready, w_sig, a_sig, g_out = (s.sem(n) for n in ("loaded", "z_ready", "w_sig", "a_sig", "g_out"))
        order, cum_ready, prev_ready, kk_ready, sq_ready, ss_ready = (
            s.sem(n) for n in ("order", "cum_ready", "prev_ready", "kk_ready", "sq_ready", "ss_ready"))
        root_ready, ecum_ready, eprev_ready, rk_ready, bs_ready, fac_ready, stored = (
            s.sem(n) for n in ("root_ready", "ecum_ready", "eprev_ready", "rk_ready", "bs_ready", "fac_ready", "stored"))
        H = T1 // 2

        def hv(ap):
            return ap.rearrange("p (h t) -> p h t", h=2)

        STORES = 7
        with nc.Block() as block:
            @block.sync
            def _(sp):
                with sp.Fori(0, 8) as i:
                    sp.wait_ge(fac_ready, i)
                    sp.dma_start(vec[:], c["rwkv_vec"][i]).then_inc(loaded, 16)
                    sp.dma_start(lora_w[:], c["lora_up"][i]).then_inc(loaded, 16)
                    sp.wait_ge(fac_ready, i + 1)
                    sp.wait_ge(g_out, i + 1)
                    for q in range(5):
                        sp.dma_start(chunks[:, :, i, q, :].rearrange("c p t -> p c t"),
                                     fac[:, q, :].rearrange("p (c t) -> p c t", c=RN)).then_inc(stored, 16)
                    sp.dma_start(bonus_scr[:, i, :], bonus[:]).then_inc(stored, 16)
                    sp.dma_start(gate_scr[:, i, :], gate[:]).then_inc(stored, 16)
                    count = sp.compute_val((i + 1) * (16 * STORES))
                    settle(sp, loaded)
                    sp.wait_ge(stored, count)

            @block.tensor
            def _(pe):
                with pe.Fori(0, 8) as i:
                    pe.wait_ge(loaded, (i + 1) * 32)
                    pe.wait_ge(fac_ready, i)
                    for h in range(2):
                        cols = slice(1 + h * H, 1 + (h + 1) * H)
                        nc.tensor.matmul(zw[:, h, 0:H], lora_w[0:64, 0, :], p[0:64, 24, cols], start=True, stop=True)
                        nc.tensor.matmul(za[:, h, 0:H], lora_w[64:128, 0, :], p[64:128, 24, cols], start=True, stop=True)
                        nc.tensor.matmul(zg[:, h, 0:H], lora_w[:, 1, :], p[:, 25, cols], start=True, stop=False)
                        mm = nc.tensor.matmul(zg[:, h, 0:H], lora_w[:, 2, :], p[:, 26, cols], start=False, stop=True)
                    mm.then_inc(z_ready, 1)
                    pe.wait_ge(sq_ready, i + 1)
                    for h in range(2):
                        mm = nc.tensor.matmul(zs[:, h, 0:H], c["blk64"][:], sq[:, h * H:(h + 1) * H], start=True, stop=True)
                    mm.then_inc(ss_ready, 1)
                    pe.wait_ge(rk_ready, i + 1)
                    pe.wait_ge(w_sig, i + 1)
                    for h in range(2):
                        mm = nc.tensor.matmul(zw[:, h, 0:H], c["blk64"][:], tmp[:, h * H:(h + 1) * H], start=True, stop=True)
                    mm.then_inc(bs_ready, 1)

            @block.scalar
            def _(act):
                with act.Fori(0, 8) as i:
                    act.wait_ge(z_ready, i + 1)
                    act.wait_ge(fac_ready, i)
                    nc.scalar.activation(hv(lw[:]), zw[:, :, 0:H], ACT.Sigmoid, bias=vec[:, 3:4]).then_inc(w_sig, 1)
                    nc.scalar.activation(hv(a[:]), za[:, :, 0:H], ACT.Sigmoid, bias=vec[:, 4:5]).then_inc(a_sig, 1)
                    act.wait_ge(stored, i * (16 * STORES))
                    nc.scalar.activation(hv(gate[:]), zg[:, :, 0:H], ACT.Copy).then_inc(g_out, 1)
                    act.wait_ge(kk_ready, i + 1)
                    nc.scalar.activation(sq[:], kk[:], ACT.Square).then_inc(sq_ready, 1)
                    act.wait_ge(cum_ready, i + 1)
                    nc.scalar.activation(ecum[:], cum[:], ACT.Exp)
                    nc.scalar.activation(eneg[:], cum[:], ACT.Exp, scale=-1.0).then_inc(ecum_ready, 1)
                    act.wait_ge(prev_ready, i + 1)
                    nc.scalar.activation(eprev[:], eprev[:], ACT.Exp).then_inc(eprev_ready, 1)
                    act.wait_ge(ss_ready, i + 1)
                    nc.scalar.activation(hv(kn[:]), zs[:, :, 0:H], ACT.Sqrt).then_inc(root_ready, 1)

            @block.vector
            def _(dve):
                with dve.Fori(0, 8) as i:
                    chain = Chain(dve, order, i, 14)
                    TT, STT = nc.vector.tensor_tensor, nc.vector.scalar_tensor_tensor

                    def shift(tile, mu, out):
                        src, prev = p[:, tile, 1:T1 + 1], p[:, tile, 0:T1]
                        chain(TT(dif[:], prev, src, ALU.subtract))
                        return STT(out=out, in0=dif[:], scalar=mu, in1=src, op0=ALU.mult, op1=ALU.add)

                    dve.wait_ge(loaded, (i + 1) * 32)
                    dve.wait_ge(stored, i * (16 * STORES))
                    chain(shift(i + 8, vec[:, 1:2], k[:]))
                    nc.vector.tensor_scalar(kk[:], k[:], vec[:, 5:6], None, ALU.mult).then_inc(kk_ready, 1)
                    chain(shift(i, vec[:, 0:1], r[:]))
                    chain(shift(i + 16, vec[:, 2:3], fac[:, 4, :]))
                    dve.wait_ge(w_sig, i + 1)
                    chain(nc.vector.tensor_scalar(lw[:], lw[:], -EXP_HALF, None, ALU.mult))
                    nc.vector.tensor_tensor_scan(cum[:], c["chunk_start66"][:], lw[:], 0.0, ALU.mult, ALU.add).then_inc(cum_ready, 1)
                    dve.wait_ge(cum_ready, i + 1)
                    TT(eprev[:], cum[:], lw[:], ALU.subtract).then_inc(prev_ready, 1)
                    dve.wait_ge(a_sig, i + 1)
                    chain(nc.vector.tensor_scalar(dif[:], a[:], -1.0, vec[:, 6:7], ALU.add, ALU.mult))
                    chain(STT(out=k[:], in0=dif[:], scalar=1.0, in1=k[:], op0=ALU.add, op1=ALU.mult))
                    dve.wait_ge(root_ready, i + 1)
                    chain(nc.vector.tensor_scalar(kn[:], kn[:], 1e-12, None, ALU.max))
                    chain(nc.vector.reciprocal(kn[:], kn[:]))
                    chain(TT(kn[:], kn[:], kk[:], ALU.mult))
                    STT(out=tmp[:], in0=r[:], scalar=vec[:, 7:8], in1=k[:], op0=ALU.mult, op1=ALU.mult).then_inc(rk_ready, 1)
                    dve.wait_ge(eprev_ready, i + 1)
                    STT(out=fac[:, 0, :], in0=kn[:], scalar=-1.0, in1=eprev[:], op0=ALU.mult, op1=ALU.mult)
                    TT(fac[:, 1, :], r[:], ecum[:], ALU.mult)
                    TT(fac[:, 3, :], k[:], eneg[:], ALU.mult)
                    chain(TT(kn[:], kn[:], a[:], ALU.mult))
                    TT(fac[:, 2, :], kn[:], eneg[:], ALU.mult)
                    chain(nc.vector.tensor_copy(chunk_decay[:, i, :], ecum[:].rearrange("p (c t) -> p c t", c=RN)[:, :, RC - 1]))
                    dve.wait_ge(bs_ready, i + 1)
                    TT(hv(bonus[:]), zw[:, :, 0:H], hv(fac[:, 4, :]), ALU.mult).then_inc(fac_ready, 1)
                    chain.close()


def rwkv_chunks(nc, c, y, chunks, chunk_decay):
    HG = 4
    GS = range(16 // HG)
    L = LEVELS1
    with stage(nc) as s:
        cb = s.sb("chunk", [P, 8, 5, RC])
        state = s.sb("state", [P, 8, 64])
        tok = s.sb("tok", [RC, 8, 3, P])
        bp = s.sb("bp", [RC, 16, 2, RC])
        kp = s.sb("kp", [RC, 16, 2, RC])
        nm = s.sb("nm", [RC, L, 16, RC])
        t1 = s.sb("t1", [RC, 16, RC])
        xi = s.sb("xi", [RC, 16, RC])
        yi = s.sb("yi", [RC, 16, RC])
        bb = s.sb("bb", [RC, 16, 64])
        ua = s.sb("ua", [RC, 16, 64])
        grown = s.sb("grown", [P, 8, 64])
        psA = [s.ps("psA", [P, BANK]) for _ in GS]
        psB = [s.ps("psB", [P, BANK]) for _ in GS]
        loaded, state_zero = s.sem("loaded"), s.sem("state_zero")
        pe_done = [s.sem("pe_done") for _ in GS]
        act_done = [s.sem("act_done") for _ in GS]
        dve_done = [s.sem("dve_done") for _ in GS]
        level_done = [s.sem("level_done") for _ in GS]
        order = s.sem("order")
        PE_TOK, PE_BP, PE_KP, PE_B, PE_L0 = 1, 2, 3, 4, 5
        PE_T1, PE_XY = (lambda l: 4 + 2 * l), (lambda l: 5 + 2 * l)
        PE_U, PE_Y, PE_S, NPE = 2 * L + 4, 2 * L + 5, 2 * L + 6, 2 * L + 6
        ACT_TOK, ACT_B, ACT_T1, ACT_U, ACT_Y, NACT = 1, 2, (lambda l: 2 + l), L + 2, L + 3, L + 3
        DVE_BP, DVE_KP, DVE_XY, DVE_S, NDVE = 1, 2, (lambda l: 3 + l), L + 3, L + 3

        def heads(g):
            for j in range(HG):
                yield j, HG * g + j, 2 * g + j % 2, slice(64 * (j // 2), 64 * (j // 2) + 64)

        with nc.Block() as block:
            @block.sync
            def _(sp):
                with sp.Fori(0, RN) as n:
                    for g in GS:
                        count = sp.compute_val(n * NPE)
                        count_2 = sp.compute_val(n * NDVE)
                        settle(sp, state_zero)
                        sp.wait_ge(pe_done[g], count)
                        sp.wait_ge(dve_done[g], count_2)
                    sp.dma_start(cb[:], chunks[n]).then_inc(loaded, 16)

            @block.tensor
            def _(pe):
                pe.wait_ge(state_zero, 1)
                with pe.Fori(0, RN) as n:
                    def after(what, g, per_chunk, k):
                        pe.wait_ge(what[g], n * per_chunk + k)
                    pe.wait_ge(loaded, n * 16 + 16)
                    for g in GS:
                        after(act_done, g, NACT, 0)
                        after(dve_done, g, NDVE, 0)
                        for t, ps in ((2 * g, psA[g]), (2 * g + 1, psB[g])):
                            for q in range(3):
                                mm = nc.tensor.transpose(ps[0:RC, q * P:(q + 1) * P], cb[:, t, 2 + q, :], c["ident"][:])
                        mm.then_inc(pe_done[g], 1)
                    for q, wait_on, per, k in ((2, act_done, NACT, ACT_TOK), (3, dve_done, NDVE, DVE_BP)):
                        for g in GS:
                            after(wait_on, g, per, k)
                            for j, h, t, rows in heads(g):
                                ps = psA[g] if j < 2 else psB[g]
                                mm = nc.tensor.matmul(ps[0:RC, (j % 2) * 2 * RC:(j % 2 + 1) * 2 * RC], cb[rows, t, q, :],
                                                      cb[rows, t, 0:2, :].rearrange("p q t -> p (q t)"), start=True, stop=True)
                            mm.then_inc(pe_done[g], 1)
                    for g in GS:
                        after(dve_done, g, NDVE, DVE_KP)
                        for j, h, t, rows in heads(g):
                            out = (psA, psB)[j // 2][g][0:RC, (j % 2) * 64:(j % 2 + 1) * 64]
                            nc.tensor.matmul(out, cb[rows, t, 0, :], state[rows, t, :], start=True, stop=False)
                            mm = nc.tensor.matmul(out, kp[:, h, 0, :], tok[:, t, 2, rows], start=False, stop=True)
                        mm.then_inc(pe_done[g], 1)
                    for g in GS:
                        after(level_done, g, L, 1)
                        after(act_done, g, NACT, ACT_B)
                        for j, h, t, rows in heads(g):
                            mm = nc.tensor.matmul(psA[g][0:RC, j * RC:(j + 1) * RC], nm[:, 0, h, :], c["ident"][0:RC, 0:RC],
                                                  start=True, stop=True)
                        mm.then_inc(pe_done[g], 1)
                    for l in range(1, L):
                        for g in GS:
                            after(level_done, g, L, l + 1)
                            after(dve_done, g, NDVE, DVE_XY(l - 1))
                            for j, h, t, rows in heads(g):
                                mm = nc.tensor.matmul(psA[g][0:RC, j * RC:(j + 1) * RC], nm[:, l, h, :], xi[:, h, :],
                                                      start=True, stop=True)
                            mm.then_inc(pe_done[g], 1)
                        for g in GS:
                            after(act_done, g, NACT, ACT_T1(l))
                            for j, h, t, rows in heads(g):
                                cols = slice(j * RC, (j + 1) * RC)
                                if l < L - 1:
                                    nc.tensor.matmul(psA[g][0:RC, cols], yi[:, h, :], t1[:, h, :], start=True, stop=True)
                                mm = nc.tensor.matmul(psB[g][0:RC, cols], t1[:, h, :], yi[:, h, :], start=True, stop=True)
                            mm.then_inc(pe_done[g], 1)
                    for g in GS:
                        after(dve_done, g, NDVE, DVE_XY(L - 1))
                        for j, h, t, rows in heads(g):
                            mm = nc.tensor.matmul(psA[g][0:RC, j * 64:(j + 1) * 64], yi[:, h, :], bb[:, h, :], start=True, stop=True)
                        mm.then_inc(pe_done[g], 1)
                    for g in GS:
                        after(act_done, g, NACT, ACT_U)
                        for j, h, t, rows in heads(g):
                            out = (psA, psB)[j // 2][g][rows, (j % 2) * RC:(j % 2 + 1) * RC]
                            nc.tensor.matmul(out, tok[:, t, 2, rows], kp[:, h, 1, :], start=True, stop=False)
                            nc.tensor.matmul(out, state[rows, t, :], cb[rows, t, 1, :], start=False, stop=False)
                            mm = nc.tensor.matmul(out, ua[:, h, :], bp[:, h, 1, :], start=False, stop=True)
                        mm.then_inc(pe_done[g], 1)
                    for g in GS:
                        after(act_done, g, NACT, ACT_Y)
                        for j, h, t, rows in heads(g):
                            out = psA[g][rows, (j % 2) * 64:(j % 2 + 1) * 64]
                            nc.tensor.matmul(out, tok[:, t, 0, rows], ua[:, h, :], start=True, stop=False)
                            mm = nc.tensor.matmul(out, tok[:, t, 1, rows], tok[:, t, 2, rows], start=False, stop=True)
                        mm.then_inc(pe_done[g], 1)

            @block.scalar
            def _(act):
                with act.Fori(0, RN) as n:
                    def after(g, k):
                        act.wait_ge(pe_done[g], n * NPE + k)
                    for g in GS:
                        after(g, PE_TOK)
                        for t, ps in ((2 * g, psA[g]), (2 * g + 1, psB[g])):
                            cp = nc.scalar.activation(tok[:, t, :, :].rearrange("p q d -> p (q d)"), ps[0:RC, 0:3 * P], ACT.Copy)
                        cp.then_inc(act_done[g], 1)
                    for g in GS:
                        after(g, PE_B)
                        for h0, ps in ((HG * g, psA[g]), (HG * g + 2, psB[g])):
                            cp = nc.scalar.activation(bb[:, h0:h0 + 2, :].rearrange("p h v -> p (h v)"), ps[0:RC, 0:128], ACT.Copy)
                        cp.then_inc(act_done[g], 1)
                    for l in range(1, L):
                        for g in GS:
                            after(g, PE_T1(l))
                            nc.scalar.activation(t1[:, HG * g:HG * (g + 1), :].rearrange("p h t -> p (h t)"),
                                                 psA[g][0:RC, 0:HG * RC], ACT.Copy).then_inc(act_done[g], 1)
                    for g in GS:
                        after(g, PE_U)
                        nc.scalar.activation(ua[:, HG * g:HG * (g + 1), :].rearrange("p h v -> p (h v)"), psA[g][0:RC, 0:HG * 64],
                                             ACT.Copy).then_inc(act_done[g], 1)
                    for g in GS:
                        after(g, PE_Y)
                        for r0, ps in ((0, psA[g]), (64, psB[g])):
                            cp = nc.scalar.activation(y[r0:r0 + 64, 2 * g:2 * g + 2, bass.ds(n * RC, RC)],
                                                      ps[r0:r0 + 64, 0:2 * RC].rearrange("p (a t) -> p a t", a=2), ACT.Copy)
                        cp.then_inc(act_done[g], 1)

            @block.gpsimd
            def _(pool):
                with pool.Fori(0, RN) as n:
                    for l in range(L):
                        for g in GS:
                            if l == 0:
                                pool.wait_ge(dve_done[g], n * NDVE + DVE_BP)
                            nc.gpsimd.tensor_tensor(nm[:, l, HG * g:HG * (g + 1), :], bp[:, HG * g:HG * (g + 1), 0, :],
                                                    c["level66"][:, l, :, :], ALU.mult).then_inc(level_done[g], 1)

            @block.vector
            def _(dve):
                nc.vector.memset(state[:], 0.0).then_inc(state_zero, 1)
                with dve.Fori(0, RN) as n:
                    chain = Chain(dve, order, n, 4)
                    TT = nc.vector.tensor_tensor

                    def after(g, k):
                        dve.wait_ge(pe_done[g], n * NPE + k)
                    for what, k in ((bp, PE_BP), (kp, PE_KP)):
                        for g in GS:
                            after(g, k)
                            for half, ps in ((0, psA[g]), (1, psB[g])):
                                h0 = HG * g + 2 * half
                                r = TT(what[:, h0:h0 + 2, :, :].rearrange("p h q t -> p (h q t)"), ps[0:RC, 0:4 * RC],
                                       c["causal66"][:], ALU.mult)
                            r.then_inc(dve_done[g], 1)
                    for g in GS:
                        hs = slice(HG * g, HG * (g + 1))
                        after(g, PE_L0)
                        TT(xi[:, hs, :], psA[g][0:RC, 0:HG * RC].rearrange("p (h t) -> p h t", h=HG), c["ident66"][:], ALU.add)
                        TT(yi[:, hs, :], nm[:, 0, hs, :], c["ident66"][:], ALU.add).then_inc(dve_done[g], 1)
                    for l in range(1, L):
                        for g in GS:
                            hs = slice(HG * g, HG * (g + 1))
                            after(g, PE_XY(l))
                            if l < L - 1:
                                xv = xi[:, hs, :].rearrange("p h t -> p (h t)")
                                TT(xv, psA[g][0:RC, 0:HG * RC], xv, ALU.add)
                            yv = yi[:, hs, :].rearrange("p h t -> p (h t)")
                            TT(yv, psB[g][0:RC, 0:HG * RC], yv, ALU.add).then_inc(dve_done[g], 1)
                    for g in GS:
                        after(g, PE_S)
                        ts = slice(2 * g, 2 * g + 2)
                        chain(TT(grown[:, ts, :].rearrange("p a v -> p (a v)"), psA[g][:, 0:128],
                                 state[:, ts, :].rearrange("p a v -> p (a v)"), ALU.add))
                        nc.vector.tensor_scalar(state[:, 2 * g, :], grown[:, 2 * g, :], chunk_decay[:, 2 * g, bass.ds(n, 1)], None, ALU.mult)
                        nc.vector.tensor_scalar(state[:, 2 * g + 1, :], grown[:, 2 * g + 1, :], chunk_decay[:, 2 * g + 1, bass.ds(n, 1)], None,
                                                ALU.mult).then_inc(dve_done[g], 1)
                    chain.close()


def rwkv_finish(nc, c, y, bonus_scr, gate_scr):
    H = T1 // 2
    with stage(nc) as s:
        lnw = s.sb("lnw", [P, 2, 8])
        gate = [s.sb("gate", [P, T1]) for _ in range(2)]
        bonus = [s.sb("bonus", [P, T1]) for _ in range(2)]
        sq = [s.sb("sq", [P, T1]) for _ in range(2)]
        var = [s.sb("var", [P, T1]) for _ in range(2)]
        cen = [s.sb("cen", [P, T1]) for _ in range(2)]
        pm = [s.ps("mean", [P, 2, BANK]) for _ in range(2)]
        pv = [s.ps("var", [P, 2, BANK]) for _ in range(2)]
        vec_in, mean_ready, var_ready = s.sem("vec_in"), s.sem("mean_ready"), s.sem("var_ready")
        loaded = [s.sem("loaded") for _ in range(2)]
        cen_ready, sq_ready, eps_ready, root_ready, done, order = (
            s.sem(n) for n in ("cen_ready", "sq_ready", "eps_ready", "root_ready", "done", "order"))

        def hv(ap):
            return ap.rearrange("p (h t) -> p h t", h=2)
        with nc.Block() as block:
            @block.sync
            def _(sp):
                sp.dma_start(lnw[:], c["rwkv_ln"]).then_inc(vec_in, 16)
                with sp.Fori(0, 4) as it:
                    for b in range(2):
                        sp.wait_ge(done, it * 2)
                        sp.dma_start(gate[b][:], gate_scr[:, it * 2 + b, :]).then_inc(loaded[b], 16)
                        sp.dma_start(bonus[b][:], bonus_scr[:, it * 2 + b, :]).then_inc(loaded[b], 16)

            @block.tensor
            def _(pe):
                with pe.Fori(0, 4) as it:
                    for b in range(2):
                        pe.wait_ge(done, it * 2)
                        for h in range(2):
                            mm = nc.tensor.matmul(pm[b][:, h, 0:H], c["mean64"][:], y[:, it * 2 + b, h * H:(h + 1) * H],
                                                  start=True, stop=True)
                        mm.then_inc(mean_ready, 1)
                    for b in range(2):
                        pe.wait_ge(sq_ready, it * 2 + b + 1)
                        for h in range(2):
                            mm = nc.tensor.matmul(pv[b][:, h, 0:H], c["mean64"][:], sq[b][:, h * H:(h + 1) * H],
                                                  start=True, stop=True)
                        mm.then_inc(var_ready, 1)

            @block.scalar
            def _(act):
                with act.Fori(0, 4) as it:
                    for b in range(2):
                        act.wait_ge(cen_ready, it * 2 + b + 1)
                        nc.scalar.activation(sq[b][:], cen[b][:], ACT.Square).then_inc(sq_ready, 1)
                    for b in range(2):
                        act.wait_ge(eps_ready, it * 2 + b + 1)
                        nc.scalar.activation(var[b][:], var[b][:], ACT.Sqrt).then_inc(root_ready, 1)

            @block.vector
            def _(dve):
                TT, TS = nc.vector.tensor_tensor, nc.vector.tensor_scalar
                dve.wait_ge(vec_in, 16)
                with dve.Fori(0, 4) as it:
                    chain = Chain(dve, order, it, 8)
                    for b in range(2):
                        dve.wait_ge(mean_ready, it * 2 + b + 1)
                        TT(hv(cen[b][:]), hv(y[:, it * 2 + b, :]), pm[b][:, :, 0:H], ALU.subtract).then_inc(cen_ready, 1)
                    for b in range(2):
                        dve.wait_ge(var_ready, it * 2 + b + 1)
                        TS(hv(var[b][:]), pv[b][:, :, 0:H], 64e-5, None, ALU.add).then_inc(eps_ready, 1)
                    for b in range(2):
                        i = it * 2 + b
                        dve.wait_ge(root_ready, i + 1)
                        chain(nc.vector.reciprocal(var[b][:], var[b][:]))
                        chain(TT(cen[b][:], cen[b][:], var[b][:], ALU.mult))
                        chain(TS(cen[b][:], cen[b][:], lnw[:, 0, bass.ds(i, 1)], lnw[:, 1, bass.ds(i, 1)], ALU.mult, ALU.add))
                        dve.wait_ge(loaded[b], it * 32 + 32)
                        chain(TT(cen[b][:], cen[b][:], bonus[b][:], ALU.add))
                        TT(y[:, i, :], cen[b][:], gate[b][:], ALU.mult).then_inc(done, 1)
                    chain.close()


LAMBDA_INIT = 0.8 - 0.6 * math.exp(-0.3 * 0)
NEG = -1e30


def head_rms(nc, ones, o, weight, T, eps, factor=1.0, gate=None, mean=1.0 / P):
    N = o.shape[1]
    nh, th = halves(T)
    with stage(nc) as s:
        w = s.sb("w", [P, N])
        sq = [s.sb("sq", [P, T]) for _ in range(2)]
        rstd = [s.sb("rstd", [P, T]) for _ in range(2)]
        acc = [s.ps("acc", [P, nh, BANK]) for _ in range(2)]
        w_in, w_ready, sq_ready, summed, mean_ready, root_ready, done, order = (
            s.sem(n) for n in ("w_in", "w_ready", "sq_ready", "summed", "mean_ready", "root_ready", "done", "order"))
        with nc.Block() as block:
            @block.sync
            def _(sp):
                sp.dma_start(w[:], weight).then_inc(w_in, 16)

            @block.scalar
            def _(act):
                with act.Fori(0, N // 2) as it:
                    act.wait_ge(summed, it * 2)
                    for b in range(2):
                        nc.scalar.activation(sq[b][:], o[:, it * 2 + b, :], ACT.Square).then_inc(sq_ready, 1)
                    for b in range(2):
                        act.wait_ge(mean_ready, it * 2 + b + 1)
                        nc.scalar.activation(rstd[b][:], rstd[b][:], ACT.Sqrt).then_inc(root_ready, 1)

            @block.tensor
            def _(pe):
                with pe.Fori(0, N // 2) as it:
                    pe.wait_ge(mean_ready, it * 2)
                    for b in range(2):
                        pe.wait_ge(sq_ready, it * 2 + b + 1)
                        for h in range(nh):
                            mm = nc.tensor.matmul(acc[b][:, h, 0:th], ones[:], sq[b][:, h * th:(h + 1) * th], start=True, stop=True)
                        mm.then_inc(summed, 1)

            @block.vector
            def _(dve):
                dve.wait_ge(w_in, 16)
                nc.vector.tensor_scalar(w[:], w[:], factor, None, ALU.mult).then_inc(w_ready, 1)
                dve.wait_ge(w_ready, 1)
                with dve.Fori(0, N // 2) as it:
                    per = 2 + (2 if gate is not None else 0)
                    chain = Chain(dve, order, it, per)
                    dve.wait_ge(done, it * 2)
                    for b in range(2):
                        dve.wait_ge(summed, it * 2 + b + 1)
                        nc.vector.tensor_scalar(rstd[b][:].rearrange("p (h t) -> p h t", h=nh), acc[b][:, :, 0:th], mean, eps,
                                                ALU.mult, ALU.add).then_inc(mean_ready, 1)
                    for b in range(2):
                        i = it * 2 + b
                        dve.wait_ge(root_ready, i + 1)
                        chain(nc.vector.reciprocal(rstd[b][:], rstd[b][:]))
                        if gate is not None:
                            chain(nc.vector.tensor_tensor(rstd[b][:], rstd[b][:], gate[:, i, :], ALU.mult))
                        nc.vector.scalar_tensor_tensor(out=o[:, i, :], in0=o[:, i, :], scalar=w[:, bass.ds(i, 1)], in1=rstd[b][:],
                                                       op0=ALU.mult, op1=ALU.mult).then_inc(done, 1)
                    chain.close()


def diff_attention(nc, c, p, o):
    SCALE = 64 ** -0.5
    HALF = T1 // 2
    OFF = T1 - QT
    with stage(nc) as s:
        lam_in = s.sb("lam_in", [64, 4])
        lam_prod = s.sb("lam_prod", [64, 2])
        lam_exp = s.sb("lam_exp", [P, 2])
        neg_lam = s.sb("neg_lam", [P, 1])
        rot, swapped = s.sb("rot", [P, 2, T1]), s.sb("swapped", [P, T1])
        vt = s.sb("vt", [QT, QN, P])
        sc = [[s.sb("sc", [QT, T1]) for _ in range(2)] for _ in range(2)]
        wt = [s.sb("w", [QT, T1]) for _ in range(2)]
        wT = [s.sb("wT", [QT, QN, QT]) for _ in range(2)]
        small = [[s.sb("small", [QT, 4]) for _ in range(2)] for _ in range(2)]
        ps_s = [s.ps("ps_s", [P, 2, BANK]) for _ in range(2)]
        ps_t = s.ps("ps_t", [P, 2, BANK])
        ps_o = s.ps("ps_o", [P, BANK])
        loaded, lam_mult, lam_sum, lam_done, lam_ready = (s.sem(n) for n in ("loaded", "lam_mult", "lam_sum", "lam_done", "lam_ready"))
        swap_ready, rope_done, vt_ready, vt_copied = (s.sem(n) for n in ("swap_ready", "rope_done", "vt_ready", "vt_copied"))
        sc_ready = [s.sem("sc_ready") for _ in range(2)]
        max_ready = [s.sem("max_ready") for _ in range(2)]
        exp_ready = [s.sem("exp_ready") for _ in range(2)]
        w_ready, wt_ready, wt_copied, pv_ready, pv_copied, order, order2 = (
            s.sem(n) for n in ("w_ready", "wt_ready", "wt_copied", "pv_ready", "pv_copied", "order", "order2"))

        def hv(ap):
            return ap.rearrange("p (h t) -> p h t", h=2)

        def width(q):
            return HALF if q < QN // 2 else T1

        with nc.Block() as block:
            @block.sync
            def _(sp):
                sp.dma_start(lam_in[:], c["lambda_qk"]).then_inc(loaded, 16)

            @block.tensor
            def _(pe):
                pe.wait_ge(lam_mult, 1)
                nc.tensor.matmul(ps_o[:, 0:2], c["ones"][0:64, :], lam_prod[:], start=True, stop=True).then_inc(lam_sum, 1)
                pe.wait_ge(lam_done, 1)
                with pe.Fori(0, 8) as i:
                    for e in range(2):
                        pe.wait_ge(max_ready[e], i * QN)
                        for h in range(2):
                            mm = nc.tensor.matmul(ps_s[e][:, h, 0:HALF], c["rope_swap"][:], p[:, i + 8 * e, h * HALF:(h + 1) * HALF],
                                                  start=True, stop=True)
                        mm.then_inc(swap_ready, 1)
                    pe.wait_ge(wt_copied, i * QN)
                    pe.wait_ge(rope_done, i * 3 + 3)
                    for j in range(QN):
                        mm = nc.tensor.transpose(ps_t[0:QT, j // 3, (j % 3) * P:(j % 3 + 1) * P], swapped[:, j * QT:(j + 1) * QT],
                                                 c["ident"][:])
                    mm.then_inc(vt_ready, 1)
                    for step in range(QN + 3):
                        if step < QN:
                            n = width(step)
                            for e in range(2):
                                pe.wait_ge(max_ready[e], i * QN + step)
                                for h in range(n // HALF):
                                    mm = nc.tensor.matmul(ps_s[e][0:QT, h, 0:HALF], rot[64 * e:64 * e + 64, 0, step * QT:(step + 1) * QT],
                                                          rot[64 * e:64 * e + 64, 1, h * HALF:(h + 1) * HALF], start=True, stop=True)
                                mm.then_inc(sc_ready[e], 1)
                        q = step - 2
                        if 0 <= q < QN:
                            pe.wait_ge(w_ready, i * QN + q + 1)
                            if q == 0:
                                pe.wait_ge(vt_copied, i + 1)
                            pe.wait_ge(wt_copied, i * QN + q)
                            for j in range(q + 1):
                                mm = nc.tensor.transpose(ps_t[0:QT, j // 3, (j % 3) * QT:(j % 3 + 1) * QT],
                                                         wt[q % 2][:, j * QT:(j + 1) * QT], c["ident"][0:QT, 0:QT])
                            mm.then_inc(wt_ready, 1)
                        q = step - 3
                        if 0 <= q < QN:
                            pe.wait_ge(wt_copied, i * QN + q + 1)
                            pe.wait_ge(pv_copied, i * QN + q)
                            for j in range(q + 1):
                                mm = nc.tensor.matmul(ps_o[:, 0:QT], vt[:, j, :], wT[q % 2][:, j, :], start=(j == 0), stop=(j == q))
                            mm.then_inc(pv_ready, 1)

            @block.scalar
            def _(act):
                act.wait_ge(lam_sum, 1)
                nc.scalar.activation(lam_exp[:], ps_o[:, 0:2], ACT.Exp).then_inc(lam_done, 1)
                with act.Fori(0, 8) as i:
                    act.wait_ge(vt_ready, i + 1)
                    nc.scalar.activation(vt[:].rearrange("p (h j) d -> p h (j d)", h=2), ps_t[0:QT, :, 0:3 * P], ACT.Copy).then_inc(vt_copied, 1)
                    for step in range(QN + 3):
                        if step < QN:
                            for e in range(2):
                                b, sm, n = sc[e][step % 2], small[e][step % 2], width(step)
                                act.wait_ge(max_ready[e], i * QN + step + 1)
                                nc.scalar.activation(b[:, 0:n], b[:, 0:n], ACT.Exp, scale=SCALE, bias=sm[:, 1:2],
                                                     accum_out=sm[:, 2:3]).then_inc(exp_ready[e], 1)
                        q = step - 2
                        if 0 <= q < QN:
                            act.wait_ge(wt_ready, i * QN + q + 1)
                            if q >= 2:
                                act.wait_ge(pv_ready, i * QN + q - 1)
                            m = min(q + 1, 3)
                            cp = nc.scalar.activation(wT[q % 2][:, 0:m, :].rearrange("p j t -> p (j t)"), ps_t[0:QT, 0, 0:m * QT], ACT.Copy)
                            if q >= 3:
                                cp = nc.scalar.activation(wT[q % 2][:, 3:q + 1, :].rearrange("p j t -> p (j t)"),
                                                          ps_t[0:QT, 1, 0:(q - 2) * QT], ACT.Copy)
                            cp.then_inc(wt_copied, 1)
                        q = step - 3
                        if 0 <= q < QN:
                            act.wait_ge(pv_ready, i * QN + q + 1)
                            nc.scalar.activation(o[:, i, q * QT:(q + 1) * QT], ps_o[:, 0:QT], ACT.Copy).then_inc(pv_copied, 1)

            @block.vector
            def _(dve):
                TT, TS = nc.vector.tensor_tensor, nc.vector.tensor_scalar
                head = Chain(dve, order)
                dve.wait_ge(loaded, 16)
                TT(lam_prod[:], lam_in[:, 0:2], lam_in[:, 2:4], ALU.mult).then_inc(lam_mult, 1)
                dve.wait_ge(lam_done, 1)
                head(TT(neg_lam[:], lam_exp[:, 1:2], lam_exp[:, 0:1], ALU.subtract))
                head(TS(neg_lam[:], neg_lam[:], -LAMBDA_INIT, None, ALU.add))
                with dve.Fori(0, 8) as i:
                    chain = Chain(dve, order2, i, 4 + 2 * QN + 4 * QN)
                    for e in range(2):
                        dve.wait_ge(swap_ready, i * 2 + e + 1)
                        if e == 0:
                            dve.wait_ge(sc_ready[1], i * QN)
                            dve.wait_ge(vt_ready, i)
                        chain(TT(hv(swapped[:]), ps_s[e][:, :, 0:HALF], hv(c["rope_sin"][:]), ALU.mult))
                        chain(TT(rot[:, e, :], p[:, i + 8 * e, :], c["rope_cos"][:], ALU.mult))
                        TT(rot[:, e, :], rot[:, e, :], swapped[:], ALU.add).then_inc(rope_done, 1)
                        dve.wait_ge(rope_done, i * 3 + e + 1)
                    nc.vector.tensor_copy(swapped[:], p[:, i + 16, :]).then_inc(rope_done, 1)
                    for step in range(QN + 1):
                        if step < QN:
                            n = width(step)
                            for e in range(2):
                                b, sm = sc[e][step % 2], small[e][step % 2]
                                count = dve.compute_val(i * QN + step + 1)
                                count_2 = dve.compute_val(i * QN + max(step - 1, 0))
                                settle(dve, loaded)
                                dve.wait_ge(sc_ready[e], count)
                                dve.wait_ge(w_ready, count_2)
                                mask = c["mask88"][:, OFF - QT * step:OFF - QT * step + n]
                                if n == HALF:
                                    chain(nc.vector.tensor_tensor_reduce(out=b[:, 0:n], in0=ps_s[e][0:QT, 0, 0:HALF], in1=mask, scale=1.0,
                                                                         scalar=NEG, op0=ALU.add, op1=ALU.max, accum_out=sm[:, 0:1]))
                                else:
                                    chain(nc.vector.tensor_tensor_reduce(out=hv(b[:]), in0=ps_s[e][0:QT, :, 0:HALF], in1=hv(mask), scale=1.0,
                                                                         scalar=NEG, op0=ALU.add, op1=ALU.max, accum_out=sm[:, 0:1]))
                                TS(sm[:, 1:2], sm[:, 0:1], -SCALE, None, ALU.mult).then_inc(max_ready[e], 1)
                        q = step - 1
                        if 0 <= q < QN:
                            n = width(q)
                            b0, b1, s0, s1 = sc[0][q % 2], sc[1][q % 2], small[0][q % 2], small[1][q % 2]
                            dve.wait_ge(exp_ready[0], i * QN + q + 1)
                            dve.wait_ge(exp_ready[1], i * QN + q + 1)
                            if q >= 2:
                                dve.wait_ge(wt_ready, i * QN + q - 1)
                            chain(nc.vector.reciprocal(s0[:, 3:4], s0[:, 2:3]))
                            chain(nc.vector.reciprocal(s1[:, 3:4], s1[:, 2:3]))
                            chain(TT(s1[:, 3:4], s1[:, 3:4], neg_lam[0:QT, :], ALU.mult))
                            chain(TS(b0[:, 0:n], b0[:, 0:n], s0[:, 3:4], None, ALU.mult))
                            nc.vector.scalar_tensor_tensor(out=wt[q % 2][:, 0:n], in0=b1[:, 0:n], scalar=s1[:, 3:4], in1=b0[:, 0:n],
                                                           op0=ALU.mult, op1=ALU.add).then_inc(w_ready, 1)
                    chain.close()


def gated_sum(nc, a, b, gates, out, T):
    K = a.shape[1]
    with stage(nc) as s:
        one, two, done = s.sem("one"), s.sem("two"), s.sem("done")
        with nc.Block() as block:
            @block.gpsimd
            def _(pool):
                with pool.Fori(0, K) as k:
                    nc.gpsimd.tensor_tensor(b[:, k, :], b[:, k, :], gates[:, k + K, :], ALU.mult).then_inc(two, 1)

            @block.vector
            def _(dve):
                with dve.Fori(0, K) as k:
                    nc.vector.tensor_tensor(a[:, k, :], a[:, k, :], gates[:, k, :], ALU.mult).then_inc(one, 1)
                    dve.wait_ge(one, k + 1)
                    dve.wait_ge(two, k + 1)
                    nc.vector.tensor_tensor(out[:, k, :], a[:, k, :], b[:, k, :], ALU.add).then_inc(done, 1)


T2 = 512
NC2 = (T2 - 32) // 16 + 1
TN = T2 // P
CONV_TAPS = 31


def conv_branch(nc, c, u, a):
    PAD = CONV_TAPS - 1
    with stage(nc) as s:
        glu = s.sb("glu", [P, 4, PAD + T2])
        taps = s.sb("taps", [P, 4, CONV_TAPS + 3])
        sq, mean, rstd = s.sb("sq", [P, 4, T2]), s.sb("mean", [P, T2]), s.sb("rstd", [P, T2])
        ps_m, ps_v = s.ps("ps_m", [P, BANK]), s.ps("ps_v", [P, BANK])
        loaded, padded, sig_ready, glu_ready, conv_ready = (s.sem(n) for n in ("loaded", "padded", "sig_ready", "glu_ready", "conv_ready"))
        mean_ready, cen_ready, sq_ready, var_ready, eps_ready, root_ready, norm_ready, order = (
            s.sem(n) for n in ("mean_ready", "cen_ready", "sq_ready", "var_ready", "eps_ready", "root_ready", "norm_ready", "order"))
        with nc.Block() as block:
            @block.sync
            def _(sp):
                sp.dma_start(taps[:], c["conv_taps"]).then_inc(loaded, 16)

            @block.scalar
            def _(act):
                for i in range(4):
                    nc.scalar.activation(u[:, 4 + i, :], u[:, 4 + i, :], ACT.Sigmoid).then_inc(sig_ready, 1)
                for i in range(4):
                    act.wait_ge(cen_ready, i + 1)
                    nc.scalar.activation(sq[:, i, :], a[:, i, :], ACT.Square).then_inc(sq_ready, 1)
                act.wait_ge(eps_ready, 1)
                nc.scalar.activation(rstd[:], rstd[:], ACT.Sqrt).then_inc(root_ready, 1)
                for i in range(4):
                    act.wait_ge(norm_ready, i + 1)
                    nc.scalar.activation(a[:, i, :], a[:, i, :], ACT.Silu, scale=taps[:, i, CONV_TAPS + 1:CONV_TAPS + 2],
                                         bias=taps[:, i, CONV_TAPS + 2:CONV_TAPS + 3])

            @block.tensor
            def _(pe):
                for i in range(4):
                    pe.wait_ge(conv_ready, CONV_TAPS * (i + 1))
                    mm = nc.tensor.matmul(ps_m[:], c["ones"][:], a[:, i, :], start=(i == 0), stop=(i == 3))
                mm.then_inc(mean_ready, 1)
                for i in range(4):
                    pe.wait_ge(sq_ready, i + 1)
                    mm = nc.tensor.matmul(ps_v[:], c["ones"][:], sq[:, i, :], start=(i == 0), stop=(i == 3))
                mm.then_inc(var_ready, 1)

            @block.vector
            def _(dve):
                TT, TS = nc.vector.tensor_tensor, nc.vector.tensor_scalar
                chain = Chain(dve, order)
                nc.vector.memset(glu[:, :, 0:PAD], 0.0).then_inc(padded, 1)
                for i in range(4):
                    dve.wait_ge(sig_ready, i + 1)
                    TT(glu[:, i, PAD:PAD + T2], u[:, i, :], u[:, 4 + i, :], ALU.mult).then_inc(glu_ready, 1)
                dve.wait_ge(glu_ready, 4)
                dve.wait_ge(padded, 1)
                dve.wait_ge(loaded, 16)
                for i in range(4):
                    TS(a[:, i, :], glu[:, i, 0:T2], taps[:, i, 0:1], taps[:, i, CONV_TAPS:CONV_TAPS + 1], ALU.mult,
                       ALU.add).then_inc(conv_ready, 1)
                    for j in range(1, CONV_TAPS):
                        dve.wait_ge(conv_ready, CONV_TAPS * i + j)
                        nc.vector.scalar_tensor_tensor(out=a[:, i, :], in0=glu[:, i, j:j + T2], scalar=taps[:, i, j:j + 1],
                                                       in1=a[:, i, :], op0=ALU.mult, op1=ALU.add).then_inc(conv_ready, 1)
                dve.wait_ge(mean_ready, 1)
                chain(TS(mean[:], ps_m[:], 1.0 / 512, None, ALU.mult))
                for i in range(4):
                    TT(a[:, i, :], a[:, i, :], mean[:], ALU.subtract).then_inc(cen_ready, 1)
                dve.wait_ge(var_ready, 1)
                TS(rstd[:], ps_v[:], 1.0 / 512, 1e-6, ALU.mult, ALU.add).then_inc(eps_ready, 1)
                dve.wait_ge(root_ready, 1)
                chain(nc.vector.reciprocal(rstd[:], rstd[:]))
                for i in range(4):
                    TT(a[:, i, :], a[:, i, :], rstd[:], ALU.mult).then_inc(norm_ready, 1)


def bias_tables(nc, c, bias_scr, bias_rows, bias_cmp):
    W = bias_scr.shape[1]
    NB = bias_cmp.shape[1]
    with stage(nc) as s:
        rb = s.sb("rb", [33, 8])
        rev = s.sb("rev", [33, W])
        fwd = s.sb("fwd", [33, c["buckets_fwd"].shape[1]])
        row = s.sb("row", [8, 2, W // 2])
        ps_r, ps_c = s.ps("ps_r", [P, 2, BANK]), s.ps("ps_c", [P, BANK])
        down, up = s.sb("down", [P, 8, T2]), s.sb("up", [P, 8, T2])
        ps_u = [s.ps("ps_u", [P, BANK]) for _ in range(2)]
        filled, loaded, prod, out, stored, cmp_done, rows_in, turn_ready, turned = (
            s.sem(n) for n in ("filled", "loaded", "prod", "out", "stored", "cmp_done", "rows_in", "turn_ready", "turned"))
        with nc.Block() as block:
            @block.sync
            def _(sp):
                sp.dma_start(rb[0:32, :], c["rel_bias"]).then_inc(loaded, 16)
                sp.dma_start(rev[:], c["buckets_rev"]).then_inc(loaded, 16)
                sp.dma_start(fwd[:], c["buckets_fwd"]).then_inc(loaded, 16)
                sp.wait_ge(out, 1)
                sp.dma_start(bias_scr.rearrange("h (a w) -> h a w", a=2), row[:]).then_inc(stored, 16)
                sp.wait_ge(stored, 16)
                for h in range(8):
                    src = bass.AP(tensor=bias_scr.tensor, offset=bias_scr.offset + h * W, ap=[[1, P], [1, T2]])
                    sp.dma_start(down[:, h, :], src).then_inc(rows_in, 16)
                for h in range(8):
                    sp.wait_ge(turned, h + 1)
                    sp.dma_start(bias_rows[h], up[:, h, :]).then_inc(stored, 16)
                sp.wait_ge(stored, 16 * 9)

            @block.vector
            def _(dve):
                nc.vector.memset(rb[32:33, :], NEG).then_inc(filled, 1)
                dve.wait_ge(prod, 1)
                nc.vector.tensor_copy(row[:], ps_r[0:8, :, 0:W // 2]).then_inc(out, 1)
                dve.wait_ge(prod, 2)
                nc.vector.tensor_copy(bias_cmp[:].rearrange("p m h -> p (m h)"), ps_c[:, 0:NB * 8]).then_inc(cmp_done, 1)
                for h in range(8):
                    dve.wait_ge(turn_ready, h + 1)
                    nc.vector.tensor_copy(up[:, h, :], ps_u[h % 2][:]).then_inc(turned, 1)

            @block.tensor
            def _(pe):
                pe.wait_ge(loaded, 48)
                pe.wait_ge(filled, 1)
                for h in range(2):
                    mm = nc.tensor.matmul(ps_r[0:8, h, 0:W // 2], rb[:], rev[:, h * W // 2:(h + 1) * W // 2], start=True, stop=True)
                mm.then_inc(prod, 1)
                for m in range(NB):
                    z = 353 - 16 * m + 511
                    mm = nc.tensor.matmul(ps_c[:, m * 8:(m + 1) * 8], fwd[:, z:z + P], rb[:], start=True, stop=True)
                mm.then_inc(prod, 1)
                pe.wait_ge(rows_in, 16 * 8)
                for h in range(8):
                    pe.wait_ge(turned, max(h - 1, 0))
                    nc.tensor.matmul(ps_u[h % 2][:], c["upside_down"][:], down[:, h, :], start=True, stop=True).then_inc(turn_ready, 1)


def compress(nc, c, kv, k_cmp, v_cmp):
    with stage(nc) as s:
        pe_in = [s.sb("pe_in", [P, 32, NC2]) for _ in range(2)]
        win = [s.sb("win", [P, 32, NC2]) for _ in range(2)]
        w1 = [s.sb("w1", [P, 32, 256]) for _ in range(2)]
        w2 = [s.sb("w2", [P, 2, 64]) for _ in range(2)]
        hid = [[s.sb("hid", [P, 2, NC2]) for _ in range(2)] for _ in range(2)]
        ps_h = [[s.ps("ps_h", [P, BANK]) for _ in range(2)] for _ in range(2)]
        ps_k, ps_v = s.ps("ps_k", [P, BANK]), s.ps("ps_v", [P, BANK])
        loaded = [s.sem("loaded") for _ in range(2)]
        win_ready, hid_ready, gelu_ready, out_ready, copied = (s.sem(n) for n in ("win_ready", "hid_ready", "gelu_ready", "out_ready", "copied"))
        with nc.Block() as block:
            @block.sync
            def _(sp):
                for b in range(2):
                    sp.dma_start(pe_in[b][:], c["cmp_pe"][b]).then_inc(loaded[b], 16)
                    for g in range(2):
                        sp.dma_start(w1[b][64 * g:64 * g + 64, :, :], c["cmp_w1"][b]).then_inc(loaded[b], 16)
                    sp.dma_start(w2[b][:], c["cmp_w2"][b]).then_inc(loaded[b], 16)

            @block.vector
            def _(dve):
                for b in range(2):
                    dve.wait_ge(loaded[b], 64)
                    for half in range(2):
                        v = kv[:, b, 16 * half:16 * half + 16 * NC2].rearrange("p (c l) -> p l c", l=16)
                        r = nc.vector.tensor_tensor(win[b][:, 16 * half:16 * half + 16, :], v, pe_in[b][:, 16 * half:16 * half + 16, :], ALU.add)
                    r.then_inc(win_ready, 1)

            @block.tensor
            def _(pe):
                for b in range(2):
                    pe.wait_ge(win_ready, b + 1)
                    for h in range(2):
                        for l in range(32):
                            for g in range(2):
                                rows = slice(64 * g, 64 * g + 64)
                                mm = nc.tensor.matmul(ps_h[b][g][:, h * NC2:(h + 1) * NC2], w1[b][rows, l, h * P:(h + 1) * P],
                                                      win[b][rows, l, :], start=(l == 0), stop=(l == 31))
                    mm.then_inc(hid_ready, 1)
                pe.wait_ge(gelu_ready, 4)
                for g in range(2):
                    for h in range(2):
                        nc.tensor.matmul(ps_k[64 * g:64 * g + 64, 0:NC2], w2[0][:, h, :], hid[0][g][:, h, :], start=(h == 0), stop=(h == 1))
                for g in range(2):
                    for h in range(2):
                        mm = nc.tensor.matmul(ps_v[0:NC2, 64 * g:64 * g + 64], hid[1][g][:, h, :], w2[1][:, h, :], start=(h == 0), stop=(h == 1))
                mm.then_inc(out_ready, 1)

            @block.scalar
            def _(act):
                for b in range(2):
                    act.wait_ge(hid_ready, b + 1)
                    for g in range(2):
                        nc.scalar.activation(hid[b][g][:].rearrange("p h c -> p (h c)"), ps_h[b][g][:, 0:2 * NC2],
                                             ACT.Gelu_apprx_tanh).then_inc(gelu_ready, 1)
                act.wait_ge(out_ready, 1)
                nc.scalar.activation(k_cmp[:], ps_k[:, 0:NC2], ACT.Copy)
                nc.scalar.activation(v_cmp[:], ps_v[0:NC2, 0:P], ACT.Copy).then_inc(copied, 1)


def nsa_attention(nc, c, q, kv, ng, bias_rows, bias_cmp, k_cmp, v_cmp, o):
    assert T2 // 64 <= 16 and T2 <= 512
    NU = TN * 2 * 3
    units = [(qi, e, br) for qi in range(TN) for e in range(2) for br in range(3)]
    with stage(nc) as s:
        sig = s.sb("sig", [P, T2])
        gate = s.sb("gate", [P, TN, 32])
        gs = s.sb("gs", [P, TN, 6])
        vt = s.sb("vt", [P, 2, TN, P])
        qs = s.sb("qs", [P, T2])
        bias = s.sb("bias", [P, 2, T2])
        bc = s.sb("bc", [P, 2, bias_cmp.shape[1]])
        pr = [s.sb("pr", [P, T2]) for _ in range(4)]
        wn = [s.sb("wn", [P, T2]) for _ in range(4)]
        wT = [s.sb("wT", [P, TN, P]) for _ in range(3)]
        small = [s.sb("small", [P, 4]) for _ in range(4)]
        ps_s = [s.ps("ps_s", [P, BANK]) for _ in range(3)]
        ps_t = [s.ps("ps_t", [P, BANK]) for _ in range(2)]
        ps_o = [s.ps("ps_o", [P, BANK]) for _ in range(2)]
        sig_ready, vt_ready, vt_copied, bias_in, head_ready = (s.sem(n) for n in ("sig_ready", "vt_ready", "vt_copied", "bias_in", "head_ready"))
        sc_ready, max_ready, exp_ready, r_ready, w_ready, wt_ready, wt_copied, pv_ready, o_copied, order = (
            s.sem(n) for n in ("sc_ready", "max_ready", "exp_ready", "r_ready", "w_ready", "wt_ready", "wt_copied", "pv_ready", "o_copied", "order"))

        def keys(u):
            return NC2 if units[u][2] == 2 else P * (units[u][0] + 1)

        with nc.Block() as block:
            @block.sync
            def _(sp):
                with sp.Fori(0, 4) as i:
                    sp.wait_ge(max_ready, i * NU)
                    for e in range(2):
                        sp.dma_start(bias[:, e, :], bias_rows[i + 4 * e]).then_inc(bias_in, 16)

            @block.tensor
            def _(pe):
                pe.wait_ge(sig_ready, 1)
                for j in range(TN):
                    nc.tensor.transpose(ps_s[0][:, j * P:(j + 1) * P], sig[:, j * P:(j + 1) * P], c["ident"][:])
                for b in range(2):
                    for j in range(TN):
                        mm = nc.tensor.transpose(ps_t[b][:, j * P:(j + 1) * P], kv[:, 3 + 2 * b, j * P:(j + 1) * P], c["ident"][:])
                mm.then_inc(vt_ready, 1)
                pe.wait_ge(vt_copied, 1)
                with pe.Fori(0, 4) as i:
                    pe.wait_ge(head_ready, i + 1)
                    for step in range(NU + 4):
                        if step < NU:
                            qi, e, br = units[step]
                            rows = slice(64 * e, 64 * e + 64)
                            pe.wait_ge(max_ready, i * NU + max(step - 2, 0))
                            k = k_cmp[rows, :] if br == 2 else kv[rows, 2 + 2 * br, 0:P * (qi + 1)]
                            nc.tensor.matmul(ps_s[step % 3][:, 0:keys(step)], qs[rows, qi * P:(qi + 1) * P], k,
                                             start=True, stop=True).then_inc(sc_ready, 1)
                        u = step - 3
                        if 0 <= u < NU:
                            n = keys(u)
                            pe.wait_ge(w_ready, i * NU + u + 1)
                            pe.wait_ge(wt_copied, i * NU + max(u - 1, 0))
                            if units[u][2] == 2:
                                mm = nc.tensor.transpose(ps_t[u % 2][0:NC2, 0:P], wn[u % 4][:, 0:NC2], c["ident"][:])
                            else:
                                for j in range(n // P):
                                    mm = nc.tensor.transpose(ps_t[u % 2][:, j * P:(j + 1) * P], wn[u % 4][:, j * P:(j + 1) * P], c["ident"][:])
                            mm.then_inc(wt_ready, 1)
                        u = step - 4
                        if 0 <= u < NU:
                            qi, e, br = units[u]
                            rows = slice(64 * e, 64 * e + 64)
                            pe.wait_ge(wt_copied, i * NU + u + 1)
                            if br == 0:
                                pe.wait_ge(o_copied, i * 2 * TN + max(2 * (qi - 1) + e + 1, 0))
                            if br == 2:
                                mm = nc.tensor.matmul(ps_o[e][rows, 0:P], v_cmp[:, rows], wT[u % 3][0:NC2, 0, :], start=False, stop=True)
                            else:
                                for j in range(qi + 1):
                                    mm = nc.tensor.matmul(ps_o[e][rows, 0:P], vt[:, br, j, rows], wT[u % 3][:, j, :],
                                                          start=(br == 0 and j == 0), stop=False)
                            mm.then_inc(pv_ready, 1)

            @block.scalar
            def _(act):
                nc.scalar.activation(sig[:], ng, ACT.Sigmoid).then_inc(sig_ready, 1)
                act.wait_ge(vt_ready, 1)
                nc.scalar.activation(gate[:], ps_s[0][:].rearrange("p (j t) -> p j t", j=TN)[:, :, 0:32], ACT.Copy)
                for b in range(2):
                    cp = nc.scalar.activation(vt[:, b, :, :].rearrange("p j d -> p (j d)"), ps_t[b][:], ACT.Copy)
                cp.then_inc(vt_copied, 1)
                with act.Fori(0, 4) as i:
                    for step in range(NU + 4):
                        if step < NU:
                            sm, b = small[step % 4], pr[step % 4][:, 0:keys(step)]
                            act.wait_ge(max_ready, i * NU + step + 1)
                            nc.scalar.activation(b, b, ACT.Exp, bias=sm[:, 1:2], accum_out=sm[:, 2:3]).then_inc(exp_ready, 1)
                        u = step - 3
                        if 0 <= u < NU:
                            act.wait_ge(wt_ready, i * NU + u + 1)
                            act.wait_ge(pv_ready, i * NU + max(u - 2, 0))
                            n = keys(u)
                            if units[u][2] == 2:
                                cp = nc.scalar.activation(wT[u % 3][0:NC2, 0, :], ps_t[u % 2][0:NC2, 0:P], ACT.Copy)
                            else:
                                cp = nc.scalar.activation(wT[u % 3][:].rearrange("p j t -> p (j t)")[:, 0:n], ps_t[u % 2][:, 0:n], ACT.Copy)
                            cp.then_inc(wt_copied, 1)
                        u = step - 4
                        if 0 <= u < NU and units[u][2] == 2:
                            qi, e, br = units[u]
                            rows = slice(64 * e, 64 * e + 64)
                            act.wait_ge(pv_ready, i * NU + u + 1)
                            nc.scalar.activation(o[rows, i, qi * P:(qi + 1) * P], ps_o[e][rows, 0:P], ACT.Copy).then_inc(o_copied, 1)

            @block.gpsimd
            def _(pool):
                with pool.Fori(0, 4) as i:
                    for u in range(NU):
                        pool.wait_ge(r_ready, i * NU + u + 1)
                        pool.wait_ge(wt_ready, i * NU + max(u - 3, 0))
                        nc.gpsimd.tensor_tensor(wn[u % 4][:, 0:keys(u)], pr[u % 4][:, 0:keys(u)],
                                                small[u % 4][:, 3:4].broadcast_to([P, keys(u)]), ALU.mult).then_inc(w_ready, 1)

            @block.vector
            def _(dve):
                TT, TS = nc.vector.tensor_tensor, nc.vector.tensor_scalar
                dve.wait_ge(vt_copied, 1)
                with dve.Fori(0, 4) as i:
                    chain = Chain(dve, order, i, 3 + NU * 2 + 2)
                    dve.wait_ge(sc_ready, i * NU)
                    dve.wait_ge(w_ready, i * NU)
                    chain(TS(qs[:], q[:, i, :], 0.125, None, ALU.mult))
                    chain(nc.vector.tensor_copy(gs[:], gate[:, :, bass.ds(6 * i, 6)]))
                    chain(nc.vector.tensor_copy(bc[:, 0, :], bias_cmp[:, :, bass.ds(i, 1)].rearrange("p m h -> p (m h)")))
                    nc.vector.tensor_copy(bc[:, 1, :], bias_cmp[:, :, bass.ds(i + 4, 1)].rearrange("p m h -> p (m h)")).then_inc(head_ready, 1)
                    dve.wait_ge(head_ready, i + 1)
                    dve.wait_ge(bias_in, i * 32 + 32)
                    for step in range(NU + 1):
                        if step < NU:
                            qi, e, br = units[step]
                            sm, n = small[step % 4], keys(step)
                            count = dve.compute_val(i * NU + step + 1)
                            count_2 = dve.compute_val(i * NU + max(step - 3, 0))
                            settle(dve, vt_copied)
                            dve.wait_ge(sc_ready, count)
                            dve.wait_ge(w_ready, count_2)
                            b = bc[:, e, 24 - 8 * qi:24 - 8 * qi + NC2] if br == 2 else bias[:, e, T2 - n:T2]
                            chain(nc.vector.tensor_tensor_reduce(out=pr[step % 4][:, 0:n], in0=ps_s[step % 3][:, 0:n], in1=b, scale=1.0,
                                                                 scalar=3 * NEG, op0=ALU.add, op1=ALU.max, accum_out=sm[:, 0:1]))
                            TS(sm[:, 1:2], sm[:, 0:1], -1.0, None, ALU.mult).then_inc(max_ready, 1)
                        u = step - 1
                        if 0 <= u < NU:
                            qi, e, br = units[u]
                            sm = small[u % 4]
                            dve.wait_ge(exp_ready, i * NU + u + 1)
                            chain(nc.vector.reciprocal(sm[:, 3:4], sm[:, 2:3]))
                            g = gs[:, qi, 3 * e + (1, 2, 0)[br]:3 * e + (1, 2, 0)[br] + 1]
                            if br == 2 and qi == 0:
                                chain(TT(sm[:, 3:4], sm[:, 3:4], c["row_valid"][:], ALU.mult))
                            TT(sm[:, 3:4], sm[:, 3:4], g, ALU.mult).then_inc(r_ready, 1)
                    chain.close()


def ffn_up(nc, c, w, h, dst):
    N = w.shape[0]
    with stage(nc) as s:
        taps = s.sb("taps", [P, 2 * N, 4])
        wbuf = [s.sb("wbuf", [P, 8, P]) for _ in range(4)]
        acc = [s.ps("acc", [P, BANK]) for _ in range(4)]
        raw = [s.sb("raw", [P, 2 + T2]) for _ in range(4)]
        cv = [s.sb("cv", [P, T2]) for _ in range(4)]
        w_loaded, acc_ready, acc_free = ([s.sem(n) for _ in range(4)] for n in ("w_loaded", "acc_ready", "acc_free"))
        loaded, padded, conv_ready, gelu_ready, done = (s.sem(n) for n in ("loaded", "padded", "conv_ready", "gelu_ready", "done"))
        orders = [s.sem("order") for _ in range(4)]
        with nc.Block() as block:
            @block.sync
            def _(sp):
                sp.dma_start(taps[:], c["ffn_taps"]).then_inc(loaded, 16)
                with sp.Fori(0, N // 2) as it:
                    for b in range(4):
                        sp.wait_ge(acc_ready[b], it)
                        sp.dma_start(wbuf[b][:], w[it * 2 + b // 2, b % 2]).then_inc(w_loaded[b], 16)

            @block.tensor
            def _(pe):
                with pe.Fori(0, N // 2) as it:
                    for b in range(4):
                        pe.wait_ge(acc_free[b], it)
                        pe.wait_ge(w_loaded[b], it * 16 + 16)
                        for k in range(8):
                            mm = nc.tensor.matmul(acc[b][:], wbuf[b][:, k, :], h[:, k, :], start=(k == 0), stop=(k == 7))
                        mm.then_inc(acc_ready[b], 1)

            @block.scalar
            def _(act):
                act.wait_ge(padded, 1)
                with act.Fori(0, N // 2) as it:
                    for b in range(4):
                        act.wait_ge(acc_ready[b], it + 1)
                        act.wait_ge(conv_ready, it * 4)
                        nc.scalar.activation(raw[b][:, 2:2 + T2], acc[b][:], ACT.Copy).then_inc(acc_free[b], 1)
                    for g in range(2):
                        act.wait_ge(conv_ready, it * 4 + 2 * g + 1)
                        nc.scalar.activation(cv[2 * g][:], cv[2 * g][:], ACT.Gelu_apprx_tanh).then_inc(gelu_ready, 1)

            @block.vector
            def _(dve):
                for b in range(4):
                    ms = nc.vector.memset(raw[b][:, 0:2], 0.0)
                ms.then_inc(padded, 1)
                dve.wait_ge(padded, 1)
                dve.wait_ge(loaded, 16)
                with dve.Fori(0, N // 2) as it:
                    dve.wait_ge(done, it * 2)
                    for b in range(4):
                        dve.wait_ge(acc_free[b], it + 1)
                        n = (it * 2 + b // 2) + N * (b % 2)

                        def tap(j):
                            return taps[:, n, j:j + 1]
                        nc.vector.tensor_scalar(cv[b][:], raw[b][:, 2:2 + T2], tap(2), tap(3), ALU.mult, ALU.add).then_inc(orders[b], 1)
                        dve.wait_ge(orders[b], it * 2 + 1)
                        nc.vector.scalar_tensor_tensor(out=cv[b][:], in0=raw[b][:, 1:1 + T2], scalar=tap(1), in1=cv[b][:],
                                                       op0=ALU.mult, op1=ALU.add).then_inc(orders[b], 1)
                        dve.wait_ge(orders[b], it * 2 + 2)
                        nc.vector.scalar_tensor_tensor(out=cv[b][:], in0=raw[b][:, 0:T2], scalar=tap(0), in1=cv[b][:],
                                                       op0=ALU.mult, op1=ALU.add).then_inc(conv_ready, 1)
                    for g in range(2):
                        dve.wait_ge(gelu_ready, it * 2 + g + 1)
                        dve.wait_ge(conv_ready, it * 4 + 2 * g + 2)
                        nc.vector.tensor_tensor(dst[:, it * 2 + g, :], cv[2 * g][:], cv[2 * g + 1][:], ALU.mult).then_inc(done, 1)


def add_product(nc, x, a, b):
    K = x.shape[1]
    with stage(nc) as s:
        one, done = s.sem("one"), s.sem("done")
        with nc.Block() as block:
            @block.gpsimd
            def _(pool):
                with pool.Fori(0, K) as k:
                    nc.gpsimd.tensor_tensor(a[:, k, :], a[:, k, :], b[:, k, :], ALU.mult).then_inc(one, 1)

            @block.vector
            def _(dve):
                with dve.Fori(0, K) as k:
                    dve.wait_ge(one, k + 1)
                    nc.vector.tensor_tensor(x[:, k, :], x[:, k, :], a[:, k, :], ALU.add).then_inc(done, 1)


GC = 16
GN = T2 // GC
DC = 64
DN = T2 // DC
LEVELS3 = 6
K_SCALE = 128 ** -0.5


def gate_rows(nc, c, small, rows):
    with stage(nc) as s:
        raw = s.sb("raw", [4, 4, T2])
        b = s.sb("b", [4, 4])
        ax, lin, fwd = s.sb("ax", [4, 2, T2]), s.sb("lin", [4, 2, T2]), s.sb("cum", [4, T2])
        ea, end = s.sb("ea", [4, 1]), s.sb("end", [4, T2])
        loaded, x_ready, ln_ready, order, bd_ready, exp_done, end_ready = (
            s.sem(n) for n in ("loaded", "x_ready", "ln_ready", "order", "bd_ready", "exp_done", "end_ready"))
        with nc.Block() as block:
            @block.sync
            def _(sp):
                sp.dma_start(b[:], c["gate_bias"]).then_inc(loaded, 16)
                for j in range(4):
                    sp.dma_start(raw[:, j, :], small[32 * j:32 * j + 4, :]).then_inc(loaded, 16)

            @block.scalar
            def _(act):
                act.wait_ge(x_ready, 2)
                nc.scalar.activation(ax[:], lin[:], ACT.Abs).then_inc(ln_ready, 1)
                act.wait_ge(ln_ready, 1)
                nc.scalar.activation(ax[:], ax[:], ACT.Exp, scale=-1.0).then_inc(ln_ready, 1)
                act.wait_ge(ln_ready, 2)
                nc.scalar.activation(ax[:], ax[:], ACT.Ln, bias=1.0)
                nc.scalar.activation(ea[:], b[:, 3:4], ACT.Exp)
                nc.scalar.activation(rows[:, 5, :], raw[:, 2, :], ACT.Sigmoid).then_inc(ln_ready, 1)
                act.wait_ge(bd_ready, 1)
                nc.scalar.activation(rows[:, 4, :], rows[:, 3, :], ACT.Exp).then_inc(exp_done, 1)
                act.wait_ge(end_ready, 1)
                nc.scalar.activation(rows[:, 7, :], end[:], ACT.Exp)

            @block.vector
            def _(dve):
                TT, TS, STT = nc.vector.tensor_tensor, nc.vector.tensor_scalar, nc.vector.scalar_tensor_tensor
                chain = Chain(dve, order)
                dve.wait_ge(loaded, 80)
                TS(lin[:, 0, :], raw[:, 1, :], b[:, 1:2], None, ALU.add).then_inc(x_ready, 1)
                TS(lin[:, 1, :], raw[:, 3, :], b[:, 2:3], None, ALU.add).then_inc(x_ready, 1)
                dve.wait_ge(x_ready, 2)
                dve.wait_ge(ln_ready, 3)
                chain(STT(out=lin[:, 0, :], in0=lin[:, 0, :], scalar=0.0, in1=ax[:, 0, :], op0=ALU.min, op1=ALU.subtract))
                chain(STT(out=lin[:, 1, :], in0=lin[:, 1, :], scalar=0.0, in1=ax[:, 1, :], op0=ALU.max, op1=ALU.add))
                chain(nc.vector.tensor_tensor_scan(fwd[:], c["ones"][0:4, 0:1].broadcast_to([4, T2]), lin[:, 0, :], 0.0, ALU.mult, ALU.add))
                chain(STT(out=rows[:, 0, :], in0=raw[:, 0, :], scalar=b[:, 0:1], in1=fwd[:], op0=ALU.add, op1=ALU.subtract))
                chain(nc.vector.tensor_tensor_scan(rows[:, 1, :], rows[:, 0, :], rows[:, 0, :], 0.0, ALU.max, ALU.max))
                chain(STT(out=rows[:, 2, :], in0=fwd[:], scalar=-1.0, in1=rows[:, 1, :], op0=ALU.mult, op1=ALU.subtract))
                chain(TS(lin[:, 1, :], lin[:, 1, :], ea[:, 0:1], -1.0, ALU.mult, ALU.mult))
                nc.vector.tensor_tensor_scan(rows[:, 3, :], c["chunk_start64"][0:4, :], lin[:, 1, :], 0.0, ALU.mult, ALU.add).then_inc(bd_ready, 1)
                dve.wait_ge(bd_ready, 1)
                bd = rows[:, 3, :].rearrange("p (n t) -> p n t", t=DC)
                TT(end[:].rearrange("p (n t) -> p n t", t=DC), bd[:, :, DC - 1:DC].broadcast_to([4, DN, DC]), bd, ALU.subtract).then_inc(end_ready, 1)
                dve.wait_ge(exp_done, 1)
                STT(out=rows[:, 6, :], in0=rows[:, 4, :], scalar=-1.0, in1=rows[:, 5, :], op0=ALU.mult, op1=ALU.mult)


def mlstm(nc, c, z, rows, o):
    with stage(nc) as s:
        gcol = s.sb("gcol", [P, TN, 4])
        sel = s.sb("sel", [4, P])
        kv = s.sb("kv", [P, 2, T2])
        qs, sig = s.sb("qs", [P, T2]), s.sb("sig", [P, T2])
        vt = s.sb("vt", [P, TN, P])
        mb, em = s.sb("mb", [P, T2]), s.sb("em", [P, T2])
        ex = [s.sb("ex", [P, T2]) for _ in range(2)]
        pt = [s.sb("pt", [P, T2]) for _ in range(2)]
        den = s.sb("den", [P, T2])
        k_scale, scale_set = s.sb("k_scale", [P, 1]), s.sem("scale_set")
        ps_b, ps_e, ps_v, ps_o, ps_d = (s.ps(n, [P, BANK]) for n in ("ps_b", "ps_e", "ps_v", "ps_o", "ps_d"))
        ps_k = [s.ps("ps_k", [P, BANK]) for _ in range(2)]
        (col_ready, col_copied, fixed, bc_ready, vt_ready, vt_copied, mb_ready, em_ready, kq_ready, arg_ready, ex_ready,
         pt_ready, o_ready, done, order) = (s.sem(n) for n in (
             "col_ready", "col_copied", "fixed", "bc_ready", "vt_ready", "vt_copied", "mb_ready", "em_ready", "kq_ready", "arg_ready",
             "ex_ready", "pt_ready", "o_ready", "done", "order"))
        with nc.Block() as block:
            @block.tensor
            def _(pe):
                for j in range(TN):
                    mm = nc.tensor.transpose(ps_b[:, 4 * j:4 * j + 4], rows[:, 0, j * P:(j + 1) * P], c["ident"][0:4, 0:4])
                mm.then_inc(col_ready, 1)
                pe.wait_ge(col_copied, 1)
                with pe.Fori(0, 4) as h:
                    pe.wait_ge(fixed, h + 1)
                    pe.wait_ge(done, h)
                    nc.tensor.matmul(ps_b[:], sel[:], rows[:, 1, :], start=True, stop=True)
                    nc.tensor.matmul(ps_e[:], sel[:], rows[:, 2, :], start=True, stop=True).then_inc(bc_ready, 1)
                    for j in range(TN):
                        mm = nc.tensor.transpose(ps_v[:, j * P:(j + 1) * P], kv[:, 1, j * P:(j + 1) * P], c["ident"][:])
                    mm.then_inc(vt_ready, 1)
                    for j in range(TN + 1):
                        if j < TN:
                            n = T2 - j * P
                            pe.wait_ge(pt_ready, h * TN + max(j - 1, 0))
                            nc.tensor.matmul(ps_k[j % 2][:, 0:n], kv[:, 0, j * P:(j + 1) * P], qs[:, j * P:T2],
                                             start=True, stop=True).then_inc(kq_ready, 1)
                        if j > 0:
                            i = j - 1
                            n = T2 - i * P
                            if i == 0:
                                pe.wait_ge(vt_copied, h + 1)
                            pe.wait_ge(pt_ready, h * TN + i + 1)
                            nc.tensor.matmul(ps_o[:, i * P:T2], vt[:, i, :], pt[i % 2][:, 0:n], start=(i == 0), stop=(i == TN - 1))
                            nc.tensor.matmul(ps_d[:, i * P:T2], c["ones"][:], pt[i % 2][:, 0:n], start=(i == 0),
                                             stop=(i == TN - 1)).then_inc(o_ready, 1)

            @block.gpsimd
            def _(pool):
                nc.gpsimd.memset(k_scale[:], K_SCALE).then_inc(scale_set, 1)
                pool.wait_ge(scale_set, 1)
                with pool.Fori(0, 4) as h:
                    pool.wait_ge(o_ready, h * TN)
                    nc.gpsimd.tensor_copy(kv[:, 0, :], z[:, h + 4, :])
                    nc.gpsimd.tensor_copy(kv[:, 1, :], z[:, h + 8, :])
                    nc.gpsimd.tensor_copy(sel[:], c["head_sel"][:, h, :])
                    nc.gpsimd.tensor_tensor(qs[:], z[:, h, :], k_scale[:].broadcast_to([P, T2]), ALU.mult).then_inc(fixed, 1)

            @block.scalar
            def _(act):
                act.wait_ge(col_ready, 1)
                nc.scalar.activation(gcol[:].rearrange("p j h -> p (j h)"), ps_b[:, 0:4 * TN], ACT.Copy).then_inc(col_copied, 1)
                act.wait_ge(col_copied, 1)
                with act.Fori(0, 4) as h:
                    act.wait_ge(bc_ready, h + 1)
                    act.wait_ge(done, h)
                    nc.scalar.activation(em[:], ps_e[:], ACT.Exp).then_inc(em_ready, 1)
                    act.wait_ge(vt_ready, h + 1)
                    nc.scalar.activation(vt[:].rearrange("p j d -> p (j d)"), ps_v[:], ACT.Copy).then_inc(vt_copied, 1)
                    for j in range(TN):
                        n = T2 - j * P
                        act.wait_ge(arg_ready, h * TN + j + 1)
                        nc.scalar.activation(ex[j % 2][:, 0:n], ex[j % 2][:, 0:n], ACT.Exp, bias=gcol[:, j, bass.ds(h, 1)]).then_inc(ex_ready, 1)
                    nc.scalar.activation(sig[:], z[:, h + 12, :], ACT.Sigmoid).then_inc(ex_ready, 1)

            @block.vector
            def _(dve):
                TT, STT = nc.vector.tensor_tensor, nc.vector.scalar_tensor_tensor
                with dve.Fori(0, 4) as h:
                    chain = Chain(dve, order, h, 5)
                    dve.wait_ge(bc_ready, h + 1)
                    chain(nc.vector.tensor_copy(mb[:], ps_b[:]))
                    for j in range(TN + 1):
                        if j < TN:
                            n = T2 - j * P
                            dve.wait_ge(pt_ready, h * TN + max(j - 1, 0))
                            TT(ex[j % 2][:, 0:n], c["mask_st"][:, 0:n], mb[:, j * P:T2], ALU.subtract).then_inc(arg_ready, 1)
                        if j > 0:
                            i = j - 1
                            n = T2 - i * P
                            dve.wait_ge(ex_ready, h * (TN + 1) + i + 1)
                            dve.wait_ge(kq_ready, h * TN + i + 1)
                            dve.wait_ge(o_ready, h * TN + max(i - 1, 0))
                            TT(pt[i % 2][:, 0:n], ps_k[i % 2][:, 0:n], ex[i % 2][:, 0:n], ALU.mult).then_inc(pt_ready, 1)
                    dve.wait_ge(o_ready, h * TN + TN)
                    dve.wait_ge(em_ready, h + 1)
                    dve.wait_ge(ex_ready, h * (TN + 1) + TN + 1)
                    chain(TT(den[:], ps_d[:], em[:], ALU.max))
                    chain(STT(out=den[:], in0=ps_d[:], scalar=-1.0, in1=den[:], op0=ALU.mult, op1=ALU.max))
                    chain(nc.vector.reciprocal(den[:], den[:]))
                    chain(TT(den[:], den[:], sig[:], ALU.mult))
                    TT(o[:, h, :], ps_o[:], den[:], ALU.mult).then_inc(done, 1)
                    chain.close()


def gla_intra(nc, c, z, lr, o, dec, tok_scr):
    NB = 4 * GN
    with stage(nc) as s:
        wl, bl = s.sb("wl", [16, 512]), s.sb("bl", [P, 4])
        cum = s.sb("cum", [P, 4, T2])
        lin, ax = s.sb("lin", [P, 4, T2]), s.sb("ax", [P, 4, T2])
        kd = s.sb("kd", [P, 4, T2])
        ex = [s.sb("ex", [P, 4, T2]) for _ in range(2)]
        tk = [s.sb("tk", [P, 512]) for _ in range(2)]
        ps = s.ps("ps", [P, 4, BANK])
        ps_w = s.ps("ps_w", [P, 4, BANK])
        (loaded, x_ready, lin_ready, ax_ready, ln_ready, cum_ready, order, e_ready, k_ready, a_ready, p_ready,
         tr_ready, tr_copied, eb_ready, lag_ready, lag_exp, kq_ready, sum_ready, av_ready) = (s.sem(n) for n in (
             "loaded", "x_ready", "lin_ready", "ax_ready", "ln_ready", "cum_ready", "order", "e_ready", "k_ready", "a_ready", "p_ready",
             "tr_ready", "tr_copied", "eb_ready", "lag_ready", "lag_exp", "kq_ready", "sum_ready", "av_ready"))

        stored = [s.sem("stored") for _ in range(2)]

        def blocks(ap, lo, hi):
            return ap.rearrange("p h (n t) -> p (h n) t", t=GC)[:, :, lo:hi]

        with nc.Block() as block:
            @block.sync
            def _(sp):
                sp.dma_start(wl[:], c["gla_w"]).then_inc(loaded, 16)
                sp.dma_start(bl[:], c["gla_b"]).then_inc(loaded, 16)
                for j in range(TN):
                    for b in range(2):
                        sp.wait_ge(tr_copied, 2 * j + b + 1)
                        sp.dma_start(tok_scr[j * P:(j + 1) * P, b, :], tk[b][:]).then_inc(stored[b], 16)
                for b in range(2):
                    sp.wait_ge(stored[b], 16 * TN)

            @block.tensor
            def _(pe):
                pe.wait_ge(loaded, 32)
                for i in range(4):
                    mm = nc.tensor.matmul(ps[:, i, :], wl[:, i * P:(i + 1) * P], lr, start=True, stop=True)
                mm.then_inc(x_ready, 1)
                pe.wait_ge(k_ready, 1)
                for j in range(TN):
                    for b, src in ((0, kd[:]), (1, z[:, 8:12, :])):
                        pe.wait_ge(tr_copied, max(2 * j + b - 1, 0))
                        for h in range(4):
                            mm = nc.tensor.transpose(ps_w[:, b, h * P:(h + 1) * P], src[:, h, j * P:(j + 1) * P], c["ident"][:])
                        mm.then_inc(tr_ready, 1)
                for d in range(GC):
                    n = GN * (GC - d)
                    pe.wait_ge(kq_ready, d + 1)
                    pe.wait_ge(av_ready, d)
                    for i in range(4):
                        mm = nc.tensor.matmul(ps[:, i, 0:n], c["ones"][:],
                                              ex[d % 2][:].rearrange("p h t -> p (h t)")[:, i * n:(i + 1) * n], start=True, stop=True)
                    mm.then_inc(sum_ready, 1)

            @block.scalar
            def _(act):
                act.wait_ge(lin_ready, 1)
                nc.scalar.activation(ax[:], lin[:], ACT.Abs).then_inc(ax_ready, 1)
                act.wait_ge(ax_ready, 1)
                nc.scalar.activation(ax[:], ax[:], ACT.Exp, scale=-1.0).then_inc(ax_ready, 1)
                act.wait_ge(ax_ready, 2)
                nc.scalar.activation(ax[:], ax[:], ACT.Ln, bias=1.0).then_inc(ln_ready, 1)
                act.wait_ge(cum_ready, 1)
                nc.scalar.activation(lin[:], cum[:], ACT.Exp).then_inc(eb_ready, 1)
                act.wait_ge(e_ready, 1)
                nc.scalar.activation(kd[:], kd[:], ACT.Exp)
                nc.scalar.activation(dec[:], blocks(cum[:], GC - 1, GC).rearrange("p (h n) t -> p h (n t)", h=4), ACT.Exp).then_inc(a_ready, 1)
                for j in range(TN):
                    for b in range(2):
                        act.wait_ge(tr_ready, 2 * j + b + 1)
                        act.wait_ge(stored[b], 16 * j)
                        nc.scalar.activation(tk[b][:], ps_w[:, b, :], ACT.Copy).then_inc(tr_copied, 1)
                for d in range(GC):
                    m = NB * (GC - d)
                    act.wait_ge(lag_ready, d + 1)
                    e = ex[d % 2][:].rearrange("p h t -> p (h t)")[:, 0:m]
                    nc.scalar.activation(e, e, ACT.Exp).then_inc(lag_exp, 1)

            @block.vector
            def _(dve):
                TT, TS, STT = nc.vector.tensor_tensor, nc.vector.tensor_scalar, nc.vector.scalar_tensor_tensor
                chain = Chain(dve, order)
                dve.wait_ge(x_ready, 1)
                for i in range(4):
                    r = TS(lin[:, i, :], ps[:, i, :], bl[:, i:i + 1], None, ALU.add)
                r.then_inc(lin_ready, 1)
                dve.wait_ge(lin_ready, 1)
                dve.wait_ge(ln_ready, 1)
                chain(STT(out=lin[:], in0=lin[:], scalar=0.0, in1=ax[:], op0=ALU.min, op1=ALU.subtract))
                chain(TS(lin[:], lin[:], 1.0 / 16, None, ALU.mult))
                for i in range(4):
                    r = nc.vector.tensor_tensor_scan(cum[:, i, :], c["chunk_start16"][:], lin[:, i, :], 0.0, ALU.mult, ALU.add)
                r.then_inc(cum_ready, 1)
                dve.wait_ge(cum_ready, 1)
                TT(blocks(kd[:], 0, GC), blocks(cum[:], GC - 1, GC).broadcast_to([P, NB, GC]), blocks(cum[:], 0, GC), ALU.subtract).then_inc(e_ready, 1)
                dve.wait_ge(a_ready, 1)
                TT(kd[:], kd[:], z[:, 4:8, :], ALU.mult).then_inc(k_ready, 1)
                chain(TS(z[:, 0:4, :], z[:, 0:4, :], K_SCALE, None, ALU.mult))
                for d in range(GC + 1):
                    if d < GC:
                        m = NB * (GC - d)
                        e = ex[d % 2][:].rearrange("p h t -> p (h t)")[:, 0:m].rearrange("p (n t) -> p n t", n=NB)
                        dve.wait_ge(sum_ready, max(d - 1, 0))
                        TT(e, blocks(cum[:], d, GC), blocks(cum[:], 0, GC - d), ALU.subtract).then_inc(lag_ready, 1)
                        dve.wait_ge(lag_exp, d + 1)
                        chain(TT(e, e, blocks(z[:, 4:8, :], 0, GC - d), ALU.mult))
                        TT(e, e, blocks(z[:, 0:4, :], d, GC), ALU.mult).then_inc(kq_ready, 1)
                    if d > 0:
                        l = d - 1
                        dve.wait_ge(sum_ready, l + 1)
                        n = GN * (GC - l)
                        for i in range(4):
                            pv = ps[:, i, 0:n].rearrange("p (n t) -> p n t", n=GN)
                            vv = z[:, 8 + i, :].rearrange("p (n t) -> p n t", t=GC)[:, :, 0:GC - l]
                            ov = o[:, i, :].rearrange("p (n t) -> p n t", t=GC)[:, :, l:GC]
                            if l == 0:
                                r = TT(ov, pv, vv, ALU.mult)
                            else:
                                av = ax[:, i, 0:n].rearrange("p (n t) -> p n t", n=GN)
                                r = TT(av, pv, vv, ALU.mult)
                        r.then_inc(av_ready, 1)
                        dve.wait_ge(av_ready, l + 1)
                        if l > 0:
                            for i in range(4):
                                av = ax[:, i, 0:n].rearrange("p (n t) -> p n t", n=GN)
                                ov = o[:, i, :].rearrange("p (n t) -> p n t", t=GC)[:, :, l:GC]
                                r = TT(ov, ov, av, ALU.add)
                            chain(r)
                dve.wait_ge(eb_ready, 1)
                TT(z[:, 0:4, :], z[:, 0:4, :], lin[:], ALU.mult).then_inc(p_ready, 1)


def gla_state(nc, c, z, o, dec, tok_scr):
    RING = 4
    with stage(nc) as s:
        tk = [s.sb("tk", [GC, 2, 512]) for _ in range(RING)]
        st = [s.sb("st", [P, 4, P]) for _ in range(2)]
        ps_o = [s.ps("ps_o", [P, BANK]) for _ in range(2)]
        ps_s = [s.ps("ps_s", [P, BANK]) for _ in range(2)]
        tk_in = [s.sem("tk_in") for _ in range(RING)]
        kv_ready, o_ready, st_ready, added = (s.sem(n) for n in ("kv_ready", "o_ready", "st_ready", "added"))
        with nc.Block() as block:
            @block.sync
            def _(sp):
                with sp.Fori(0, GN // RING) as it:
                    for b in range(RING):
                        sp.wait_ge(kv_ready, it * RING)
                        sp.dma_start(tk[b][:], tok_scr[bass.ds((it * RING + b) * GC, GC)]).then_inc(tk_in[b], 16)

            @block.tensor
            def _(pe):
                with pe.Fori(0, GN // RING) as it:
                    for b in range(RING):
                        n = it * RING + b
                        pe.wait_ge(tk_in[b], it * 16 + 16)
                        pe.wait_ge(st_ready, n)
                        for h in range(4):
                            mm = nc.tensor.matmul(ps_s[b % 2][:, h * P:(h + 1) * P], tk[b][:, 0, h * P:(h + 1) * P],
                                                  tk[b][:, 1, h * P:(h + 1) * P], start=True, stop=True)
                        mm.then_inc(kv_ready, 1)
                        pe.wait_ge(st_ready, n + 1)
                        pe.wait_ge(added, n)
                        for h in range(4):
                            mm = nc.tensor.matmul(ps_o[b % 2][:, h * GC:(h + 1) * GC], st[b % 2][:, h, :],
                                                  z[:, h, bass.ds(n * GC, GC)], start=True, stop=True)
                        mm.then_inc(o_ready, 1)

            @block.vector
            def _(dve):
                nc.vector.memset(st[0][:], 0.0).then_inc(st_ready, 1)
                dve.wait_ge(st_ready, 1)
                with dve.Fori(0, GN // RING) as it:
                    for b in range(RING):
                        n = it * RING + b
                        dve.wait_ge(kv_ready, n + 1)
                        dve.wait_ge(o_ready, n)
                        dve.wait_ge(st_ready, n + 1)
                        for h in range(4):
                            r = nc.vector.scalar_tensor_tensor(out=st[(b + 1) % 2][:, h, :], in0=st[b % 2][:, h, :],
                                                               scalar=dec[:, h, bass.ds(n, 1)], in1=ps_s[b % 2][:, h * P:(h + 1) * P],
                                                               op0=ALU.mult, op1=ALU.add)
                        r.then_inc(st_ready, 1)
                        dve.wait_ge(o_ready, n + 1)
                        ov = o[:, :, bass.ds(n * GC, GC)]
                        nc.vector.tensor_tensor(ov, ps_o[b % 2][:, 0:4 * GC].rearrange("p (h t) -> p h t", h=4), ov, ALU.add).then_inc(added, 1)


def gdn_conv(nc, c, z):
    with stage(nc) as s:
        taps = s.sb("taps", [P, 12, 4])
        cv = [s.sb("cv", [P, T2]) for _ in range(2)]
        loaded, conv_ready, done = s.sem("loaded"), s.sem("conv_ready"), s.sem("done")
        order = [s.sem("order") for _ in range(2)]
        with nc.Block() as block:
            @block.sync
            def _(sp):
                sp.dma_start(taps[:], c["gdn_taps"]).then_inc(loaded, 16)

            @block.vector
            def _(dve):
                dve.wait_ge(loaded, 16)
                with dve.Fori(0, 6) as it:
                    for b in range(2):
                        i = it * 2 + b
                        dve.wait_ge(done, it * 2)
                        nc.vector.tensor_scalar(cv[b][:], z[:, i, 3:3 + T2], taps[:, i, 3:4], None, ALU.mult).then_inc(order[b], 1)
                    for j in range(3):
                        for b in range(2):
                            i = it * 2 + b
                            dve.wait_ge(order[b], it * 3 + j + 1)
                            r = nc.vector.scalar_tensor_tensor(out=cv[b][:], in0=z[:, i, j:j + T2], scalar=taps[:, i, j:j + 1], in1=cv[b][:],
                                                               op0=ALU.mult, op1=ALU.add)
                            r.then_inc(order[b] if j < 2 else conv_ready, 1)

            @block.scalar
            def _(act):
                with act.Fori(0, 6) as it:
                    for b in range(2):
                        act.wait_ge(conv_ready, it * 2 + b + 1)
                        nc.scalar.activation(z[:, it * 2 + b, 3:3 + T2], cv[b][:], ACT.Silu).then_inc(done, 1)


def gdn_matrices(nc, c, z, rows, yall, qk):
    L = LEVELS3
    E = range(2)
    with stage(nc) as s:
        bcol = s.sb("bcol", [DC, DN, 4])
        sel = [s.sb("sel", [4, P]) for _ in E]
        ks, qs = [s.sb("ks", [P, T2]) for _ in E], [s.sb("qs", [P, T2]) for _ in E]
        dec, nn, t1, xi, yi = ([s.sb(n, [DC, T2]) for _ in E] for n in ("dec", "nn", "t1", "xi", "yi"))
        nm = [s.sb("nm", [DC, L, T2]) for _ in E]
        psA, psB, psC = ([s.ps(n, [P, BANK]) for _ in E] for n in ("psA", "psB", "psC"))
        col_ready, col_copied = s.sem("col_ready"), s.sem("col_copied")
        names = ("fixed", "bc_ready", "arg_ready", "bd_read", "dec_ready", "prod_ready", "n_ready", "qk_done", "level_done",
                 "t1_ready", "t1_copied", "xy_ready", "xy_done", "order")
        (fixed, bc_ready, arg_ready, bd_read, dec_ready, prod_ready, n_ready, qk_done, level_done, t1_ready, t1_copied,
         xy_ready, xy_done, order) = ([s.sem(n) for _ in E] for n in names)

        def cols(n):
            return slice(n * DC, (n + 1) * DC)

        def chunked(ap):
            return ap.rearrange("p (n t) -> p n t", t=DC)

        with nc.Block() as block:
            @block.gpsimd
            def _(pool):
                with pool.Fori(0, 2) as it:
                    for e in E:
                        h = it * 2 + e
                        pool.wait_ge(prod_ready[e], it)
                        nc.gpsimd.tensor_copy(ks[e][:], z[:, h + 4, 3:3 + T2])
                        nc.gpsimd.tensor_copy(qs[e][:], z[:, h, 3:3 + T2])
                        nc.gpsimd.tensor_copy(sel[e][:], c["head_sel"][:, h, :]).then_inc(fixed[e], 1)
                    for l in range(L):
                        for e in E:
                            pool.wait_ge(n_ready[e], it + 1)
                            nc.gpsimd.tensor_tensor(nm[e][:, l, :], nn[e][:], c["level64"][:, l, :], ALU.mult).then_inc(level_done[e], 1)

            @block.tensor
            def _(pe):
                for n in range(DN):
                    mm = nc.tensor.transpose(psC[0][0:DC, 4 * n:4 * n + 4], rows[:, 3, cols(n)], c["ident"][0:4, 0:4])
                mm.then_inc(col_ready, 1)
                pe.wait_ge(col_copied, 1)
                with pe.Fori(0, 2) as it:
                    for e in E:
                        pe.wait_ge(fixed[e], it + 1)
                        pe.wait_ge(n_ready[e], it)
                        nc.tensor.matmul(psC[e][:], sel[e][:], rows[:, 3, :], start=True, stop=True).then_inc(bc_ready[e], 1)
                    for e in E:
                        pe.wait_ge(xy_done[e], it * L)
                        for n in range(DN):
                            nc.tensor.matmul(psA[e][0:DC, cols(n)], ks[e][:, cols(n)], ks[e][:, cols(n)], start=True, stop=True)
                            nc.tensor.matmul(psB[e][0:DC, cols(n)], ks[e][:, cols(n)], qs[e][:, cols(n)], start=True, stop=True)
                        pe.wait_ge(bd_read[e], it + 1)
                        nc.tensor.matmul(psC[e][:], sel[e][:], rows[:, 5, :], start=True, stop=True).then_inc(prod_ready[e], 1)
                    for l in range(L):
                        for e in E:
                            count = pe.compute_val(it * L + l + 1)
                            count_2 = pe.compute_val(it + 1)
                            count_3 = pe.compute_val(it * L + l)
                            settle(pe, col_copied)
                            pe.wait_ge(level_done[e], count)
                            pe.wait_ge(qk_done[e], count_2)
                            pe.wait_ge(xy_done[e], count_3)
                            for n in range(DN):
                                rhs = c["ident"][0:DC, 0:DC] if l == 0 else xi[e][:, cols(n)]
                                mm = nc.tensor.matmul(psA[e][0:DC, cols(n)], nm[e][:, l, cols(n)], rhs, start=True, stop=True)
                            mm.then_inc(t1_ready[e], 1)
                        if l == 0:
                            continue
                        for e in E:
                            count = pe.compute_val(it * (L - 1) + l)
                            settle(pe, col_copied)
                            pe.wait_ge(t1_copied[e], count)
                            for n in range(DN):
                                if l < L - 1:
                                    nc.tensor.matmul(psA[e][0:DC, cols(n)], yi[e][:, cols(n)], t1[e][:, cols(n)], start=True, stop=True)
                                mm = nc.tensor.matmul(psB[e][0:DC, cols(n)], t1[e][:, cols(n)], yi[e][:, cols(n)], start=True, stop=True)
                            mm.then_inc(xy_ready[e], 1)

            @block.scalar
            def _(act):
                act.wait_ge(col_ready, 1)
                nc.scalar.activation(bcol[:].rearrange("p n h -> p (n h)"), psC[0][0:DC, 0:4 * DN], ACT.Copy).then_inc(col_copied, 1)
                with act.Fori(0, 2) as it:
                    for e in E:
                        act.wait_ge(arg_ready[e], it + 1)
                        nc.scalar.activation(dec[e][:], dec[e][:], ACT.Exp).then_inc(dec_ready[e], 1)
                    for l in range(1, L):
                        for e in E:
                            act.wait_ge(t1_ready[e], it * L + l + 1)
                            nc.scalar.activation(t1[e][:], psA[e][0:DC, :], ACT.Copy).then_inc(t1_copied[e], 1)

            @block.vector
            def _(dve):
                TT = nc.vector.tensor_tensor
                dve.wait_ge(col_copied, 1)
                with dve.Fori(0, 2) as it:
                    chain = [Chain(dve, order[e], it, 2) for e in E]
                    for e in E:
                        h = it * 2 + e
                        dve.wait_ge(bc_ready[e], it + 1)
                        dve.wait_ge(qk_done[e], it)
                        TT(chunked(dec[e][:]), chunked(psC[e][0:DC, :]), bcol[:, :, bass.ds(h, 1)].broadcast_to([DC, DN, DC]),
                           ALU.subtract).then_inc(bd_read[e], 1)
                    for e in E:
                        dve.wait_ge(bd_read[e], it + 1)
                        TT(dec[e][:], dec[e][:], c["mask64"][:], ALU.add).then_inc(arg_ready[e], 1)
                    for e in E:
                        dve.wait_ge(dec_ready[e], it + 1)
                        dve.wait_ge(level_done[e], it * L)
                        chain[e](TT(nn[e][:], dec[e][:], c["neg_strict64"][:], ALU.mult))
                        dve.wait_ge(prod_ready[e], it + 1)
                        chain[e](TT(nn[e][:], psC[e][0:DC, :], nn[e][:], ALU.mult))
                        TT(nn[e][:], psA[e][0:DC, :], nn[e][:], ALU.mult).then_inc(n_ready[e], 1)
                        TT(qk[:, it * 2 + e, :], psB[e][0:DC, :], dec[e][:], ALU.mult).then_inc(qk_done[e], 1)
                    for l in range(L):
                        for e in E:
                            if l == 0:
                                dve.wait_ge(t1_ready[e], it * L + 1)
                                TT(xi[e][:], psA[e][0:DC, :], c["ident64"][:], ALU.add)
                                TT(yi[e][:], nm[e][:, 0, :], c["ident64"][:], ALU.add).then_inc(xy_done[e], 1)
                                continue
                            dve.wait_ge(xy_ready[e], it * (L - 1) + l)
                            if l < L - 1:
                                TT(xi[e][:], psA[e][0:DC, :], xi[e][:], ALU.add)
                                TT(yi[e][:], psB[e][0:DC, :], yi[e][:], ALU.add).then_inc(xy_done[e], 1)
                            else:
                                TT(yall[:, it * 2 + e, :], psB[e][0:DC, :], yi[e][:], ALU.add).then_inc(xy_done[e], 1)
                    for e in E:
                        chain[e].close()


def gdn_factors(nc, c, z, rows, kh, bv, dec):
    with stage(nc) as s:
        sel = s.sb("sel", [4, P])
        khf, bvf = s.sb("khf", [P, T2]), s.sb("bvf", [P, T2])
        ps_b = [s.ps("ps_b", [P, BANK]) for _ in range(4)]
        ps_t = [s.ps("ps_t", [P, 2, BANK]) for _ in range(2)]
        fixed, bc_ready, kh_ready, bv_ready, tr_ready, copied, done, order = (
            s.sem(n) for n in ("fixed", "bc_ready", "kh_ready", "bv_ready", "tr_ready", "copied", "done", "order"))
        with nc.Block() as block:
            @block.gpsimd
            def _(pool):
                with pool.Fori(0, 4) as h:
                    pool.wait_ge(bc_ready, h)
                    nc.gpsimd.tensor_copy(sel[:], c["head_sel"][:, h, :]).then_inc(fixed, 1)

            @block.tensor
            def _(pe):
                with pe.Fori(0, 4) as h:
                    pe.wait_ge(fixed, h + 1)
                    pe.wait_ge(done, h)
                    for b, r in enumerate((7, 5, 6, 4)):
                        mm = nc.tensor.matmul(ps_b[b][:], sel[:], rows[:, r, :], start=True, stop=True)
                    mm.then_inc(bc_ready, 1)
                    for b, (src, ready) in enumerate(((khf, kh_ready), (bvf, bv_ready))):
                        count = pe.compute_val(h + 1)
                        count_2 = pe.compute_val(h * 2)
                        settle(pe, bc_ready)
                        pe.wait_ge(ready, count)
                        pe.wait_ge(copied, count_2)
                        for n in range(DN):
                            mm = nc.tensor.transpose(ps_t[b][0:DC, n // 4, (n % 4) * P:(n % 4 + 1) * P], src[:, n * DC:(n + 1) * DC], c["ident"][:])
                        mm.then_inc(tr_ready, 1)

            @block.scalar
            def _(act):
                with act.Fori(0, 4) as h:
                    for b, dst in enumerate((kh, bv)):
                        act.wait_ge(tr_ready, h * 2 + b + 1)
                        nc.scalar.activation(dst[:, h, :].rearrange("p (a t) -> p a t", a=2), ps_t[b][0:DC, :, :], ACT.Copy).then_inc(copied, 1)

            @block.vector
            def _(dve):
                TT = nc.vector.tensor_tensor
                with dve.Fori(0, 4) as h:
                    dve.wait_ge(bc_ready, h + 1)
                    dve.wait_ge(tr_ready, h * 2)
                    kz, qz, vz = z[:, h + 4, 3:3 + T2], z[:, h, 3:3 + T2], z[:, h + 8, 3:3 + T2]
                    TT(khf[:], ps_b[0][:], kz, ALU.mult).then_inc(kh_ready, 1)
                    TT(bvf[:], ps_b[1][:], vz, ALU.mult).then_inc(bv_ready, 1)
                    dve.wait_ge(kh_ready, h + 1)
                    TT(kz, ps_b[2][:], kz, ALU.mult)
                    TT(qz, ps_b[3][:], qz, ALU.mult)
                    nc.vector.tensor_copy(dec[:, h, :], ps_b[3][:].rearrange("p (n t) -> p n t", t=DC)[:, :, DC - 1]).then_inc(done, 1)


def gdn_chunks(nc, c, z, yall, qk, kh, bv, dec, o):
    with stage(nc) as s:
        st = s.sb("st", [P, 4, P])
        kb = [s.sb("kb", [P, 4, DC]) for _ in range(2)]
        kt = [s.sb("kt", [DC, 4, P]) for _ in range(2)]
        yt = [s.sb("yt", [DC, 4, DC]) for _ in range(2)]
        rr, vn = s.sb("rr", [DC, 512]), s.sb("vn", [DC, 512])
        ps_r, ps_v, ps_s = (s.ps(n, [P, BANK]) for n in ("ps_r", "ps_v", "ps_s"))
        ps_o = s.ps("ps_o", [P, BANK])
        fixed, r_prod, r_ready, v_prod, v_ready, o_ready, s_prod, o_done, st_ready = (
            s.sem(n) for n in ("fixed", "r_prod", "r_ready", "v_prod", "v_ready", "o_ready", "s_prod", "o_done", "st_ready"))
        with nc.Block() as block:
            @block.gpsimd
            def _(pool):
                with pool.Fori(0, DN // 2) as it:
                    for b in range(2):
                        n = it * 2 + b
                        pool.wait_ge(s_prod, it * 2)
                        nc.gpsimd.tensor_copy(kb[b][:], z[:, 4:8, bass.ds(n * DC + 3, DC)])
                        nc.gpsimd.tensor_copy(kt[b][:], kh[:, :, bass.ds(n * P, P)])
                        nc.gpsimd.tensor_copy(yt[b][:], yall[:, :, bass.ds(n * DC, DC)]).then_inc(fixed, 1)

            @block.tensor
            def _(pe):
                with pe.Fori(0, DN // 2) as it:
                    for b in range(2):
                        n = it * 2 + b
                        pe.wait_ge(fixed, n + 1)
                        pe.wait_ge(st_ready, n + 1)
                        for h in range(4):
                            mm = nc.tensor.matmul(ps_r[0:DC, h * P:(h + 1) * P], kb[b][:, h, :], st[:, h, :], start=True, stop=True)
                        mm.then_inc(r_prod, 1)
                        count = pe.compute_val(n + 1)
                        settle(pe, fixed)
                        pe.wait_ge(r_ready, count)
                        for h in range(4):
                            mm = nc.tensor.matmul(ps_v[0:DC, h * P:(h + 1) * P], yt[b][:, h, :], rr[:, h * P:(h + 1) * P], start=True, stop=True)
                        mm.then_inc(v_prod, 1)
                        pe.wait_ge(v_ready, n + 1)
                        pe.wait_ge(o_done, n)
                        for h in range(4):
                            out = ps_o[:, h * DC:(h + 1) * DC]
                            nc.tensor.matmul(out, st[:, h, :], z[:, h, bass.ds(n * DC + 3, DC)], start=True, stop=False)
                            mm = nc.tensor.matmul(out, vn[:, h * P:(h + 1) * P], qk[:, h, bass.ds(n * DC, DC)], start=False, stop=True)
                        mm.then_inc(o_ready, 1)
                        for h in range(4):
                            mm = nc.tensor.matmul(ps_s[:, h * P:(h + 1) * P], kt[b][:, h, :], vn[:, h * P:(h + 1) * P], start=True, stop=True)
                        mm.then_inc(s_prod, 1)

            @block.scalar
            def _(act):
                with act.Fori(0, DN) as n:
                    act.wait_ge(v_prod, n + 1)
                    nc.scalar.activation(vn[:], ps_v[0:DC, :], ACT.Copy).then_inc(v_ready, 1)
                    act.wait_ge(o_ready, n + 1)
                    nc.scalar.activation(o[:, :, bass.ds(n * DC, DC)], ps_o[:, 0:4 * DC].rearrange("p (h t) -> p h t", h=4), ACT.Copy).then_inc(o_done, 1)

            @block.vector
            def _(dve):
                nc.vector.memset(st[:], 0.0).then_inc(st_ready, 1)
                with dve.Fori(0, DN) as n:
                    dve.wait_ge(r_prod, n + 1)
                    nc.vector.tensor_tensor(rr[:].rearrange("p (h v) -> p h v", h=4), ps_r[0:DC, :].rearrange("p (h v) -> p h v", h=4),
                                            bv[:, :, bass.ds(n * P, P)], ALU.add).then_inc(r_ready, 1)
                    dve.wait_ge(s_prod, n + 1)
                    dve.wait_ge(st_ready, n + 1)
                    for h in range(4):
                        r = nc.vector.scalar_tensor_tensor(out=st[:, h, :], in0=st[:, h, :], scalar=dec[:, h, bass.ds(n, 1)],
                                                           in1=ps_s[:, h * P:(h + 1) * P], op0=ALU.mult, op1=ALU.add)
                    r.then_inc(st_ready, 1)


def silu_tiles(nc, x):
    with stage(nc):
        with nc.Block() as block:
            @block.scalar
            def _(act):
                with act.Fori(0, x.shape[1]) as i:
                    nc.scalar.activation(x[:, i, :], x[:, i, :], ACT.Silu)


def zero(nc, x):
    with stage(nc):
        with nc.Block() as block:
            @block.vector
            def _(dve):
                nc.vector.memset(x, 0.0)


def copy_tile(nc, dst, src):
    with stage(nc):
        with nc.Block() as block:
            @block.vector
            def _(dve):
                nc.vector.tensor_copy(dst, src)



def resident(nc, memory, name, shape):
    return memory.enter_context(nc.sbuf_tensor(f"{name}_{nc.next_id()}", shape, F32))


def with_constants(nc, memory, a, names):
    c = dict(a)
    for name in names:
        c[name] = resident(nc, memory, name, a[name].shape)
    load(nc, [(c[name][:], a[name]) for name in names])
    return c


def first_block(nc, a, x, ones_ident, x_out):
    chunks = nc.dram_tensor("rwkv_chunks", (RN, P, 8, 5, RC), F32).ap()
    bonus = nc.dram_tensor("rwkv_bonus", (P, 8, T1), F32).ap()
    gate = nc.dram_tensor("rwkv_gate", (P, 8, T1), F32).ap()

    def act(memory, name, k, t=T1):
        return resident(nc, memory, name, [P, k, t])
    with ExitStack() as m:
        c = with_constants(nc, m, {**a, **ones_ident}, CONSTANTS[1])
        h, y = act(m, "h", 8), act(m, "y", 8)
        rmsnorm(nc, c["ones"], x, a["norm_mix_1"], h, T1, 1e-5, src=a["x_1"])
        with ExitStack() as m2:
            decay = resident(nc, m2, "chunk_decay", [P, 8, RN])
            with ExitStack() as m3:
                p = act(m3, "p", 27, T1 + 1)
                zero(nc, p[:, :, 0:1])
                dense(nc, a["w_rwkv_1"], h, p[:, :, 1:T1 + 1], T1, func=ACT.Copy, n_body=3)
                rwkv_lora_inputs(nc, c, p)
                rwkv_prepare(nc, c, p, chunks, decay, bonus, gate)
            rwkv_chunks(nc, c, y, chunks, decay)
        rwkv_finish(nc, c, y, bonus, gate)
        o = act(m, "o", 8)
        with ExitStack() as m2:
            p = act(m2, "p", 24)
            dense(nc, a["w_qkv_1"], h, p, T1, func=ACT.Copy, n_body=4)
            diff_attention(nc, c, p, o)
        head_rms(nc, c["ones"], o, a["subln_1"], T1, 1e-5, factor=1 - LAMBDA_INIT)
        with ExitStack() as m2:
            o_rwkv, o_diff, gates = act(m2, "o_rwkv", 8), act(m2, "o_diff", 8), act(m2, "gates", 16)
            dense(nc, a["rwkv_out_1"], y, o_rwkv, T1, func=ACT.Copy, n_body=4)
            dense(nc, a["diff_out_1"], o, o_diff, T1, func=ACT.Copy, n_body=4)
            dense(nc, a["w_gates_1"], h, gates, T1, func=ACT.Sigmoid, n_body=4)
            gated_sum(nc, o_rwkv, o_diff, gates, y, T1)
        dense(nc, a["w_out_1"], y, x, T1, residual=x, n_body=4)
    with ExitStack() as m:
        h, hidden = act(m, "h", 8), act(m, "hidden", 32)
        rmsnorm(nc, ones_ident["ones"], x, a["norm_mlp_1"], h, T1, 1e-5)
        dense(nc, a["mlp_in_1"], h, hidden, T1, func="relu2", n_body=4)
        dense(nc, a["mlp_out_1"], hidden, x, T1, residual=x, n_body=2)
        rmsnorm(nc, ones_ident["ones"], x, a["norm_final_1"], x_out, T1, 1e-5)


def second_block(nc, a, x, ones_ident):
    bias_scr = nc.dram_tensor("bias_by_distance", (8, 640), F32).ap()
    bias_rows = nc.dram_tensor("bias_rows", (8, P, T2), F32).ap()

    def act(memory, name, k, t=T2):
        return resident(nc, memory, name, [P, k, t])
    with ExitStack() as m:
        c = with_constants(nc, m, {**a, **ones_ident}, CONSTANTS[2])
        h, conv, o = act(m, "h", 8), act(m, "conv", 4), act(m, "o", 4)
        rmsnorm(nc, c["ones"], x, a["norm_mix_2"], h, T2, 1e-6)
        with ExitStack() as m2:
            z = act(m2, "z", 19)
            bias_cmp = resident(nc, m2, "bias_cmp", [P, 55, 8])
            k_cmp, v_cmp = resident(nc, m2, "k_cmp", [P, NC2]), resident(nc, m2, "v_cmp", [NC2, P])
            dense(nc, a["w_in_2"], h, z, T2, func=ACT.Copy, n_body=1)
            conv_branch(nc, c, z[:, 0:8, :], conv)
            bias_tables(nc, c, bias_scr, bias_rows, bias_cmp)
            compress(nc, c, z[:, 12:18, :], k_cmp, v_cmp)
            nsa_attention(nc, c, z[:, 8:12, :], z[:, 12:18, :], z[:, 18, :], bias_rows, bias_cmp, k_cmp, v_cmp, o)
        y_conv, y_attn, gates = act(m, "y_conv", 8), act(m, "y_attn", 8), act(m, "gates", 16)
        dense(nc, a["conv_out_2"], conv, y_conv, T2, func=ACT.Copy, n_body=4)
        dense(nc, a["attn_out_2"], o, y_attn, T2, func=ACT.Copy, n_body=4)
        dense(nc, a["w_gates_2"], h, gates, T2, func=ACT.Sigmoid, n_body=4)
        gated_sum(nc, y_conv, y_attn, gates, h, T2)
        dense(nc, a["w_out_2"], h, x, T2, residual=x, n_body=4)
    with ExitStack() as m:
        h, u = act(m, "h", 8), act(m, "u", 22)
        rmsnorm(nc, ones_ident["ones"], x, a["norm_ffn_2"], h, T2, 1e-6)
        ffn_up(nc, a, a["ffn_up_2"], h, u)
        dense(nc, a["ffn_down_2"], u, x, T2, residual=x, n_body=4)
    with ExitStack() as m:
        h, gate, emb, p = act(m, "h", 8), act(m, "gate", 8), act(m, "emb", 8), act(m, "p", 2)
        load(nc, [(p[:], a["p_2"])])
        rmsnorm(nc, ones_ident["ones"], x, a["norm_ple_2"], h, T2, 1e-6)
        dense(nc, a["ple_gate_2"], h, gate, T2, func=ACT.Sigmoid, n_body=4)
        dense(nc, a["ple_2"], p, emb, T2, func=ACT.Copy, n_body=4)
        add_product(nc, x, gate, emb)
        rmsnorm(nc, ones_ident["ones"], x, a["norm_final_2"], x, T2, 1e-6)


def third_block(nc, a, x, ones_ident, out):
    gla_tok = nc.dram_tensor("gla_by_token", (T2, 2, 512), F32).ap()

    def act(memory, name, k, t=T2):
        return resident(nc, memory, name, [P, k, t])
    with ExitStack() as m:
        c = with_constants(nc, m, {**a, **ones_ident}, CONSTANTS[3])
        h, low_rank = act(m, "h", 8), act(m, "low_rank", 1)
        rows = resident(nc, m, "rows", [4, 8, T2])
        o_m, o_l, o_d = act(m, "o_m", 4), act(m, "o_l", 4), act(m, "o_d", 4)
        rmsnorm(nc, c["ones"], x, a["norm_mix_3"], h, T2, 1e-6)
        with ExitStack() as m2:
            z = act(m2, "z", 18)
            dense(nc, a["w_mlstm_3"], h, z, T2, func=ACT.Copy, n_body=3)
            copy_tile(nc, low_rank[:, 0, :], z[:, 17, :])
            gate_rows(nc, c, z[:, 16, :], rows)
            mlstm(nc, c, z, rows, o_m)
        head_rms(nc, c["ones"], o_m, a["norm_mlstm_3"], T2, 1e-6)
        with ExitStack() as m2:
            z, decay = act(m2, "z", 16), resident(nc, m2, "decay", [P, 4, GN])
            dense(nc, a["w_gla_in_3"], h, z, T2, func=ACT.Copy, n_body=4)
            gla_intra(nc, c, z[:], low_rank[0:16, 0, :], o_l, decay, gla_tok)
            gla_state(nc, c, z, o_l, decay, gla_tok)
            silu_tiles(nc, z[:, 12:16, :])
            head_rms(nc, c["ones"], o_l, a["norm_gla_3"], T2, 1e-6, gate=z[:, 12:16, :])
        with ExitStack() as m2:
            z, decay = act(m2, "z", 16, T2 + 3), resident(nc, m2, "decay", [P, 4, DN])
            inverse, qk = resident(nc, m2, "inverse", [DC, 4, T2]), resident(nc, m2, "qk", [DC, 4, T2])
            zero(nc, z[:, :, 0:3])
            dense(nc, a["w_gdn_3"], h, z[:, :, 3:T2 + 3], T2, func=ACT.Copy, n_body=4)
            gdn_conv(nc, c, z)
            head_rms(nc, c["ones"], z[:, 0:8, 3:T2 + 3], a["l2_weight"], T2, 1e-6, mean=1.0)
            gdn_matrices(nc, c, z, rows, inverse, qk)
            kh, bv = resident(nc, m2, "kh", [DC, 4, DN * P]), resident(nc, m2, "bv", [DC, 4, DN * P])
            gdn_factors(nc, c, z, rows, kh, bv, decay)
            gdn_chunks(nc, c, z, inverse, qk, kh, bv, decay, o_d)
            silu_tiles(nc, z[:, 12:16, 3:T2 + 3])
            head_rms(nc, c["ones"], o_d, a["norm_gdn_3"], T2, 1e-6, gate=z[:, 12:16, 3:T2 + 3])
        up_a, up_b = act(m, "up_a", 8), act(m, "up_b", 8)
        with ExitStack() as m2:
            gates = act(m2, "gates", 24)
            dense(nc, a["w_gates_3"], h, gates, T2, func=ACT.Sigmoid, n_body=4)
            dense(nc, a["up_3"][0], o_m, up_a, T2, func=ACT.Copy, n_body=4)
            dense(nc, a["up_3"][1], o_l, up_b, T2, func=ACT.Copy, n_body=4)
            gated_sum(nc, up_a, up_b, gates, h, T2)
            dense(nc, a["up_3"][2], o_d, up_a, T2, func=ACT.Copy, n_body=4)
            add_product(nc, h, up_a, gates[:, 16:24, :])
        dense(nc, a["w_out_3"], h, x, T2, residual=x, n_body=4)
    with ExitStack() as m:
        h, hidden = act(m, "h", 8), act(m, "hidden", 32)
        rmsnorm(nc, ones_ident["ones"], x, a["norm_mlp_3"], h, T2, 1e-6)
        dense(nc, a["mlp_in_3"], h, hidden, T2, func="relu2", n_body=4)
        dense(nc, a["mlp_out_3"], hidden, x, T2, residual=x, n_body=2)
        rmsnorm(nc, ones_ident["ones"], x, a["norm_final_3"], h, T2, 1e-6, dst=out)


def program(nc, a, out):
    with ExitStack() as memory:
        common = {n: resident(nc, memory, n, a[n].shape) for n in CONSTANTS[0]}
        load(nc, [(common[n][:], a[n]) for n in CONSTANTS[0]])
        x2 = resident(nc, memory, "x2", [P, 8, T2])
        with ExitStack() as m:
            x, x_out = resident(nc, m, "x", [P, 8, T1]), resident(nc, m, "x_out", [P, 8, T1])
            first_block(nc, a, x, common, x_out)
            copy_tile(nc, x2[:], x_out[:, :, T1 - T2:T1])
        second_block(nc, a, x2, common)
        third_block(nc, a, x2, common, out)



CONSTANTS = {
    0: ["ones", "ident"],
    1: ["blk64", "mean64", "chunk_start66", "causal66", "level66", "ident66", "mask88", "rope_cos", "rope_sin", "rope_swap"],
    2: ["row_valid", "upside_down"],
    3: ["mask_st", "head_sel", "chunk_start64", "chunk_start16", "mask64", "neg_strict64", "ident64", "level64"],
}


def bucket_one_hot(distance):
    n = np.maximum(distance, 0)
    large = 16 + (np.log(np.maximum(n, 16).astype(np.float32) / np.float32(16)) / np.float32(math.log(8))
                  * np.float32(16)).astype(np.int32)
    bucket = np.where(distance < 0, 32, np.where(n < 16, n, np.minimum(large, 31)))
    return (np.arange(33)[:, None] == bucket[None, :]).astype(np.float32)


def level_masks(size, levels):
    s_, t_ = np.mgrid[0:size, 0:size]
    out = np.zeros((size, levels, size), np.float32)
    for l in range(levels):
        w = 1 << l
        out[:, l] = (s_ // (2 * w) == t_ // (2 * w)) & ((s_ // w) % 2 == 0) & ((t_ // w) % 2 == 1)
    return out


def constants():
    f = np.float32
    eye = np.eye(P, dtype=f)
    heads2 = np.kron(np.eye(2), np.ones((64, 64))).astype(f)
    out = {"ones": np.ones((P, P), f), "ident": eye, "blk64": heads2, "mean64": heads2 / f(64)}
    for name, t, n in (("chunk_start66", T1, RC), ("chunk_start64", T2, DC), ("chunk_start16", T2, GC)):
        out[name] = np.ones((P, t), f)
        out[name][:, ::n] = 0
    s_, t_ = np.mgrid[0:RC, 0:RC]
    out["causal66"] = np.tile(np.concatenate([s_ < t_, s_ <= t_], 1).astype(f), (1, 2))
    out["level66"] = np.repeat(level_masks(RC, LEVELS1)[:, :, None, :], 4, 2)
    out["ident66"] = np.tile(np.eye(RC, dtype=f)[:, None, :], (1, 4, 1))
    off = T1 - QT
    out["mask88"] = np.where(np.arange(T1 + off)[None, :] - off <= np.arange(QT)[:, None], 0, NEG).astype(f)
    inv = (500000.0 ** (-np.arange(0, 16, 2, dtype=f) / f(16))).astype(f)
    angle = (np.arange(T1, dtype=f)[:, None] * inv[None, :]).T
    cos, sin, swap = np.ones((P, T1), f), np.zeros((P, T1), f), np.zeros((P, P), f)
    for b in (0, 64):
        for half in (0, 8):
            cos[b + half:b + half + 8], sin[b + half:b + half + 8] = np.cos(angle), np.sin(angle)
        for j in range(8):
            swap[b + 8 + j, b + j], swap[b + j, b + 8 + j] = -1, 1
    out["rope_cos"], out["rope_sin"], out["rope_swap"] = cos, sin, swap
    out["buckets_rev"] = bucket_one_hot(511 - np.arange(640))
    out["buckets_fwd"] = bucket_one_hot(np.arange(1024) - 511)
    out["upside_down"] = eye[::-1]
    out["row_valid"] = (np.arange(P)[:, None] >= 31).astype(f)
    s_, t_ = np.mgrid[0:P, 0:T2]
    out["mask_st"] = np.where(s_ <= t_, 0, NEG).astype(f)
    out["head_sel"] = np.repeat(np.eye(4, dtype=f)[:, :, None], P, 2)
    s_, t_ = np.mgrid[0:DC, 0:DC]
    out["mask64"] = np.tile(np.where(s_ <= t_, 0, NEG).astype(f), (1, DN))
    out["neg_strict64"] = np.tile(-(s_ < t_).astype(f), (1, DN))
    out["ident64"] = np.tile(np.eye(DC, dtype=f), (1, DN))
    out["level64"] = np.tile(level_masks(DC, LEVELS3), (1, 1, DN))
    out["l2_weight"] = np.repeat(np.array([[K_SCALE] * 4 + [1.0] * 4], f), P, 0)
    return out


def tiles(w, kp=8):
    k, n = w.shape
    return w.reshape(k // (P * kp), kp, P, n // P, P).transpose(3, 0, 2, 1, 4)


def by_feature(x):
    return x.T.reshape(-1, P, x.shape[0]).transpose(1, 0, 2)


def column(v):
    return v.reshape(-1, P).T


def blank(rows, cols):
    return np.zeros((rows, cols), np.float32)


def arguments(i):
    cat = np.concatenate
    a = constants()
    w, mu = i["w_in"][0], i["rwkv_mu"][0]
    a["x_1"] = by_feature(cat([i["meta_tokens"], i["x"][0]], 0))
    a["norm_mix_1"], a["norm_mlp_1"], a["norm_final_1"] = column(i["norm_mix_w"][0]), column(i["norm_mlp_w"][0]), column(i["final_norm_w"])
    a["w_rwkv_1"] = tiles(cat([w[:, :3360], blank(1024, 96)], 1))
    a["w_qkv_1"], a["w_gates_1"] = tiles(w[:, 3360:6432]), tiles(w[:, 6432:])
    a["lora_mu"] = column(cat([mu[3072:], np.zeros(96, np.float32)]))
    vectors = [mu[:1024], mu[1024:2048], mu[2048:3072]] + [
        i[n][0].reshape(-1) for n in ("rwkv_w0", "rwkv_a0", "rwkv_k_k", "rwkv_k_a", "rwkv_r_k")]
    a["rwkv_vec"] = np.stack(vectors).reshape(8, 8, P).transpose(1, 2, 0)
    up = cat([i["rwkv_w2"][0], i["rwkv_a2"][0], i["rwkv_g2"][0], blank(96, 1024)], 0)
    a["lora_up"] = up.reshape(3, P, 8, P).transpose(2, 1, 0, 3)
    a["rwkv_ln"] = np.stack([i["rwkv_ln_w"][0], i["rwkv_ln_b"][0]]).reshape(2, 8, P).transpose(2, 0, 1)
    a["lambda_qk"] = np.stack([i[n][0] for n in ("diff_lq1", "diff_lq2", "diff_lk1", "diff_lk2")], 1)
    a["subln_1"] = np.tile(column(i["diff_subln_w"][0]), (1, 8))
    for name, key in (("rwkv_out_1", "rwkv_w_o"), ("diff_out_1", "diff_w_o"), ("w_out_1", "w_out"), ("mlp_in_1", "mlp_w1"),
                      ("mlp_out_1", "mlp_w2")):
        a[name] = tiles(i[key][0])
    w = i["w_in_2"][0]
    heads = [j + 4 * e for j in range(4) for e in range(2)]
    q_cols = [64 * h + d for h in heads for d in range(64)]
    gate_cols = [2304 + 3 * h + b for h in heads for b in range(3)]
    a["w_in_2"] = tiles(cat([w[:, :1024], w[:, [1024 + q for q in q_cols]], w[:, 1536:2304], w[:, gate_cols], blank(1024, 104)], 1))
    a["w_gates_2"] = tiles(w[:, 2328:])
    vectors = cat([i["conv_dw_w_2"][0], i["conv_dw_b_2"], i["conv_ln_g_2"], i["conv_ln_b_2"]], 0)
    a["conv_taps"] = vectors.reshape(-1, 4, P).transpose(2, 1, 0)
    a["conv_out_2"], a["attn_out_2"] = tiles(i["w_conv_out_2"][0], 4), tiles(i["w_attn_out_2"][0][q_cols], 4)
    a["rel_bias"] = i["rel_bias_2"]
    pe = np.stack([i["cmp_pe_k_2"][0].T, i["cmp_pe_v_2"][0].T])
    a["cmp_pe"] = np.repeat(cat([pe, pe], 1)[..., None], NC2, -1)
    a["cmp_w1"] = np.stack([i["w_ck1_2"][0], i["w_cv1_2"][0]]).reshape(2, 32, 64, 256).transpose(0, 2, 1, 3)
    a["cmp_w2"] = np.stack([i["w_ck2_2"][0], i["w_cv2_2"][0]]).reshape(2, 2, P, 64).transpose(0, 2, 1, 3)
    a["w_out_2"], a["ple_gate_2"], a["ple_2"] = tiles(i["w_out_2"][0]), tiles(i["w_ple_gate_2"][0]), tiles(i["w_ple_2"][0], 2)
    up = tiles(i["w_up_2"][0])[:, 0]
    a["ffn_up_2"] = np.stack([up[:22], up[22:]], 1)
    a["ffn_taps"] = cat([i["ffn_dw_w_2"][0], i["ffn_dw_b_2"]], 0).reshape(4, 44, P).transpose(2, 1, 0)
    a["ffn_down_2"] = tiles(i["w_down_2"][0], 11)
    a["p_2"] = by_feature(i["p_2"][0, 0])
    for name, key in (("norm_mix_2", "norm_mix_2"), ("norm_ffn_2", "norm_ffn_2"), ("norm_ple_2", "norm_ple_2"), ("norm_final_2", "norm_final_2")):
        a[name] = column(i[key])
    w = i["w_in_3"][0]
    small = [part for at in (2048, 2052, 6168, 6172) for part in (w[:, at:at + 4], blank(1024, 28))]
    a["w_mlstm_3"] = tiles(cat([w[:, :2048]] + small + [w[:, 4104:4120], blank(1024, 112)], 1))
    a["w_gla_in_3"], a["w_gdn_3"], a["w_gates_3"] = tiles(w[:, 2056:4104]), tiles(w[:, 4120:6168]), tiles(w[:, 6176:])
    a["gate_bias"] = np.stack([i["b_if_3"][0, :4], i["b_if_3"][0, 4:], i["dt_bias_3"][0], i["a_log_3"][0]], 1)
    a["gla_w"], a["gla_b"] = i["w_gla_lr_3"][0], column(i["b_gla_3"])
    a["gdn_taps"] = i["conv_gdn_3"][0].reshape(4, 12, P).transpose(2, 1, 0)
    for name, key in (("norm_mix_3", "g_norm_mix_3"), ("norm_mlp_3", "g_norm_mlp_3"), ("norm_mlstm_3", "g_head_mlstm_3"),
                      ("norm_gla_3", "g_head_gla_3"), ("norm_gdn_3", "g_head_gdn_3"), ("norm_final_3", "g_final_3")):
        a[name] = column(i[key])
    a["up_3"] = np.stack([tiles(i["w_up_3"][0, n], 4) for n in range(3)])
    a["w_out_3"], a["mlp_in_3"], a["mlp_out_3"] = tiles(i["w_out_3"][0]), tiles(i["w_mlp_in_3"][0]), tiles(i["w_mlp_out_3"][0])
    return a


def kernel(**inputs):
    import concourse.bacc as bacc
    from concourse.bass_utils import run_bass_kernel_spmd

    nc = bacc.Bacc("TRN2", target_bir_lowering=False, num_devices=1)
    arrays, args = {}, {}
    for name, value in arguments({n: np.asarray(v) for n, v in inputs.items()}).items():
        value = np.ascontiguousarray(value)
        arrays[f"in_{name}"] = value
        args[name] = nc.dram_tensor(f"in_{name}", value.shape, mybir.dt.from_np(value.dtype), kind="ExternalInput").ap()
    out = nc.dram_tensor("out_features", (P, 8, T2), F32, kind="ExternalOutput").ap()
    program(nc, args, out)
    result = run_bass_kernel_spmd(nc, [arrays], core_ids=[0]).results[0]["out_features"]
    return result.transpose(2, 1, 0).reshape(1, T2, 8 * P)
```

```python
import math
from contextlib import ExitStack, contextmanager

import numpy as np
import concourse.bass as bass
from concourse import mybir

F32 = mybir.dt.float32
F32R = mybir.dt.float32r
ALU = mybir.AluOpType
ACT = mybir.ActivationFunctionType
AX_X = mybir.AxisListType.X
P = 128
BANK = 512


class Stage:

    def __init__(self, nc, memory):
        self.nc, self.memory, self.sems = nc, memory, []

    def sb(self, name, shape, dtype=F32):
        return self.memory.enter_context(self.nc.sbuf_tensor(f"{name}_{self.nc.next_id()}", shape, dtype))

    def ps(self, name, shape):
        return self.memory.enter_context(self.nc.psum_tensor(f"{name}_{self.nc.next_id()}", shape, F32))

    def sem(self, name):
        s = self.nc.alloc_semaphore(f"{name}_{self.nc.next_id()}")
        self.sems.append(s)
        return s


@contextmanager
def stage(nc):
    with ExitStack() as memory:
        s = Stage(nc, memory)
        yield s
    nc.clear_and_free_semaphores(s.sems)
    nc.all_engine_barrier()


def halves(T):
    n = -(-T // BANK)
    assert T % n == 0
    return n, T // n


def dense(nc, w, x, dst, T, func=None, residual=None, gate=None, n_body=2, ring=None, loads=(), side=None):
    N, KG, _, KP, _ = w.shape
    K = KG * KP
    U = n_body * KG
    R = ring or U
    A = R - 1
    rounds, last = N // n_body, N // n_body - 1
    assert N % n_body == 0 and U % R == 0 and R >= 2
    nh, th = halves(T)
    assert n_body * nh <= 8
    raw_x = None if isinstance(x, tuple) else x
    n_pieces = min(4, KP)
    pieces = [range(KP * i // n_pieces, KP * (i + 1) // n_pieces) for i in range(n_pieces)]
    with stage(nc) as s:
        wbuf = [s.sb("wbuf", [P, KP, P]) for _ in range(R)]
        whi, wlo = ([s.sb(n, [P, KP, P], F32R) for _ in range(R)] for n in ("whi", "wlo"))
        if raw_x is None:
            xhi, xlo = x
        else:
            xhi, xlo = s.sb("xhi", [P, K, T], F32R), s.sb("xlo", [P, K, T], F32R)
        acc = [s.ps("acc", [P, nh, BANK]) for _ in range(n_body)]
        square = [s.sb("square", [P, nh, th]) for _ in range(2)] if func == "relu2" else None
        gated = s.sb("gated", [P, nh, th]) if gate is not None and residual is not None else None
        w_loaded = [s.sem("w_loaded") for _ in range(R)]
        piece_loaded = [s.sem("piece_loaded") for _ in pieces]
        piece_hi, piece_lo = s.sem("piece_hi"), s.sem("piece_lo")
        arrived, side_order = s.sem("arrived"), s.sem("side_order")
        hi_ready, lo_ready, x_hi, x_lo, w_used, acc_free, square_free, order = (
            s.sem(n) for n in ("hi_ready", "lo_ready", "x_hi", "x_lo", "w_used", "acc_free", "square_free", "order"))

        def token_view(ap):
            return ap.rearrange("p (h t) -> p h t", h=nh)

        def run(eng, body):
            body(0)
            if rounds > 2:
                with eng.Fori(1, last) as it:
                    body(it)
            if rounds > 1:
                body(last)

        def is_last(it):
            return isinstance(it, int) and it == last

        def lo_part(eng, it, u):
            eng.wait_ge(hi_ready, it * U + (u + 1))
            eng.tensor_tensor(wlo[u % R][:], wbuf[u % R][:], whi[u % R][:].bitcast(F32), ALU.subtract).then_inc(lo_ready, 1)

        def first_lo_part(eng, i, ks):
            last_piece = i == n_pieces - 1
            eng.wait_ge(*((hi_ready, 1) if last_piece else (piece_hi, i + 1)))
            eng.tensor_tensor(wlo[0][:, ks.start:ks.stop, :], wbuf[0][:, ks.start:ks.stop, :],
                              whi[0][:, ks.start:ks.stop, :].bitcast(F32),
                              ALU.subtract).then_inc(lo_ready if last_piece else piece_lo, 1)

        with nc.Block() as block:
            @block.sync
            def _(sp):
                for i, ks in enumerate(pieces):
                    sp.dma_start(wbuf[0][:, ks.start:ks.stop, :], w[0, 0, :, ks.start:ks.stop, :]).then_inc(piece_loaded[i], 16)
                for q in range(1, R):
                    sp.dma_start(wbuf[q][:], w[q // KG, q % KG]).then_inc(w_loaded[q], 16)

                def body(it):
                    for u in range(U - R if is_last(it) else U):
                        sp.wait_ge(lo_ready, it * U + (u + 1))
                        sp.dma_start(wbuf[u % R][:], w[it * n_body + (u + R) // KG, (u + R) % KG]).then_inc(w_loaded[u % R], 16)
                run(sp, body)

            @block.tensor
            def _(pe):
                def body(it):
                    first = isinstance(it, int) and it == 0
                    for u in range(U):
                        b, g, j = u // KG, u % KG, u % R
                        if g == 0 and not first:
                            pe.wait_ge(acc_free, it * n_body + (b + 1 - n_body))
                        if not (first and u == 0):
                            pe.wait_ge(lo_ready, it * U + (u + 1))
                        for k in range(KP):
                            kx = g * KP + k
                            for i, ks in enumerate(pieces):
                                if first and u == 0 and k == ks.start:
                                    pe.wait_ge(*((piece_lo, i + 1) if i < n_pieces - 1 else (lo_ready, 1)))
                            if first and b == 0 and raw_x is not None:
                                pe.wait_ge(x_lo, kx + 1)
                            for h in range(nh):
                                cols = slice(h * th, (h + 1) * th)
                                for i, (wt, xt) in enumerate(((whi, xhi), (whi, xlo), (wlo, xhi))):
                                    mm = nc.tensor.matmul(acc[b][:, h, 0:th], wt[j][:, k, :], xt[:, kx, cols],
                                                          start=(kx == 0 and i == 0), stop=(kx == K - 1 and i == 2))
                        mm.then_inc(w_used, 1)
                body(0)
                if rounds > 1:
                    with pe.Fori(1, rounds) as it:
                        body(it)

            @block.scalar
            def _(act):
                def hi_part(it, u):
                    act.wait_ge(w_loaded[u % R], (it * (U // R) + (u // R + (1 if u % R else 0))) * 16)
                    nc.scalar.activation(whi[u % R][:], wbuf[u % R][:], ACT.Copy).then_inc(hi_ready, 1)

                def x_part(k):
                    if raw_x is not None:
                        nc.scalar.activation(xhi[:, k, :], raw_x[:, k, :], ACT.Copy).then_inc(x_hi, 1)

                for i, ks in enumerate(pieces):
                    act.wait_ge(piece_loaded[i], 16)
                    nc.scalar.activation(whi[0][:, ks.start:ks.stop, :], wbuf[0][:, ks.start:ks.stop, :],
                                         ACT.Copy).then_inc(piece_hi if i < n_pieces - 1 else hi_ready, 1)
                    for k in ks:
                        x_part(k)
                for k in range(KP, K):
                    x_part(k)
                for u in range(1, A):
                    hi_part(0, u)
                for to, source in loads:
                    act.dma_start(to, source).then_inc(arrived, 16)

                def body(it):
                    for u in range(U):
                        if not is_last(it) or u + A < U:
                            if not (isinstance(it, int) and it == 0 and u == 0):
                                act.wait_ge(w_used, it * U + u)
                            hi_part(it, u + A)
                        if u % KG == KG - 1 and func is not None:
                            b = u // KG
                            act.wait_ge(w_used, it * U + (u + 1))
                            if func == "relu2":
                                if b >= 2 or not (isinstance(it, int) and it == 0):
                                    act.wait_ge(square_free, it * n_body + (b - 1))
                                nc.scalar.activation(square[b % 2][:], acc[b][:, :, 0:th], ACT.Relu).then_inc(acc_free, 1)
                            else:
                                nc.scalar.activation(token_view(dst[:, it * n_body + b, :]), acc[b][:, :, 0:th],
                                                     func).then_inc(acc_free, 1)
                run(act, body)
                if loads:
                    act.wait_ge(arrived, 16 * len(loads))

            if side is not None:
                @block.gpsimd
                def _(pool):
                    for i, ks in enumerate(pieces):
                        first_lo_part(nc.gpsimd, i, ks)
                    for u in range(1, A):
                        lo_part(nc.gpsimd, 0, u)

                    def body(it):
                        for u in range(U):
                            if not is_last(it) or u + A < U:
                                lo_part(nc.gpsimd, it, u + A)
                    run(pool, body)

            @block.vector
            def _(dve):
                def x_part(k):
                    if raw_x is not None:
                        dve.wait_ge(x_hi, k + 1)
                        nc.vector.tensor_tensor(xlo[:, k, :], raw_x[:, k, :], xhi[:, k, :].bitcast(F32),
                                                ALU.subtract).then_inc(x_lo, 1)

                for i, ks in enumerate(pieces):
                    if side is None:
                        first_lo_part(nc.vector, i, ks)
                    for k in ks:
                        x_part(k)
                for k in range(KP, K):
                    x_part(k)
                for u in range(1, A if side is None else 0):
                    lo_part(nc.vector, 0, u)

                def body(it):
                    chain = Chain(dve, order, it, 2 * n_body if func == "relu2" else n_body if gated is not None else 0)
                    for u in range(U):
                        if side is None and (not is_last(it) or u + A < U):
                            lo_part(nc.vector, it, u + A)
                        if side is not None:
                            side(dve, side_order, it, u)
                        if u % KG == KG - 1 and (func is None or func == "relu2"):
                            b = u // KG
                            n = it * n_body + b
                            if func is None:
                                dve.wait_ge(w_used, it * U + (u + 1))
                                out, total = token_view(dst[:, n, :]), acc[b][:, :, 0:th]
                                if gate is not None:
                                    product = nc.vector.tensor_tensor(out if gated is None else gated[:], total,
                                                                      token_view(gate[:, n, :]), ALU.mult)
                                    product.then_inc(acc_free, 1)
                                    if gated is not None:
                                        dve.wait_ge(acc_free, it * n_body + (b + 1))
                                        chain(nc.vector.tensor_tensor(out, gated[:], token_view(residual[:, n, :]), ALU.add))
                                else:
                                    nc.vector.tensor_tensor(out, total, token_view(residual[:, n, :]), ALU.add).then_inc(acc_free, 1)
                            else:
                                sq, hi, lo = square[b % 2], token_view(dst[0][:, n, :]), token_view(dst[1][:, n, :])
                                dve.wait_ge(acc_free, it * n_body + (b + 1))
                                chain(nc.vector.tensor_tensor(sq[:], sq[:], sq[:], ALU.mult))
                                chain(nc.vector.tensor_copy(hi, sq[:]))
                                nc.vector.tensor_tensor(lo, sq[:], hi.bitcast(F32), ALU.subtract).then_inc(square_free, 1)
                    chain.close()
                run(dve, body)


def settle(eng, sem):
    eng.wait_ge(sem, 1)


class Chain:

    def __init__(self, eng, sem, round_no=0, per_round=0):
        self.eng, self.sem, self.n, self.round_no, self.per_round = eng, sem, 0, round_no, per_round

    def __call__(self, ins):
        self.n += 1
        ins.then_inc(self.sem, 1)
        self.eng.wait_ge(self.sem, self.round_no * self.per_round + self.n)

    def close(self):
        assert self.n == self.per_round, self.n


def load(nc, pairs):
    with stage(nc) as s:
        arrived = s.sem("arrived")
        with nc.Block() as block:
            @block.sync
            def _(sp):
                for dst, src in pairs:
                    sp.dma_start(dst, src).then_inc(arrived, 16)
                sp.wait_ge(arrived, 16 * len(pairs))


def rmsnorm(nc, ones, x, weight, out, T, eps, src=None, dst=None):
    pair = isinstance(out, tuple)
    K = x.shape[1]
    nh, th = halves(T)
    with stage(nc) as s:
        w = s.sb("norm_w", [P, K])
        sq = s.sb("squares", [P, K, T])
        rstd = s.sb("rstd", [P, T])
        acc = s.ps("sum_squares", [P, nh, BANK])
        loaded, squared, summed = s.sem("loaded"), s.sem("squared"), s.sem("summed")
        mean_ready, root_ready, order, stored = s.sem("mean_ready"), s.sem("root_ready"), s.sem("order"), s.sem("stored")
        ready, hi_ready = s.sem("normed"), s.sem("hi_ready")
        whole = sq if pair else out
        acc_v = acc[:, :, 0:th]
        rstd_v = rstd[:].rearrange("p (h t) -> p h t", h=nh)
        with nc.Block() as block:
            @block.sync
            def _(sp):
                sp.dma_start(w[:], weight).then_inc(loaded, 16)
                if src is not None:
                    for k in range(K):
                        sp.dma_start(x[:, k, :], src[:, k, :]).then_inc(loaded, 16)
                if dst is not None:
                    for k in range(K):
                        sp.wait_ge(ready, k + 1)
                        sp.dma_start(dst[:, k, :], out[:, k, :]).then_inc(stored, 16)
                    sp.wait_ge(stored, 16 * K)

            @block.scalar
            def _(act):
                for k in range(K):
                    if src is not None and k == 0:
                        act.wait_ge(loaded, 16 + 16 * K)
                    nc.scalar.activation(sq[:, k, :], x[:, k, :], ACT.Square).then_inc(squared, 1)
                act.wait_ge(mean_ready, 1)
                nc.scalar.activation(rstd[:], rstd[:], ACT.Sqrt).then_inc(root_ready, 1)
                if pair:
                    for k in range(K):
                        act.wait_ge(ready, k + 1)
                        nc.scalar.activation(out[0][:, k, :], whole[:, k, :], ACT.Copy).then_inc(hi_ready, 1)

            @block.tensor
            def _(pe):
                for k in range(K):
                    pe.wait_ge(squared, k + 1)
                    for h in range(nh):
                        mm = nc.tensor.matmul(acc[:, h, 0:th], ones[:], sq[:, k, h * th:(h + 1) * th],
                                              start=(k == 0), stop=(k == K - 1))
                mm.then_inc(summed, 1)

            @block.vector
            def _(dve):
                def low_part(k):
                    dve.wait_ge(hi_ready, k + 1)
                    nc.vector.tensor_tensor(out[1][:, k, :], whole[:, k, :], out[0][:, k, :].bitcast(F32), ALU.subtract)

                chain = Chain(dve, order)
                dve.wait_ge(summed, 1)
                nc.vector.tensor_scalar(rstd_v, acc_v, 1.0 / (K * P), eps, ALU.mult, ALU.add).then_inc(mean_ready, 1)
                dve.wait_ge(root_ready, 1)
                chain(nc.vector.reciprocal(rstd[:], rstd[:]))
                dve.wait_ge(loaded, 16 if src is None else 16 + 16 * K)
                for k in range(K):
                    nc.vector.scalar_tensor_tensor(out=whole[:, k, :], in0=x[:, k, :], scalar=w[:, k:k + 1], in1=rstd[:],
                                                   op0=ALU.mult, op1=ALU.mult).then_inc(ready, 1)
                    if pair and k > 0:
                        low_part(k - 1)
                if pair:
                    low_part(K - 1)


T1 = 528
RC = 66
RN = T1 // RC
QT = 88
QN = T1 // QT
EXP_HALF = math.exp(-0.5)
LEVELS1 = math.ceil(math.log2(RC))


def rwkv_lora_inputs(nc, c, p):
    with stage(nc) as s:
        mu = s.sb("mu", [P, 3])
        diff = s.sb("diff", [P, 3, T1])
        loaded, order, mixed = s.sem("loaded"), s.sem("order"), s.sem("mixed")
        with nc.Block() as block:
            @block.sync
            def _(sp):
                sp.dma_start(mu[:], c["lora_mu"]).then_inc(loaded, 16)

            @block.vector
            def _(dve):
                chain = Chain(dve, order)
                chain(nc.vector.tensor_tensor(diff[:], p[:, 24:27, 0:T1], p[:, 24:27, 1:T1 + 1], ALU.subtract))
                dve.wait_ge(loaded, 16)
                for i in range(3):
                    nc.vector.scalar_tensor_tensor(out=p[:, 24 + i, 1:T1 + 1], in0=diff[:, i, :], scalar=mu[:, i:i + 1],
                                                   in1=p[:, 24 + i, 1:T1 + 1], op0=ALU.mult, op1=ALU.add).then_inc(mixed, 1)

            @block.scalar
            def _(act):
                act.wait_ge(mixed, 3)
                nc.scalar.activation(p[0:64, 24, 1:T1 + 1], p[0:64, 24, 1:T1 + 1], ACT.Tanh)
                nc.scalar.activation(p[:, 25:27, 1:T1 + 1], p[:, 25:27, 1:T1 + 1], ACT.Sigmoid)


def rwkv_prepare(nc, c, p, chunks, chunk_decay, bonus_scr, gate_scr):
    with stage(nc) as s:
        vecs = [s.sb("vec", [P, 8]) for _ in range(2)]
        lora_ws = [s.sb("lora_w", [P, 3, P]) for _ in range(2)]
        facs = [s.sb("factors", [P, 5, T1]) for _ in range(2)]
        r, k, kk, kn, a, lw, cum, ecum, eneg, eprev, tmp, sq = (
            s.sb(n, [P, T1]) for n in "r k kk kn a lw cum ecum eneg eprev tmp sq".split())
        bonuses, gates = ([s.sb(n, [P, T1]) for _ in range(2)] for n in ("bonus", "gate"))
        dif = s.sb("dif", [P, T1])
        za, zw, zg, zs = (s.ps(n, [P, 2, BANK]) for n in ("za", "zw", "zg", "zs"))
        z_ready, w_sig, a_sig, g_out = (s.sem(n) for n in ("z_ready", "w_sig", "a_sig", "g_out"))
        loaded, stored = ([s.sem(n) for _ in range(2)] for n in ("loaded", "stored"))
        order, cum_ready, prev_ready, kk_ready, sq_ready, ss_ready = (
            s.sem(n) for n in ("order", "cum_ready", "prev_ready", "kk_ready", "sq_ready", "ss_ready"))
        root_ready, ecum_ready, eprev_ready, rk_ready, bs_ready, fac_ready = (
            s.sem(n) for n in ("root_ready", "ecum_ready", "eprev_ready", "rk_ready", "bs_ready", "fac_ready"))
        H = T1 // 2

        def hv(ap):
            return ap.rearrange("p (h t) -> p h t", h=2)

        STORES = 7
        with nc.Block() as block:
            @block.sync
            def _(sp):
                def load_tile(i, b):
                    sp.dma_start(vecs[b][:], c["rwkv_vec"][i]).then_inc(loaded[b], 16)
                    sp.dma_start(lora_ws[b][:], c["lora_up"][i]).then_inc(loaded[b], 16)

                def store_tile(i, b):
                    sp.wait_ge(fac_ready, i + 1)
                    sp.wait_ge(g_out, i + 1)
                    for q in range(5):
                        sp.dma_start(chunks[:, :, i, q, :].rearrange("c p t -> p c t"),
                                     facs[b][:, q, :].rearrange("p (c t) -> p c t", c=RN)).then_inc(stored[b], 16)
                    sp.dma_start(bonus_scr[:, i, :], bonuses[b][:]).then_inc(stored[b], 16)
                    sp.dma_start(gate_scr[:, i, :], gates[b][:]).then_inc(stored[b], 16)

                for b in range(2):
                    load_tile(b, b)
                with sp.Fori(0, 3) as it:
                    for b in range(2):
                        store_tile(it * 2 + b, b)
                        load_tile(it * 2 + (b + 2), b)
                for b in range(2):
                    store_tile(6 + b, b)
                for b in range(2):
                    sp.wait_ge(stored[b], 4 * (16 * STORES))

            @block.tensor
            def _(pe):
                with pe.Fori(0, 4) as it:
                    for b in range(2):
                        i, vec, lora_w, fac, bonus, gate = it * 2 + b, vecs[b], lora_ws[b], facs[b], bonuses[b], gates[b]
                        pe.wait_ge(loaded[b], it * 32 + 32)
                        pe.wait_ge(fac_ready, i)
                        for h in range(2):
                            cols = slice(1 + h * H, 1 + (h + 1) * H)
                            nc.tensor.matmul(zw[:, h, 0:H], lora_w[0:64, 0, :], p[0:64, 24, cols], start=True, stop=True)
                            nc.tensor.matmul(za[:, h, 0:H], lora_w[64:128, 0, :], p[64:128, 24, cols], start=True, stop=True)
                            nc.tensor.matmul(zg[:, h, 0:H], lora_w[:, 1, :], p[:, 25, cols], start=True, stop=False)
                            mm = nc.tensor.matmul(zg[:, h, 0:H], lora_w[:, 2, :], p[:, 26, cols], start=False, stop=True)
                        mm.then_inc(z_ready, 1)
                        pe.wait_ge(sq_ready, i + 1)
                        for h in range(2):
                            mm = nc.tensor.matmul(zs[:, h, 0:H], c["blk64"][:], sq[:, h * H:(h + 1) * H], start=True, stop=True)
                        mm.then_inc(ss_ready, 1)
                        pe.wait_ge(rk_ready, i + 1)
                        pe.wait_ge(w_sig, i + 1)
                        for h in range(2):
                            mm = nc.tensor.matmul(zw[:, h, 0:H], c["blk64"][:], tmp[:, h * H:(h + 1) * H], start=True, stop=True)
                        mm.then_inc(bs_ready, 1)

            @block.scalar
            def _(act):
                with act.Fori(0, 4) as it:
                    for b in range(2):
                        i, vec, lora_w, fac, bonus, gate = it * 2 + b, vecs[b], lora_ws[b], facs[b], bonuses[b], gates[b]
                        act.wait_ge(z_ready, i + 1)
                        act.wait_ge(fac_ready, i)
                        nc.scalar.activation(hv(lw[:]), zw[:, :, 0:H], ACT.Sigmoid, bias=vec[:, 3:4]).then_inc(w_sig, 1)
                        nc.scalar.activation(hv(a[:]), za[:, :, 0:H], ACT.Sigmoid, bias=vec[:, 4:5]).then_inc(a_sig, 1)
                        act.wait_ge(stored[b], it * (16 * STORES))
                        nc.scalar.activation(hv(gate[:]), zg[:, :, 0:H], ACT.Copy).then_inc(g_out, 1)
                        act.wait_ge(kk_ready, i + 1)
                        nc.scalar.activation(sq[:], kk[:], ACT.Square).then_inc(sq_ready, 1)
                        act.wait_ge(cum_ready, i + 1)
                        nc.scalar.activation(ecum[:], cum[:], ACT.Exp)
                        nc.scalar.activation(eneg[:], cum[:], ACT.Exp, scale=-1.0).then_inc(ecum_ready, 1)
                        act.wait_ge(prev_ready, i + 1)
                        nc.scalar.activation(eprev[:], eprev[:], ACT.Exp).then_inc(eprev_ready, 1)
                        act.wait_ge(ss_ready, i + 1)
                        nc.scalar.activation(hv(kn[:]), zs[:, :, 0:H], ACT.Sqrt).then_inc(root_ready, 1)

            @block.vector
            def _(dve):
                with dve.Fori(0, 4) as it:
                    for b in range(2):
                        i, vec, lora_w, fac, bonus, gate = it * 2 + b, vecs[b], lora_ws[b], facs[b], bonuses[b], gates[b]
                        chain = Chain(dve, order, i, 14)
                        TT, STT = nc.vector.tensor_tensor, nc.vector.scalar_tensor_tensor

                        def shift(tile, mu, out):
                            src, prev = p[:, tile, 1:T1 + 1], p[:, tile, 0:T1]
                            chain(TT(dif[:], prev, src, ALU.subtract))
                            return STT(out=out, in0=dif[:], scalar=mu, in1=src, op0=ALU.mult, op1=ALU.add)

                        dve.wait_ge(loaded[b], it * 32 + 32)
                        dve.wait_ge(stored[b], it * (16 * STORES))
                        chain(shift(i + 8, vec[:, 1:2], k[:]))
                        nc.vector.tensor_scalar(kk[:], k[:], vec[:, 5:6], None, ALU.mult).then_inc(kk_ready, 1)
                        chain(shift(i, vec[:, 0:1], r[:]))
                        chain(shift(i + 16, vec[:, 2:3], fac[:, 4, :]))
                        dve.wait_ge(w_sig, i + 1)
                        chain(nc.vector.tensor_scalar(lw[:], lw[:], -EXP_HALF, None, ALU.mult))
                        nc.vector.tensor_tensor_scan(cum[:], c["chunk_start66"][:], lw[:], 0.0, ALU.mult, ALU.add).then_inc(cum_ready, 1)
                        dve.wait_ge(cum_ready, i + 1)
                        TT(eprev[:], cum[:], lw[:], ALU.subtract).then_inc(prev_ready, 1)
                        dve.wait_ge(a_sig, i + 1)
                        chain(nc.vector.tensor_scalar(dif[:], a[:], -1.0, vec[:, 6:7], ALU.add, ALU.mult))
                        chain(STT(out=k[:], in0=dif[:], scalar=1.0, in1=k[:], op0=ALU.add, op1=ALU.mult))
                        dve.wait_ge(root_ready, i + 1)
                        chain(nc.vector.tensor_scalar(kn[:], kn[:], 1e-12, None, ALU.max))
                        chain(nc.vector.reciprocal(kn[:], kn[:]))
                        chain(TT(kn[:], kn[:], kk[:], ALU.mult))
                        STT(out=tmp[:], in0=r[:], scalar=vec[:, 7:8], in1=k[:], op0=ALU.mult, op1=ALU.mult).then_inc(rk_ready, 1)
                        dve.wait_ge(eprev_ready, i + 1)
                        STT(out=fac[:, 0, :], in0=kn[:], scalar=-1.0, in1=eprev[:], op0=ALU.mult, op1=ALU.mult)
                        TT(fac[:, 1, :], r[:], ecum[:], ALU.mult)
                        TT(fac[:, 3, :], k[:], eneg[:], ALU.mult)
                        chain(TT(kn[:], kn[:], a[:], ALU.mult))
                        TT(fac[:, 2, :], kn[:], eneg[:], ALU.mult)
                        chain(nc.vector.tensor_copy(chunk_decay[:, i, :], ecum[:].rearrange("p (c t) -> p c t", c=RN)[:, :, RC - 1]))
                        dve.wait_ge(bs_ready, i + 1)
                        TT(hv(bonus[:]), zw[:, :, 0:H], hv(fac[:, 4, :]), ALU.mult).then_inc(fac_ready, 1)
                        chain.close()


def rwkv_chunks(nc, c, y, chunks, chunk_decay):
    HG = 4
    GS = range(16 // HG)
    L = LEVELS1
    with stage(nc) as s:
        cbs = [s.sb("chunk", [P, 8, 5, RC]) for _ in range(2)]
        state = s.sb("state", [P, 8, 64])
        tok = s.sb("tok", [RC, 8, 3, P])
        bp = s.sb("bp", [RC, 16, 2, RC])
        kp = s.sb("kp", [RC, 16, 2, RC])
        nm = s.sb("nm", [RC, L, 16, RC])
        t1 = s.sb("t1", [RC, 16, RC])
        xi = s.sb("xi", [RC, 16, RC])
        yi = s.sb("yi", [RC, 16, RC])
        bb = s.sb("bb", [RC, 16, 64])
        ua = s.sb("ua", [RC, 16, 64])
        grown = s.sb("grown", [P, 8, 64])
        psA = [s.ps("psA", [P, BANK]) for _ in GS]
        psB = [s.ps("psB", [P, BANK]) for _ in GS]
        loaded, state_zero = [s.sem("loaded") for _ in range(2)], s.sem("state_zero")
        pe_done = [s.sem("pe_done") for _ in GS]
        act_done = [s.sem("act_done") for _ in GS]
        dve_done = [s.sem("dve_done") for _ in GS]
        level_done = [s.sem("level_done") for _ in GS]
        order = s.sem("order")
        PE_TOK, PE_BP, PE_KP, PE_B, PE_L0 = 1, 2, 3, 4, 5
        PE_T1, PE_XY = (lambda l: 4 + 2 * l), (lambda l: 5 + 2 * l)
        PE_U, PE_Y, PE_S, NPE = 2 * L + 4, 2 * L + 5, 2 * L + 6, 2 * L + 6
        ACT_TOK, ACT_B, ACT_T1, ACT_U, ACT_Y, NACT = 1, 2, (lambda l: 2 + l), L + 2, L + 3, L + 3
        DVE_BP, DVE_KP, DVE_XY, DVE_S, NDVE = 1, 2, (lambda l: 3 + l), L + 3, L + 3

        def heads(g):
            for j in range(HG):
                yield j, HG * g + j, 2 * g + j % 2, slice(64 * (j // 2), 64 * (j // 2) + 64)

        with nc.Block() as block:
            @block.sync
            def _(sp):
                for b in range(2):
                    sp.dma_start(cbs[b][:], chunks[b]).then_inc(loaded[b], 16)
                with sp.Fori(0, RN // 2 - 1) as it:
                    for b in range(2):
                        for g in GS:
                            count = sp.compute_val((it * 2 + (b + 1)) * NPE)
                            settle(sp, state_zero)
                            sp.wait_ge(pe_done[g], count)
                        sp.dma_start(cbs[b][:], chunks[it * 2 + (b + 2)]).then_inc(loaded[b], 16)

            @block.tensor
            def _(pe):
                pe.wait_ge(state_zero, 1)
                with pe.Fori(0, RN // 2) as it:
                    for b in range(2):
                        n, cb = it * 2 + b, cbs[b]
                        def after(what, g, per_chunk, k):
                            pe.wait_ge(what[g], n * per_chunk + k)
                        pe.wait_ge(loaded[b], it * 16 + 16)
                        for g in GS:
                            after(act_done, g, NACT, 0)
                            after(dve_done, g, NDVE, 0)
                            for t, ps in ((2 * g, psA[g]), (2 * g + 1, psB[g])):
                                for q in range(3):
                                    mm = nc.tensor.transpose(ps[0:RC, q * P:(q + 1) * P], cb[:, t, 2 + q, :], c["ident"][:])
                            mm.then_inc(pe_done[g], 1)
                        for q, wait_on, per, k in ((2, act_done, NACT, ACT_TOK), (3, dve_done, NDVE, DVE_BP)):
                            for g in GS:
                                after(wait_on, g, per, k)
                                for j, h, t, rows in heads(g):
                                    ps = psA[g] if j < 2 else psB[g]
                                    mm = nc.tensor.matmul(ps[0:RC, (j % 2) * 2 * RC:(j % 2 + 1) * 2 * RC], cb[rows, t, q, :],
                                                          cb[rows, t, 0:2, :].rearrange("p q t -> p (q t)"), start=True, stop=True)
                                mm.then_inc(pe_done[g], 1)
                        for g in GS:
                            after(dve_done, g, NDVE, DVE_KP)
                            for j, h, t, rows in heads(g):
                                out = (psA, psB)[j // 2][g][0:RC, (j % 2) * 64:(j % 2 + 1) * 64]
                                nc.tensor.matmul(out, cb[rows, t, 0, :], state[rows, t, :], start=True, stop=False)
                                mm = nc.tensor.matmul(out, kp[:, h, 0, :], tok[:, t, 2, rows], start=False, stop=True)
                            mm.then_inc(pe_done[g], 1)
                        for g in GS:
                            after(level_done, g, L, 1)
                            after(act_done, g, NACT, ACT_B)
                            for j, h, t, rows in heads(g):
                                mm = nc.tensor.matmul(psA[g][0:RC, j * RC:(j + 1) * RC], nm[:, 0, h, :], c["ident"][0:RC, 0:RC],
                                                      start=True, stop=True)
                            mm.then_inc(pe_done[g], 1)
                        for l in range(1, L):
                            for g in GS:
                                after(level_done, g, L, l + 1)
                                after(dve_done, g, NDVE, DVE_XY(l - 1))
                                for j, h, t, rows in heads(g):
                                    mm = nc.tensor.matmul(psA[g][0:RC, j * RC:(j + 1) * RC], nm[:, l, h, :], xi[:, h, :],
                                                          start=True, stop=True)
                                mm.then_inc(pe_done[g], 1)
                            for g in GS:
                                after(act_done, g, NACT, ACT_T1(l))
                                for j, h, t, rows in heads(g):
                                    cols = slice(j * RC, (j + 1) * RC)
                                    if l < L - 1:
                                        nc.tensor.matmul(psA[g][0:RC, cols], yi[:, h, :], t1[:, h, :], start=True, stop=True)
                                    mm = nc.tensor.matmul(psB[g][0:RC, cols], t1[:, h, :], yi[:, h, :], start=True, stop=True)
                                mm.then_inc(pe_done[g], 1)
                        for g in GS:
                            after(dve_done, g, NDVE, DVE_XY(L - 1))
                            for j, h, t, rows in heads(g):
                                mm = nc.tensor.matmul(psA[g][0:RC, j * 64:(j + 1) * 64], yi[:, h, :], bb[:, h, :], start=True, stop=True)
                            mm.then_inc(pe_done[g], 1)
                        for g in GS:
                            after(act_done, g, NACT, ACT_U)
                            for j, h, t, rows in heads(g):
                                out = (psA, psB)[j // 2][g][rows, (j % 2) * RC:(j % 2 + 1) * RC]
                                nc.tensor.matmul(out, tok[:, t, 2, rows], kp[:, h, 1, :], start=True, stop=False)
                                nc.tensor.matmul(out, state[rows, t, :], cb[rows, t, 1, :], start=False, stop=False)
                                mm = nc.tensor.matmul(out, ua[:, h, :], bp[:, h, 1, :], start=False, stop=True)
                            mm.then_inc(pe_done[g], 1)
                        for g in GS:
                            after(act_done, g, NACT, ACT_Y)
                            for j, h, t, rows in heads(g):
                                out = psA[g][rows, (j % 2) * 64:(j % 2 + 1) * 64]
                                nc.tensor.matmul(out, tok[:, t, 0, rows], ua[:, h, :], start=True, stop=False)
                                mm = nc.tensor.matmul(out, tok[:, t, 1, rows], tok[:, t, 2, rows], start=False, stop=True)
                            mm.then_inc(pe_done[g], 1)

            @block.scalar
            def _(act):
                with act.Fori(0, RN // 2) as it:
                    for b in range(2):
                        n, cb = it * 2 + b, cbs[b]
                        def after(g, k):
                            act.wait_ge(pe_done[g], n * NPE + k)
                        for g in GS:
                            after(g, PE_TOK)
                            for t, ps in ((2 * g, psA[g]), (2 * g + 1, psB[g])):
                                cp = nc.scalar.activation(tok[:, t, :, :].rearrange("p q d -> p (q d)"), ps[0:RC, 0:3 * P], ACT.Copy)
                            cp.then_inc(act_done[g], 1)
                        for g in GS:
                            after(g, PE_B)
                            for h0, ps in ((HG * g, psA[g]), (HG * g + 2, psB[g])):
                                cp = nc.scalar.activation(bb[:, h0:h0 + 2, :].rearrange("p h v -> p (h v)"), ps[0:RC, 0:128], ACT.Copy)
                            cp.then_inc(act_done[g], 1)
                        for l in range(1, L):
                            for g in GS:
                                after(g, PE_T1(l))
                                nc.scalar.activation(t1[:, HG * g:HG * (g + 1), :].rearrange("p h t -> p (h t)"),
                                                     psA[g][0:RC, 0:HG * RC], ACT.Copy).then_inc(act_done[g], 1)
                        for g in GS:
                            after(g, PE_U)
                            nc.scalar.activation(ua[:, HG * g:HG * (g + 1), :].rearrange("p h v -> p (h v)"), psA[g][0:RC, 0:HG * 64],
                                                 ACT.Copy).then_inc(act_done[g], 1)
                        for g in GS:
                            after(g, PE_Y)
                            for r0, ps in ((0, psA[g]), (64, psB[g])):
                                cp = nc.scalar.activation(y[r0:r0 + 64, 2 * g:2 * g + 2, bass.ds(n * RC, RC)],
                                                          ps[r0:r0 + 64, 0:2 * RC].rearrange("p (a t) -> p a t", a=2), ACT.Copy)
                            cp.then_inc(act_done[g], 1)

            @block.gpsimd
            def _(pool):
                with pool.Fori(0, RN // 2) as it:
                    for b in range(2):
                        n, cb = it * 2 + b, cbs[b]
                        for l in range(L):
                            for g in GS:
                                if l == 0:
                                    pool.wait_ge(dve_done[g], n * NDVE + DVE_BP)
                                nc.gpsimd.tensor_tensor(nm[:, l, HG * g:HG * (g + 1), :], bp[:, HG * g:HG * (g + 1), 0, :],
                                                        c["level66"][:, l, :, :], ALU.mult).then_inc(level_done[g], 1)

            @block.vector
            def _(dve):
                nc.vector.memset(state[:], 0.0).then_inc(state_zero, 1)
                with dve.Fori(0, RN // 2) as it:
                    for b in range(2):
                        n, cb = it * 2 + b, cbs[b]
                        chain = Chain(dve, order, n, 4)
                        TT = nc.vector.tensor_tensor

                        def after(g, k):
                            dve.wait_ge(pe_done[g], n * NPE + k)
                        for what, k in ((bp, PE_BP), (kp, PE_KP)):
                            for g in GS:
                                after(g, k)
                                for half, ps in ((0, psA[g]), (1, psB[g])):
                                    h0 = HG * g + 2 * half
                                    r = TT(what[:, h0:h0 + 2, :, :].rearrange("p h q t -> p (h q t)"), ps[0:RC, 0:4 * RC],
                                           c["causal66"][:], ALU.mult)
                                r.then_inc(dve_done[g], 1)
                        for g in GS:
                            hs = slice(HG * g, HG * (g + 1))
                            after(g, PE_L0)
                            TT(xi[:, hs, :], psA[g][0:RC, 0:HG * RC].rearrange("p (h t) -> p h t", h=HG), c["ident66"][:], ALU.add)
                            TT(yi[:, hs, :], nm[:, 0, hs, :], c["ident66"][:], ALU.add).then_inc(dve_done[g], 1)
                        for l in range(1, L):
                            for g in GS:
                                hs = slice(HG * g, HG * (g + 1))
                                after(g, PE_XY(l))
                                if l < L - 1:
                                    xv = xi[:, hs, :].rearrange("p h t -> p (h t)")
                                    TT(xv, psA[g][0:RC, 0:HG * RC], xv, ALU.add)
                                yv = yi[:, hs, :].rearrange("p h t -> p (h t)")
                                TT(yv, psB[g][0:RC, 0:HG * RC], yv, ALU.add).then_inc(dve_done[g], 1)
                        for g in GS:
                            after(g, PE_S)
                            ts = slice(2 * g, 2 * g + 2)
                            chain(TT(grown[:, ts, :].rearrange("p a v -> p (a v)"), psA[g][:, 0:128],
                                     state[:, ts, :].rearrange("p a v -> p (a v)"), ALU.add))
                            nc.vector.tensor_scalar(state[:, 2 * g, :], grown[:, 2 * g, :], chunk_decay[:, 2 * g, bass.ds(n, 1)], None, ALU.mult)
                            nc.vector.tensor_scalar(state[:, 2 * g + 1, :], grown[:, 2 * g + 1, :], chunk_decay[:, 2 * g + 1, bass.ds(n, 1)], None,
                                                    ALU.mult).then_inc(dve_done[g], 1)
                        chain.close()


def rwkv_finish(nc, c, y, bonus_scr, gate_scr):
    H = T1 // 2
    with stage(nc) as s:
        lnw = s.sb("lnw", [P, 2, 8])
        gate = [s.sb("gate", [P, T1]) for _ in range(2)]
        bonus = [s.sb("bonus", [P, T1]) for _ in range(2)]
        sq = [s.sb("sq", [P, T1]) for _ in range(2)]
        var = [s.sb("var", [P, T1]) for _ in range(2)]
        cen = [s.sb("cen", [P, T1]) for _ in range(2)]
        pm = [s.ps("mean", [P, 2, BANK]) for _ in range(2)]
        pv = [s.ps("var", [P, 2, BANK]) for _ in range(2)]
        vec_in, mean_ready, var_ready = s.sem("vec_in"), s.sem("mean_ready"), s.sem("var_ready")
        loaded = [s.sem("loaded") for _ in range(2)]
        cen_ready, sq_ready, eps_ready, root_ready, done, order = (
            s.sem(n) for n in ("cen_ready", "sq_ready", "eps_ready", "root_ready", "done", "order"))

        def hv(ap):
            return ap.rearrange("p (h t) -> p h t", h=2)
        with nc.Block() as block:
            @block.sync
            def _(sp):
                sp.dma_start(lnw[:], c["rwkv_ln"]).then_inc(vec_in, 16)
                with sp.Fori(0, 4) as it:
                    for b in range(2):
                        sp.wait_ge(done, it * 2)
                        sp.dma_start(gate[b][:], gate_scr[:, it * 2 + b, :]).then_inc(loaded[b], 16)
                        sp.dma_start(bonus[b][:], bonus_scr[:, it * 2 + b, :]).then_inc(loaded[b], 16)

            @block.tensor
            def _(pe):
                with pe.Fori(0, 4) as it:
                    for b in range(2):
                        pe.wait_ge(done, it * 2)
                        for h in range(2):
                            mm = nc.tensor.matmul(pm[b][:, h, 0:H], c["mean64"][:], y[:, it * 2 + b, h * H:(h + 1) * H],
                                                  start=True, stop=True)
                        mm.then_inc(mean_ready, 1)
                    for b in range(2):
                        pe.wait_ge(sq_ready, it * 2 + b + 1)
                        for h in range(2):
                            mm = nc.tensor.matmul(pv[b][:, h, 0:H], c["mean64"][:], sq[b][:, h * H:(h + 1) * H],
                                                  start=True, stop=True)
                        mm.then_inc(var_ready, 1)

            @block.scalar
            def _(act):
                with act.Fori(0, 4) as it:
                    for b in range(2):
                        act.wait_ge(cen_ready, it * 2 + b + 1)
                        nc.scalar.activation(sq[b][:], cen[b][:], ACT.Square).then_inc(sq_ready, 1)
                    for b in range(2):
                        act.wait_ge(eps_ready, it * 2 + b + 1)
                        nc.scalar.activation(var[b][:], var[b][:], ACT.Sqrt).then_inc(root_ready, 1)

            @block.vector
            def _(dve):
                TT, TS = nc.vector.tensor_tensor, nc.vector.tensor_scalar
                dve.wait_ge(vec_in, 16)
                with dve.Fori(0, 4) as it:
                    chain = Chain(dve, order, it, 8)
                    for b in range(2):
                        dve.wait_ge(mean_ready, it * 2 + b + 1)
                        TT(hv(cen[b][:]), hv(y[:, it * 2 + b, :]), pm[b][:, :, 0:H], ALU.subtract).then_inc(cen_ready, 1)
                    for b in range(2):
                        dve.wait_ge(var_ready, it * 2 + b + 1)
                        TS(hv(var[b][:]), pv[b][:, :, 0:H], 64e-5, None, ALU.add).then_inc(eps_ready, 1)
                    for b in range(2):
                        i = it * 2 + b
                        dve.wait_ge(root_ready, i + 1)
                        chain(nc.vector.reciprocal(var[b][:], var[b][:]))
                        chain(TT(cen[b][:], cen[b][:], var[b][:], ALU.mult))
                        chain(TS(cen[b][:], cen[b][:], lnw[:, 0, bass.ds(i, 1)], lnw[:, 1, bass.ds(i, 1)], ALU.mult, ALU.add))
                        dve.wait_ge(loaded[b], it * 32 + 32)
                        chain(TT(cen[b][:], cen[b][:], bonus[b][:], ALU.add))
                        TT(y[:, i, :], cen[b][:], gate[b][:], ALU.mult).then_inc(done, 1)
                    chain.close()


LAMBDA_INIT = 0.8 - 0.6 * math.exp(-0.3 * 0)
NEG = -1e30


def head_rms(nc, ones, o, weight, T, eps, factor=1.0, gate=None, mean=1.0 / P):
    N = o.shape[1]
    nh, th = halves(T)
    with stage(nc) as s:
        w = s.sb("w", [P, N])
        sq = [s.sb("sq", [P, T]) for _ in range(2)]
        rstd = [s.sb("rstd", [P, T]) for _ in range(2)]
        acc = [s.ps("acc", [P, nh, BANK]) for _ in range(2)]
        w_in, w_ready, sq_ready, summed, mean_ready, root_ready, done, order = (
            s.sem(n) for n in ("w_in", "w_ready", "sq_ready", "summed", "mean_ready", "root_ready", "done", "order"))
        with nc.Block() as block:
            @block.sync
            def _(sp):
                sp.dma_start(w[:], weight).then_inc(w_in, 16)

            @block.scalar
            def _(act):
                with act.Fori(0, N // 2) as it:
                    act.wait_ge(summed, it * 2)
                    for b in range(2):
                        nc.scalar.activation(sq[b][:], o[:, it * 2 + b, :], ACT.Square).then_inc(sq_ready, 1)
                    for b in range(2):
                        act.wait_ge(mean_ready, it * 2 + b + 1)
                        nc.scalar.activation(rstd[b][:], rstd[b][:], ACT.Sqrt).then_inc(root_ready, 1)

            @block.tensor
            def _(pe):
                with pe.Fori(0, N // 2) as it:
                    pe.wait_ge(mean_ready, it * 2)
                    for b in range(2):
                        pe.wait_ge(sq_ready, it * 2 + b + 1)
                        for h in range(nh):
                            mm = nc.tensor.matmul(acc[b][:, h, 0:th], ones[:], sq[b][:, h * th:(h + 1) * th], start=True, stop=True)
                        mm.then_inc(summed, 1)

            @block.vector
            def _(dve):
                dve.wait_ge(w_in, 16)
                nc.vector.tensor_scalar(w[:], w[:], factor, None, ALU.mult).then_inc(w_ready, 1)
                dve.wait_ge(w_ready, 1)
                with dve.Fori(0, N // 2) as it:
                    per = 2 + (2 if gate is not None else 0)
                    chain = Chain(dve, order, it, per)
                    dve.wait_ge(done, it * 2)
                    for b in range(2):
                        dve.wait_ge(summed, it * 2 + b + 1)
                        nc.vector.tensor_scalar(rstd[b][:].rearrange("p (h t) -> p h t", h=nh), acc[b][:, :, 0:th], mean, eps,
                                                ALU.mult, ALU.add).then_inc(mean_ready, 1)
                    for b in range(2):
                        i = it * 2 + b
                        dve.wait_ge(root_ready, i + 1)
                        chain(nc.vector.reciprocal(rstd[b][:], rstd[b][:]))
                        if gate is not None:
                            chain(nc.vector.tensor_tensor(rstd[b][:], rstd[b][:], gate[:, i, :], ALU.mult))
                        nc.vector.scalar_tensor_tensor(out=o[:, i, :], in0=o[:, i, :], scalar=w[:, bass.ds(i, 1)], in1=rstd[b][:],
                                                       op0=ALU.mult, op1=ALU.mult).then_inc(done, 1)
                    chain.close()


def diff_attention(nc, c, p, o):
    SCALE = 64 ** -0.5
    HALF = T1 // 2
    OFF = T1 - QT
    with stage(nc) as s:
        lam_in = s.sb("lam_in", [64, 4])
        lam_prod = s.sb("lam_prod", [64, 2])
        lam_exp = s.sb("lam_exp", [P, 2])
        neg_lam = s.sb("neg_lam", [P, 1])
        rot, swapped = s.sb("rot", [P, 2, T1]), s.sb("swapped", [P, T1])
        vt = s.sb("vt", [QT, QN, P])
        sc = [[s.sb("sc", [QT, T1]) for _ in range(2)] for _ in range(2)]
        wt = [s.sb("w", [QT, T1]) for _ in range(2)]
        wT = [s.sb("wT", [QT, QN, QT]) for _ in range(2)]
        small = [[s.sb("small", [QT, 4]) for _ in range(2)] for _ in range(2)]
        ps_s = [s.ps("ps_s", [P, 2, BANK]) for _ in range(2)]
        ps_t = s.ps("ps_t", [P, 2, BANK])
        ps_o = s.ps("ps_o", [P, BANK])
        loaded, lam_mult, lam_sum, lam_done, lam_ready = (s.sem(n) for n in ("loaded", "lam_mult", "lam_sum", "lam_done", "lam_ready"))
        swap_ready, rope_done, vt_ready, vt_copied = (s.sem(n) for n in ("swap_ready", "rope_done", "vt_ready", "vt_copied"))
        sc_ready = [s.sem("sc_ready") for _ in range(2)]
        max_ready = [s.sem("max_ready") for _ in range(2)]
        exp_ready = [s.sem("exp_ready") for _ in range(2)]
        w_ready, wt_ready, wt_copied, pv_ready, pv_copied, order, order2 = (
            s.sem(n) for n in ("w_ready", "wt_ready", "wt_copied", "pv_ready", "pv_copied", "order", "order2"))

        def hv(ap):
            return ap.rearrange("p (h t) -> p h t", h=2)

        def width(q):
            return HALF if q < QN // 2 else T1

        with nc.Block() as block:
            @block.sync
            def _(sp):
                sp.dma_start(lam_in[:], c["lambda_qk"]).then_inc(loaded, 16)

            @block.tensor
            def _(pe):
                pe.wait_ge(lam_mult, 1)
                nc.tensor.matmul(ps_o[:, 0:2], c["ones"][0:64, :], lam_prod[:], start=True, stop=True).then_inc(lam_sum, 1)
                pe.wait_ge(lam_done, 1)
                with pe.Fori(0, 8) as i:
                    for e in range(2):
                        pe.wait_ge(max_ready[e], i * QN)
                        for h in range(2):
                            mm = nc.tensor.matmul(ps_s[e][:, h, 0:HALF], c["rope_swap"][:], p[:, i + 8 * e, h * HALF:(h + 1) * HALF],
                                                  start=True, stop=True)
                        mm.then_inc(swap_ready, 1)
                    pe.wait_ge(wt_copied, i * QN)
                    pe.wait_ge(rope_done, i * 3 + 3)
                    for j in range(QN):
                        mm = nc.tensor.transpose(ps_t[0:QT, j // 3, (j % 3) * P:(j % 3 + 1) * P], swapped[:, j * QT:(j + 1) * QT],
                                                 c["ident"][:])
                    mm.then_inc(vt_ready, 1)
                    for step in range(QN + 3):
                        if step < QN:
                            n = width(step)
                            for e in range(2):
                                pe.wait_ge(max_ready[e], i * QN + step)
                                for h in range(n // HALF):
                                    mm = nc.tensor.matmul(ps_s[e][0:QT, h, 0:HALF], rot[64 * e:64 * e + 64, 0, step * QT:(step + 1) * QT],
                                                          rot[64 * e:64 * e + 64, 1, h * HALF:(h + 1) * HALF], start=True, stop=True)
                                mm.then_inc(sc_ready[e], 1)
                        q = step - 2
                        if 0 <= q < QN:
                            pe.wait_ge(w_ready, i * QN + q + 1)
                            if q == 0:
                                pe.wait_ge(vt_copied, i + 1)
                            pe.wait_ge(wt_copied, i * QN + q)
                            for j in range(q + 1):
                                mm = nc.tensor.transpose(ps_t[0:QT, j // 3, (j % 3) * QT:(j % 3 + 1) * QT],
                                                         wt[q % 2][:, j * QT:(j + 1) * QT], c["ident"][0:QT, 0:QT])
                            mm.then_inc(wt_ready, 1)
                        q = step - 3
                        if 0 <= q < QN:
                            pe.wait_ge(wt_copied, i * QN + q + 1)
                            pe.wait_ge(pv_copied, i * QN + q)
                            for j in range(q + 1):
                                mm = nc.tensor.matmul(ps_o[:, 0:QT], vt[:, j, :], wT[q % 2][:, j, :], start=(j == 0), stop=(j == q))
                            mm.then_inc(pv_ready, 1)

            @block.scalar
            def _(act):
                act.wait_ge(lam_sum, 1)
                nc.scalar.activation(lam_exp[:], ps_o[:, 0:2], ACT.Exp).then_inc(lam_done, 1)
                with act.Fori(0, 8) as i:
                    act.wait_ge(vt_ready, i + 1)
                    nc.scalar.activation(vt[:].rearrange("p (h j) d -> p h (j d)", h=2), ps_t[0:QT, :, 0:3 * P], ACT.Copy).then_inc(vt_copied, 1)
                    for step in range(QN + 3):
                        if step < QN:
                            for e in range(2):
                                b, sm, n = sc[e][step % 2], small[e][step % 2], width(step)
                                act.wait_ge(max_ready[e], i * QN + step + 1)
                                nc.scalar.activation(b[:, 0:n], b[:, 0:n], ACT.Exp, scale=SCALE, bias=sm[:, 1:2],
                                                     accum_out=sm[:, 2:3]).then_inc(exp_ready[e], 1)
                        q = step - 2
                        if 0 <= q < QN:
                            act.wait_ge(wt_ready, i * QN + q + 1)
                            if q >= 2:
                                act.wait_ge(pv_ready, i * QN + q - 1)
                            m = min(q + 1, 3)
                            cp = nc.scalar.activation(wT[q % 2][:, 0:m, :].rearrange("p j t -> p (j t)"), ps_t[0:QT, 0, 0:m * QT], ACT.Copy)
                            if q >= 3:
                                cp = nc.scalar.activation(wT[q % 2][:, 3:q + 1, :].rearrange("p j t -> p (j t)"),
                                                          ps_t[0:QT, 1, 0:(q - 2) * QT], ACT.Copy)
                            cp.then_inc(wt_copied, 1)
                        q = step - 3
                        if 0 <= q < QN:
                            act.wait_ge(pv_ready, i * QN + q + 1)
                            nc.scalar.activation(o[:, i, q * QT:(q + 1) * QT], ps_o[:, 0:QT], ACT.Copy).then_inc(pv_copied, 1)

            @block.vector
            def _(dve):
                TT, TS = nc.vector.tensor_tensor, nc.vector.tensor_scalar
                head = Chain(dve, order)
                dve.wait_ge(loaded, 16)
                TT(lam_prod[:], lam_in[:, 0:2], lam_in[:, 2:4], ALU.mult).then_inc(lam_mult, 1)
                dve.wait_ge(lam_done, 1)
                head(TT(neg_lam[:], lam_exp[:, 1:2], lam_exp[:, 0:1], ALU.subtract))
                head(TS(neg_lam[:], neg_lam[:], -LAMBDA_INIT, None, ALU.add))
                with dve.Fori(0, 8) as i:
                    chain = Chain(dve, order2, i, 4 + 2 * QN + 4 * QN)
                    for e in range(2):
                        dve.wait_ge(swap_ready, i * 2 + e + 1)
                        if e == 0:
                            dve.wait_ge(sc_ready[1], i * QN)
                            dve.wait_ge(vt_ready, i)
                        chain(TT(hv(swapped[:]), ps_s[e][:, :, 0:HALF], hv(c["rope_sin"][:]), ALU.mult))
                        chain(TT(rot[:, e, :], p[:, i + 8 * e, :], c["rope_cos"][:], ALU.mult))
                        TT(rot[:, e, :], rot[:, e, :], swapped[:], ALU.add).then_inc(rope_done, 1)
                        dve.wait_ge(rope_done, i * 3 + e + 1)
                    nc.vector.tensor_copy(swapped[:], p[:, i + 16, :]).then_inc(rope_done, 1)
                    for step in range(QN + 1):
                        if step < QN:
                            n = width(step)
                            for e in range(2):
                                b, sm = sc[e][step % 2], small[e][step % 2]
                                count = dve.compute_val(i * QN + step + 1)
                                count_2 = dve.compute_val(i * QN + max(step - 1, 0))
                                settle(dve, loaded)
                                dve.wait_ge(sc_ready[e], count)
                                dve.wait_ge(w_ready, count_2)
                                mask = c["mask88"][:, OFF - QT * step:OFF - QT * step + n]
                                if n == HALF:
                                    chain(nc.vector.tensor_tensor_reduce(out=b[:, 0:n], in0=ps_s[e][0:QT, 0, 0:HALF], in1=mask, scale=1.0,
                                                                         scalar=NEG, op0=ALU.add, op1=ALU.max, accum_out=sm[:, 0:1]))
                                else:
                                    chain(nc.vector.tensor_tensor_reduce(out=hv(b[:]), in0=ps_s[e][0:QT, :, 0:HALF], in1=hv(mask), scale=1.0,
                                                                         scalar=NEG, op0=ALU.add, op1=ALU.max, accum_out=sm[:, 0:1]))
                                TS(sm[:, 1:2], sm[:, 0:1], -SCALE, None, ALU.mult).then_inc(max_ready[e], 1)
                        q = step - 1
                        if 0 <= q < QN:
                            n = width(q)
                            b0, b1, s0, s1 = sc[0][q % 2], sc[1][q % 2], small[0][q % 2], small[1][q % 2]
                            dve.wait_ge(exp_ready[0], i * QN + q + 1)
                            dve.wait_ge(exp_ready[1], i * QN + q + 1)
                            if q >= 2:
                                dve.wait_ge(wt_ready, i * QN + q - 1)
                            chain(nc.vector.reciprocal(s0[:, 3:4], s0[:, 2:3]))
                            chain(nc.vector.reciprocal(s1[:, 3:4], s1[:, 2:3]))
                            chain(TT(s1[:, 3:4], s1[:, 3:4], neg_lam[0:QT, :], ALU.mult))
                            chain(TS(b0[:, 0:n], b0[:, 0:n], s0[:, 3:4], None, ALU.mult))
                            nc.vector.scalar_tensor_tensor(out=wt[q % 2][:, 0:n], in0=b1[:, 0:n], scalar=s1[:, 3:4], in1=b0[:, 0:n],
                                                           op0=ALU.mult, op1=ALU.add).then_inc(w_ready, 1)
                    chain.close()


T2 = 512
NC2 = (T2 - 32) // 16 + 1
TN = T2 // P
CONV_TAPS = 31


def conv_inputs(nc, c, u, glu, taps):
    PAD = CONV_TAPS - 1
    with stage(nc) as s:
        loaded, sig_ready = s.sem("loaded"), s.sem("sig_ready")
        with nc.Block() as block:
            @block.sync
            def _(sp):
                sp.dma_start(taps[:], c["conv_taps"]).then_inc(loaded, 16)
                sp.wait_ge(loaded, 16)

            @block.scalar
            def _(act):
                for i in range(4):
                    nc.scalar.activation(u[:, 4 + i, :], u[:, 4 + i, :], ACT.Sigmoid).then_inc(sig_ready, 1)

            @block.vector
            def _(dve):
                nc.vector.memset(glu[:, :, 0:PAD], 0.0)
                for i in range(4):
                    dve.wait_ge(sig_ready, i + 1)
                    nc.vector.tensor_tensor(glu[:, i, PAD:PAD + T2], u[:, i, :], u[:, 4 + i, :], ALU.mult)


def conv_steps(nc, glu, taps, a, steps):
    per_step = -(-CONV_TAPS // steps)

    def side(dve, order, it, u):
        def column(j):
            return taps[:, bass.ds(it, 1), j:j + 1].rearrange("p a b -> p (a b)")
        for j in range(per_step * u, min(per_step * (u + 1), CONV_TAPS)):
            out, shifted = a[:, it, :], glu[:, it, j:j + T2]
            if j == 0:
                nc.vector.tensor_scalar(out, shifted, column(0), column(CONV_TAPS), ALU.mult, ALU.add).then_inc(order, 1)
            else:
                dve.wait_ge(order, it * CONV_TAPS + j)
                nc.vector.scalar_tensor_tensor(out=out, in0=shifted, scalar=column(j), in1=out, op0=ALU.mult, op1=ALU.add).then_inc(order, 1)
    return side


def conv_norm(nc, c, taps, a):
    with stage(nc) as s:
        sq, mean, rstd = s.sb("sq", [P, 4, T2]), s.sb("mean", [P, T2]), s.sb("rstd", [P, T2])
        ps_m, ps_v = s.ps("ps_m", [P, BANK]), s.ps("ps_v", [P, BANK])
        mean_ready, cen_ready, sq_ready, var_ready, eps_ready, root_ready, norm_ready, order = (
            s.sem(n) for n in ("mean_ready", "cen_ready", "sq_ready", "var_ready", "eps_ready", "root_ready", "norm_ready", "order"))
        with nc.Block() as block:
            @block.scalar
            def _(act):
                for i in range(4):
                    act.wait_ge(cen_ready, i + 1)
                    nc.scalar.activation(sq[:, i, :], a[:, i, :], ACT.Square).then_inc(sq_ready, 1)
                act.wait_ge(eps_ready, 1)
                nc.scalar.activation(rstd[:], rstd[:], ACT.Sqrt).then_inc(root_ready, 1)
                for i in range(4):
                    act.wait_ge(norm_ready, i + 1)
                    nc.scalar.activation(a[:, i, :], a[:, i, :], ACT.Silu, scale=taps[:, i, CONV_TAPS + 1:CONV_TAPS + 2],
                                         bias=taps[:, i, CONV_TAPS + 2:CONV_TAPS + 3])

            @block.tensor
            def _(pe):
                for i in range(4):
                    mm = nc.tensor.matmul(ps_m[:], c["ones"][:], a[:, i, :], start=(i == 0), stop=(i == 3))
                mm.then_inc(mean_ready, 1)
                for i in range(4):
                    pe.wait_ge(sq_ready, i + 1)
                    mm = nc.tensor.matmul(ps_v[:], c["ones"][:], sq[:, i, :], start=(i == 0), stop=(i == 3))
                mm.then_inc(var_ready, 1)

            @block.vector
            def _(dve):
                TT, TS = nc.vector.tensor_tensor, nc.vector.tensor_scalar
                chain = Chain(dve, order)
                dve.wait_ge(mean_ready, 1)
                chain(TS(mean[:], ps_m[:], 1.0 / 512, None, ALU.mult))
                for i in range(4):
                    TT(a[:, i, :], a[:, i, :], mean[:], ALU.subtract).then_inc(cen_ready, 1)
                dve.wait_ge(var_ready, 1)
                TS(rstd[:], ps_v[:], 1.0 / 512, 1e-6, ALU.mult, ALU.add).then_inc(eps_ready, 1)
                dve.wait_ge(root_ready, 1)
                chain(nc.vector.reciprocal(rstd[:], rstd[:]))
                for i in range(4):
                    TT(a[:, i, :], a[:, i, :], rstd[:], ALU.mult).then_inc(norm_ready, 1)


def bias_tables(nc, c, bias_scr, bias_rows, bias_cmp):
    W = bias_scr.shape[1]
    NB = bias_cmp.shape[1]
    with stage(nc) as s:
        rb = s.sb("rb", [33, 8])
        rev = s.sb("rev", [33, W])
        fwd = s.sb("fwd", [33, c["buckets_fwd"].shape[1]])
        row = s.sb("row", [8, 2, W // 2])
        ps_r, ps_c = s.ps("ps_r", [P, 2, BANK]), s.ps("ps_c", [P, BANK])
        down, up = s.sb("down", [P, 8, T2]), s.sb("up", [P, 8, T2])
        ps_u = [s.ps("ps_u", [P, BANK]) for _ in range(2)]
        filled, loaded, prod, out, stored, cmp_done, rows_in, turn_ready, turned = (
            s.sem(n) for n in ("filled", "loaded", "prod", "out", "stored", "cmp_done", "rows_in", "turn_ready", "turned"))
        with nc.Block() as block:
            @block.sync
            def _(sp):
                sp.dma_start(rb[0:32, :], c["rel_bias"]).then_inc(loaded, 16)
                sp.dma_start(rev[:], c["buckets_rev"]).then_inc(loaded, 16)
                sp.dma_start(fwd[:], c["buckets_fwd"]).then_inc(loaded, 16)
                sp.wait_ge(out, 1)
                sp.dma_start(bias_scr.rearrange("h (a w) -> h a w", a=2), row[:]).then_inc(stored, 16)
                sp.wait_ge(stored, 16)
                for h in range(8):
                    src = bass.AP(tensor=bias_scr.tensor, offset=bias_scr.offset + h * W, ap=[[1, P], [1, T2]])
                    sp.dma_start(down[:, h, :], src).then_inc(rows_in, 16)
                for h in range(8):
                    sp.wait_ge(turned, h + 1)
                    sp.dma_start(bias_rows[h], up[:, h, :]).then_inc(stored, 16)
                sp.wait_ge(stored, 16 * 9)

            @block.vector
            def _(dve):
                nc.vector.memset(rb[32:33, :], NEG).then_inc(filled, 1)
                dve.wait_ge(prod, 1)
                nc.vector.tensor_copy(row[:], ps_r[0:8, :, 0:W // 2]).then_inc(out, 1)
                dve.wait_ge(prod, 2)
                nc.vector.tensor_copy(bias_cmp[:].rearrange("p m h -> p (m h)"), ps_c[:, 0:NB * 8]).then_inc(cmp_done, 1)
                for h in range(8):
                    dve.wait_ge(turn_ready, h + 1)
                    nc.vector.tensor_copy(up[:, h, :], ps_u[h % 2][:]).then_inc(turned, 1)

            @block.tensor
            def _(pe):
                pe.wait_ge(loaded, 48)
                pe.wait_ge(filled, 1)
                for h in range(2):
                    mm = nc.tensor.matmul(ps_r[0:8, h, 0:W // 2], rb[:], rev[:, h * W // 2:(h + 1) * W // 2], start=True, stop=True)
                mm.then_inc(prod, 1)
                for m in range(NB):
                    z = 353 - 16 * m + 511
                    mm = nc.tensor.matmul(ps_c[:, m * 8:(m + 1) * 8], fwd[:, z:z + P], rb[:], start=True, stop=True)
                mm.then_inc(prod, 1)
                pe.wait_ge(rows_in, 16 * 8)
                for h in range(8):
                    pe.wait_ge(turned, max(h - 1, 0))
                    nc.tensor.matmul(ps_u[h % 2][:], c["upside_down"][:], down[:, h, :], start=True, stop=True).then_inc(turn_ready, 1)


def compress(nc, weights, ident, kv, k_cmp, v_cmp):
    M = 2 * NC2
    with stage(nc) as s:
        win = [s.sb("win", [P, 32, M]) for _ in range(2)]
        pe_in, w1, w2 = weights["cmp_pe"], weights["cmp_w1"], weights["cmp_w2"]
        act_out = [s.sb("act_out", [M, 256]) for _ in range(2)]
        hid = s.sb("hid", [P, 4, M])
        ps_h = [s.ps("ps_h", [P, BANK]) for _ in range(2)]
        ps_t, ps_k, ps_v = s.ps("ps_t", [P, BANK]), s.ps("ps_k", [P, BANK]), s.ps("ps_v", [P, BANK])
        cleared, win_ready, hid_ready, gelu_ready, tr_ready, tr_copied, out_ready, copied = (s.sem(n) for n in (
            "cleared", "win_ready", "hid_ready", "gelu_ready", "tr_ready", "tr_copied", "out_ready", "copied"))
        with nc.Block() as block:
            @block.vector
            def _(dve):
                for b in range(2):
                    nc.vector.memset(win[b][:], 0.0).then_inc(cleared, 1)
                for b in range(2):
                    dve.wait_ge(cleared, b + 1)
                    for g in range(2):
                        rows = slice(64 * g, 64 * g + 64)
                        for half in range(2):
                            places = slice(16 * half, 16 * half + 16)
                            v = kv[rows, b, 16 * half:16 * half + 16 * NC2].rearrange("p (c l) -> p l c", l=16)
                            r = nc.vector.tensor_tensor(win[b][rows, places, g * NC2:(g + 1) * NC2], v, pe_in[b][rows, places, :], ALU.add)
                    r.then_inc(win_ready, 1)

            @block.tensor
            def _(pe):
                for b in range(2):
                    pe.wait_ge(win_ready, b + 1)
                    for l in range(32):
                        mm = nc.tensor.matmul(ps_h[b][0:M, 0:256], win[b][:, l, :], w1[b][:, l, :], start=(l == 0), stop=(l == 31))
                    mm.then_inc(hid_ready, 1)
                for b in range(2):
                    pe.wait_ge(gelu_ready, b + 1)
                    for h in range(2):
                        mm = nc.tensor.transpose(ps_t[:, (2 * b + h) * M:(2 * b + h + 1) * M], act_out[b][:, h * P:(h + 1) * P], ident[0:M, 0:M])
                mm.then_inc(tr_ready, 1)
                pe.wait_ge(tr_copied, 1)
                for g in range(2):
                    cols = slice(g * NC2, (g + 1) * NC2)
                    for h in range(2):
                        nc.tensor.matmul(ps_k[64 * g:64 * g + 64, 0:NC2], w2[0][:, h, :], hid[:, h, cols], start=(h == 0), stop=(h == 1))
                for g in range(2):
                    cols = slice(g * NC2, (g + 1) * NC2)
                    for h in range(2):
                        mm = nc.tensor.matmul(ps_v[0:NC2, 64 * g:64 * g + 64], hid[:, 2 + h, cols], w2[1][:, h, :], start=(h == 0), stop=(h == 1))
                mm.then_inc(out_ready, 1)

            @block.scalar
            def _(act):
                for b in range(2):
                    act.wait_ge(hid_ready, b + 1)
                    nc.scalar.activation(act_out[b][:], ps_h[b][0:M, 0:256], ACT.Gelu_apprx_tanh).then_inc(gelu_ready, 1)
                act.wait_ge(tr_ready, 1)
                nc.scalar.activation(hid[:].rearrange("p a m -> p (a m)"), ps_t[:, 0:4 * M], ACT.Copy).then_inc(tr_copied, 1)
                act.wait_ge(out_ready, 1)
                nc.scalar.activation(k_cmp[:], ps_k[:, 0:NC2], ACT.Copy)
                nc.scalar.activation(v_cmp[:], ps_v[0:NC2, 0:P], ACT.Copy).then_inc(copied, 1)


def nsa_attention(nc, c, q, kv, ng, bias_rows, bias_cmp, k_cmp, v_cmp, o):
    assert T2 // 64 <= 16 and T2 <= 512
    NU = TN * 2 * 3
    units = [(qi, e, br) for qi in range(TN) for e in range(2) for br in range(3)]
    with stage(nc) as s:
        sig = s.sb("sig", [P, T2])
        gate = s.sb("gate", [P, TN, 32])
        gs = s.sb("gs", [P, TN, 6])
        vt = s.sb("vt", [P, 2, TN, P])
        qs = s.sb("qs", [P, T2])
        bias = s.sb("bias", [P, 2, T2])
        bc = s.sb("bc", [P, 2, bias_cmp.shape[1]])
        pr = [s.sb("pr", [P, T2]) for _ in range(4)]
        wn = [s.sb("wn", [P, T2]) for _ in range(4)]
        wT = [s.sb("wT", [P, TN, P]) for _ in range(3)]
        small = [s.sb("small", [P, 4]) for _ in range(4)]
        ps_s = [s.ps("ps_s", [P, BANK]) for _ in range(3)]
        ps_t = [s.ps("ps_t", [P, BANK]) for _ in range(2)]
        ps_o = [s.ps("ps_o", [P, BANK]) for _ in range(2)]
        sig_ready, vt_ready, vt_copied, bias_in, head_ready = (s.sem(n) for n in ("sig_ready", "vt_ready", "vt_copied", "bias_in", "head_ready"))
        sc_ready, max_ready, exp_ready, r_ready, w_ready, wt_ready, wt_copied, pv_ready, o_copied, order = (
            s.sem(n) for n in ("sc_ready", "max_ready", "exp_ready", "r_ready", "w_ready", "wt_ready", "wt_copied", "pv_ready", "o_copied", "order"))

        def keys(u):
            return NC2 if units[u][2] == 2 else P * (units[u][0] + 1)

        with nc.Block() as block:
            @block.sync
            def _(sp):
                with sp.Fori(0, 4) as i:
                    sp.wait_ge(max_ready, i * NU)
                    for e in range(2):
                        sp.dma_start(bias[:, e, :], bias_rows[i + 4 * e]).then_inc(bias_in, 16)

            @block.tensor
            def _(pe):
                pe.wait_ge(sig_ready, 1)
                for j in range(TN):
                    nc.tensor.transpose(ps_s[0][:, j * P:(j + 1) * P], sig[:, j * P:(j + 1) * P], c["ident"][:])
                for b in range(2):
                    for j in range(TN):
                        mm = nc.tensor.transpose(ps_t[b][:, j * P:(j + 1) * P], kv[:, 3 + 2 * b, j * P:(j + 1) * P], c["ident"][:])
                mm.then_inc(vt_ready, 1)
                pe.wait_ge(vt_copied, 1)
                with pe.Fori(0, 4) as i:
                    pe.wait_ge(head_ready, i + 1)
                    for step in range(NU + 4):
                        if step < NU:
                            qi, e, br = units[step]
                            rows = slice(64 * e, 64 * e + 64)
                            pe.wait_ge(max_ready, i * NU + max(step - 2, 0))
                            k = k_cmp[rows, :] if br == 2 else kv[rows, 2 + 2 * br, 0:P * (qi + 1)]
                            nc.tensor.matmul(ps_s[step % 3][:, 0:keys(step)], qs[rows, qi * P:(qi + 1) * P], k,
                                             start=True, stop=True).then_inc(sc_ready, 1)
                        u = step - 3
                        if 0 <= u < NU:
                            n = keys(u)
                            pe.wait_ge(w_ready, i * NU + u + 1)
                            pe.wait_ge(wt_copied, i * NU + max(u - 1, 0))
                            if units[u][2] == 2:
                                mm = nc.tensor.transpose(ps_t[u % 2][0:NC2, 0:P], wn[u % 4][:, 0:NC2], c["ident"][:])
                            else:
                                for j in range(n // P):
                                    mm = nc.tensor.transpose(ps_t[u % 2][:, j * P:(j + 1) * P], wn[u % 4][:, j * P:(j + 1) * P], c["ident"][:])
                            mm.then_inc(wt_ready, 1)
                        u = step - 4
                        if 0 <= u < NU:
                            qi, e, br = units[u]
                            rows = slice(64 * e, 64 * e + 64)
                            pe.wait_ge(wt_copied, i * NU + u + 1)
                            if br == 0:
                                pe.wait_ge(o_copied, i * 2 * TN + max(2 * (qi - 1) + e + 1, 0))
                            if br == 2:
                                mm = nc.tensor.matmul(ps_o[e][rows, 0:P], v_cmp[:, rows], wT[u % 3][0:NC2, 0, :], start=False, stop=True)
                            else:
                                for j in range(qi + 1):
                                    mm = nc.tensor.matmul(ps_o[e][rows, 0:P], vt[:, br, j, rows], wT[u % 3][:, j, :],
                                                          start=(br == 0 and j == 0), stop=False)
                            mm.then_inc(pv_ready, 1)

            @block.scalar
            def _(act):
                nc.scalar.activation(sig[:], ng, ACT.Sigmoid).then_inc(sig_ready, 1)
                act.wait_ge(vt_ready, 1)
                nc.scalar.activation(gate[:], ps_s[0][:].rearrange("p (j t) -> p j t", j=TN)[:, :, 0:32], ACT.Copy)
                for b in range(2):
                    cp = nc.scalar.activation(vt[:, b, :, :].rearrange("p j d -> p (j d)"), ps_t[b][:], ACT.Copy)
                cp.then_inc(vt_copied, 1)
                with act.Fori(0, 4) as i:
                    for step in range(NU + 4):
                        if step < NU:
                            sm, b = small[step % 4], pr[step % 4][:, 0:keys(step)]
                            act.wait_ge(max_ready, i * NU + step + 1)
                            nc.scalar.activation(b, b, ACT.Exp, bias=sm[:, 1:2], accum_out=sm[:, 2:3]).then_inc(exp_ready, 1)
                        u = step - 3
                        if 0 <= u < NU:
                            act.wait_ge(wt_ready, i * NU + u + 1)
                            act.wait_ge(pv_ready, i * NU + max(u - 2, 0))
                            n = keys(u)
                            if units[u][2] == 2:
                                cp = nc.scalar.activation(wT[u % 3][0:NC2, 0, :], ps_t[u % 2][0:NC2, 0:P], ACT.Copy)
                            else:
                                cp = nc.scalar.activation(wT[u % 3][:].rearrange("p j t -> p (j t)")[:, 0:n], ps_t[u % 2][:, 0:n], ACT.Copy)
                            cp.then_inc(wt_copied, 1)
                        u = step - 4
                        if 0 <= u < NU and units[u][2] == 2:
                            qi, e, br = units[u]
                            rows = slice(64 * e, 64 * e + 64)
                            act.wait_ge(pv_ready, i * NU + u + 1)
                            nc.scalar.activation(o[rows, i, qi * P:(qi + 1) * P], ps_o[e][rows, 0:P], ACT.Copy).then_inc(o_copied, 1)

            @block.gpsimd
            def _(pool):
                with pool.Fori(0, 4) as i:
                    for u in range(NU):
                        pool.wait_ge(r_ready, i * NU + u + 1)
                        pool.wait_ge(wt_ready, i * NU + max(u - 3, 0))
                        nc.gpsimd.tensor_tensor(wn[u % 4][:, 0:keys(u)], pr[u % 4][:, 0:keys(u)],
                                                small[u % 4][:, 3:4].broadcast_to([P, keys(u)]), ALU.mult).then_inc(w_ready, 1)

            @block.vector
            def _(dve):
                TT, TS = nc.vector.tensor_tensor, nc.vector.tensor_scalar
                dve.wait_ge(vt_copied, 1)
                with dve.Fori(0, 4) as i:
                    chain = Chain(dve, order, i, 3 + NU * 2 + 2)
                    dve.wait_ge(sc_ready, i * NU)
                    dve.wait_ge(w_ready, i * NU)
                    chain(TS(qs[:], q[:, i, :], 0.125, None, ALU.mult))
                    chain(nc.vector.tensor_copy(gs[:], gate[:, :, bass.ds(6 * i, 6)]))
                    chain(nc.vector.tensor_copy(bc[:, 0, :], bias_cmp[:, :, bass.ds(i, 1)].rearrange("p m h -> p (m h)")))
                    nc.vector.tensor_copy(bc[:, 1, :], bias_cmp[:, :, bass.ds(i + 4, 1)].rearrange("p m h -> p (m h)")).then_inc(head_ready, 1)
                    dve.wait_ge(head_ready, i + 1)
                    dve.wait_ge(bias_in, i * 32 + 32)
                    for step in range(NU + 1):
                        if step < NU:
                            qi, e, br = units[step]
                            sm, n = small[step % 4], keys(step)
                            count = dve.compute_val(i * NU + step + 1)
                            count_2 = dve.compute_val(i * NU + max(step - 3, 0))
                            settle(dve, vt_copied)
                            dve.wait_ge(sc_ready, count)
                            dve.wait_ge(w_ready, count_2)
                            b = bc[:, e, 24 - 8 * qi:24 - 8 * qi + NC2] if br == 2 else bias[:, e, T2 - n:T2]
                            chain(nc.vector.tensor_tensor_reduce(out=pr[step % 4][:, 0:n], in0=ps_s[step % 3][:, 0:n], in1=b, scale=1.0,
                                                                 scalar=3 * NEG, op0=ALU.add, op1=ALU.max, accum_out=sm[:, 0:1]))
                            TS(sm[:, 1:2], sm[:, 0:1], -1.0, None, ALU.mult).then_inc(max_ready, 1)
                        u = step - 1
                        if 0 <= u < NU:
                            qi, e, br = units[u]
                            sm = small[u % 4]
                            dve.wait_ge(exp_ready, i * NU + u + 1)
                            chain(nc.vector.reciprocal(sm[:, 3:4], sm[:, 2:3]))
                            g = gs[:, qi, 3 * e + (1, 2, 0)[br]:3 * e + (1, 2, 0)[br] + 1]
                            if br == 2 and qi == 0:
                                chain(TT(sm[:, 3:4], sm[:, 3:4], c["row_valid"][:], ALU.mult))
                            TT(sm[:, 3:4], sm[:, 3:4], g, ALU.mult).then_inc(r_ready, 1)
                    chain.close()


def ffn_up(nc, c, w, h, dst):
    N = w.shape[0]
    U, A = 4, 3
    rounds, last = N // 2, N // 2 - 1
    hhi, hlo = h
    with stage(nc) as s:
        taps = s.sb("taps", [P, 2 * N, 4])
        wbuf = [s.sb("wbuf", [P, 8, P]) for _ in range(U)]
        whi, wlo = ([s.sb(n, [P, 8, P], F32R) for _ in range(U)] for n in ("whi", "wlo"))
        acc = [s.ps("acc", [P, BANK]) for _ in range(U)]
        raw = [s.sb("raw", [P, 2 + T2]) for _ in range(U)]
        cv = [s.sb("cv", [P, T2]) for _ in range(U)]
        w_loaded = [s.sem("w_loaded") for _ in range(U)]
        hi_ready, lo_ready, w_used, acc_free = (s.sem(n) for n in ("hi_ready", "lo_ready", "w_used", "acc_free"))
        loaded, padded, conv_ready, gelu_ready, order = (s.sem(n) for n in ("loaded", "padded", "conv_ready", "gelu_ready", "order"))

        def run(eng, body):
            body(0)
            with eng.Fori(1, last) as it:
                body(it)
            body(last)

        def is_round(it, n):
            return isinstance(it, int) and it == n

        with nc.Block() as block:
            @block.sync
            def _(sp):
                sp.dma_start(taps[:], c["ffn_taps"]).then_inc(loaded, 16)
                for b in range(U):
                    sp.dma_start(wbuf[b][:], w[b // 2, b % 2]).then_inc(w_loaded[b], 16)

                def body(it):
                    for b in range(U):
                        sp.wait_ge(lo_ready, it * U + (b + 1))
                        sp.dma_start(wbuf[b][:], w[it * 2 + (2 + b // 2), b % 2]).then_inc(w_loaded[b], 16)
                body(0)
                with sp.Fori(1, last) as it:
                    body(it)

            @block.tensor
            def _(pe):
                def body(it):
                    for b in range(U):
                        if not is_round(it, 0):
                            pe.wait_ge(acc_free, it * U + (b + 1 - U))
                        pe.wait_ge(lo_ready, it * U + (b + 1))
                        for k in range(8):
                            for i, (wt, xt) in enumerate(((whi, hhi), (whi, hlo), (wlo, hhi))):
                                mm = nc.tensor.matmul(acc[b][:], wt[b][:, k, :], xt[:, k, :], start=(k == 0 and i == 0), stop=(k == 7 and i == 2))
                        mm.then_inc(w_used, 1)
                run(pe, body)

            @block.scalar
            def _(act):
                def hi_part(it, u):
                    act.wait_ge(w_loaded[u % U], (it + (u // U + 1)) * 16)
                    nc.scalar.activation(whi[u % U][:], wbuf[u % U][:], ACT.Copy).then_inc(hi_ready, 1)

                for u in range(A):
                    hi_part(0, u)
                act.wait_ge(padded, 1)

                def body(it):
                    for b in range(U):
                        if not is_round(it, last) or b + A < U:
                            if not (is_round(it, 0) and b == 0):
                                act.wait_ge(w_used, it * U + b)
                            hi_part(it, b + A)
                        act.wait_ge(w_used, it * U + (b + 1))
                        if not is_round(it, 0):
                            act.wait_ge(conv_ready, it * U + (b + 1 - U))
                        nc.scalar.activation(raw[b][:, 2:2 + T2], acc[b][:], ACT.Copy).then_inc(acc_free, 1)
                    for g in range(2):
                        act.wait_ge(conv_ready, it * U + (2 * g + 1))
                        nc.scalar.activation(cv[2 * g][:], cv[2 * g][:], ACT.Gelu_apprx_tanh).then_inc(gelu_ready, 1)
                run(act, body)

            @block.vector
            def _(dve):
                TT, TS, STT = nc.vector.tensor_tensor, nc.vector.tensor_scalar, nc.vector.scalar_tensor_tensor
                for b in range(U):
                    ms = nc.vector.memset(raw[b][:, 0:2], 0.0)
                ms.then_inc(padded, 1)

                def lo_part(it, u):
                    dve.wait_ge(hi_ready, it * U + (u + 1))
                    TT(wlo[u % U][:], wbuf[u % U][:], whi[u % U][:].bitcast(F32), ALU.subtract).then_inc(lo_ready, 1)

                for u in range(A):
                    lo_part(0, u)
                dve.wait_ge(padded, 1)
                dve.wait_ge(loaded, 16)

                def body(it):
                    chain = Chain(dve, order, it, 2 * U + 6)
                    for b in range(U):
                        if not is_round(it, last) or b + A < U:
                            lo_part(it, b + A)
                        dve.wait_ge(acc_free, it * U + (b + 1))
                        n = it * 2 + (b // 2 + N * (b % 2))

                        def tap(j):
                            return taps[:, bass.ds(n, 1), j:j + 1].rearrange("p a b -> p (a b)")
                        chain(TS(cv[b][:], raw[b][:, 2:2 + T2], tap(2), tap(3), ALU.mult, ALU.add))
                        chain(STT(out=cv[b][:], in0=raw[b][:, 1:1 + T2], scalar=tap(1), in1=cv[b][:], op0=ALU.mult, op1=ALU.add))
                        STT(out=cv[b][:], in0=raw[b][:, 0:T2], scalar=tap(0), in1=cv[b][:], op0=ALU.mult, op1=ALU.add).then_inc(conv_ready, 1)
                    for g in range(2):
                        dve.wait_ge(gelu_ready, it * 2 + (g + 1))
                        dve.wait_ge(conv_ready, it * U + (2 * g + 2))
                        n = it * 2 + g
                        chain(TT(cv[2 * g][:], cv[2 * g][:], cv[2 * g + 1][:], ALU.mult))
                        chain(nc.vector.tensor_copy(dst[0][:, n, :], cv[2 * g][:]))
                        chain(TT(dst[1][:, n, :], cv[2 * g][:], dst[0][:, n, :].bitcast(F32), ALU.subtract))
                    chain.close()
                run(dve, body)


GC = 16
GN = T2 // GC
DC = 64
DN = T2 // DC
LEVELS3 = 6
K_SCALE = 128 ** -0.5


def gate_rows(nc, c, small, rows):
    with stage(nc) as s:
        raw = s.sb("raw", [4, 4, T2])
        b = s.sb("b", [4, 4])
        ax, lin, fwd = s.sb("ax", [4, 2, T2]), s.sb("lin", [4, 2, T2]), s.sb("cum", [4, T2])
        ea, end = s.sb("ea", [4, 1]), s.sb("end", [4, T2])
        loaded, x_ready, ln_ready, order, bd_ready, exp_done, end_ready = (
            s.sem(n) for n in ("loaded", "x_ready", "ln_ready", "order", "bd_ready", "exp_done", "end_ready"))
        with nc.Block() as block:
            @block.sync
            def _(sp):
                sp.dma_start(b[:], c["gate_bias"]).then_inc(loaded, 16)
                for j in range(4):
                    sp.dma_start(raw[:, j, :], small[32 * j:32 * j + 4, :]).then_inc(loaded, 16)

            @block.scalar
            def _(act):
                act.wait_ge(x_ready, 2)
                nc.scalar.activation(ax[:], lin[:], ACT.Abs).then_inc(ln_ready, 1)
                act.wait_ge(ln_ready, 1)
                nc.scalar.activation(ax[:], ax[:], ACT.Exp, scale=-1.0).then_inc(ln_ready, 1)
                act.wait_ge(ln_ready, 2)
                nc.scalar.activation(ax[:], ax[:], ACT.Ln, bias=1.0)
                nc.scalar.activation(ea[:], b[:, 3:4], ACT.Exp)
                nc.scalar.activation(rows[:, 5, :], raw[:, 2, :], ACT.Sigmoid).then_inc(ln_ready, 1)
                act.wait_ge(bd_ready, 1)
                nc.scalar.activation(rows[:, 4, :], rows[:, 3, :], ACT.Exp).then_inc(exp_done, 1)
                act.wait_ge(end_ready, 1)
                nc.scalar.activation(rows[:, 7, :], end[:], ACT.Exp)

            @block.vector
            def _(dve):
                TT, TS, STT = nc.vector.tensor_tensor, nc.vector.tensor_scalar, nc.vector.scalar_tensor_tensor
                chain = Chain(dve, order)
                dve.wait_ge(loaded, 80)
                TS(lin[:, 0, :], raw[:, 1, :], b[:, 1:2], None, ALU.add).then_inc(x_ready, 1)
                TS(lin[:, 1, :], raw[:, 3, :], b[:, 2:3], None, ALU.add).then_inc(x_ready, 1)
                dve.wait_ge(x_ready, 2)
                dve.wait_ge(ln_ready, 3)
                chain(STT(out=lin[:, 0, :], in0=lin[:, 0, :], scalar=0.0, in1=ax[:, 0, :], op0=ALU.min, op1=ALU.subtract))
                chain(STT(out=lin[:, 1, :], in0=lin[:, 1, :], scalar=0.0, in1=ax[:, 1, :], op0=ALU.max, op1=ALU.add))
                chain(nc.vector.tensor_tensor_scan(fwd[:], c["ones"][0:4, 0:1].broadcast_to([4, T2]), lin[:, 0, :], 0.0, ALU.mult, ALU.add))
                chain(STT(out=rows[:, 0, :], in0=raw[:, 0, :], scalar=b[:, 0:1], in1=fwd[:], op0=ALU.add, op1=ALU.subtract))
                chain(nc.vector.tensor_tensor_scan(rows[:, 1, :], rows[:, 0, :], rows[:, 0, :], 0.0, ALU.max, ALU.max))
                chain(STT(out=rows[:, 2, :], in0=fwd[:], scalar=-1.0, in1=rows[:, 1, :], op0=ALU.mult, op1=ALU.subtract))
                chain(TS(lin[:, 1, :], lin[:, 1, :], ea[:, 0:1], -1.0, ALU.mult, ALU.mult))
                nc.vector.tensor_tensor_scan(rows[:, 3, :], c["chunk_start64"][0:4, :], lin[:, 1, :], 0.0, ALU.mult, ALU.add).then_inc(bd_ready, 1)
                dve.wait_ge(bd_ready, 1)
                bd = rows[:, 3, :].rearrange("p (n t) -> p n t", t=DC)
                TT(end[:].rearrange("p (n t) -> p n t", t=DC), bd[:, :, DC - 1:DC].broadcast_to([4, DN, DC]), bd, ALU.subtract).then_inc(end_ready, 1)
                dve.wait_ge(exp_done, 1)
                STT(out=rows[:, 6, :], in0=rows[:, 4, :], scalar=-1.0, in1=rows[:, 5, :], op0=ALU.mult, op1=ALU.mult)


def mlstm(nc, c, z, rows, o):
    with stage(nc) as s:
        gcol = s.sb("gcol", [P, TN, 4])
        sel = s.sb("sel", [4, P])
        kv = s.sb("kv", [P, 2, T2])
        qs, sig = s.sb("qs", [P, T2]), s.sb("sig", [P, T2])
        vt = s.sb("vt", [P, TN, P])
        mb, em = s.sb("mb", [P, T2]), s.sb("em", [P, T2])
        ex = [s.sb("ex", [P, T2]) for _ in range(2)]
        pt = [s.sb("pt", [P, T2]) for _ in range(2)]
        den = s.sb("den", [P, T2])
        k_scale, scale_set = s.sb("k_scale", [P, 1]), s.sem("scale_set")
        ps_b, ps_e, ps_v, ps_o, ps_d = (s.ps(n, [P, BANK]) for n in ("ps_b", "ps_e", "ps_v", "ps_o", "ps_d"))
        ps_k = [s.ps("ps_k", [P, BANK]) for _ in range(2)]
        (col_ready, col_copied, fixed, bc_ready, vt_ready, vt_copied, mb_ready, em_ready, kq_ready, arg_ready, ex_ready,
         pt_ready, o_ready, done, order) = (s.sem(n) for n in (
             "col_ready", "col_copied", "fixed", "bc_ready", "vt_ready", "vt_copied", "mb_ready", "em_ready", "kq_ready", "arg_ready",
             "ex_ready", "pt_ready", "o_ready", "done", "order"))
        with nc.Block() as block:
            @block.tensor
            def _(pe):
                for j in range(TN):
                    mm = nc.tensor.transpose(ps_b[:, 4 * j:4 * j + 4], rows[:, 0, j * P:(j + 1) * P], c["ident"][0:4, 0:4])
                mm.then_inc(col_ready, 1)
                pe.wait_ge(col_copied, 1)
                with pe.Fori(0, 4) as h:
                    pe.wait_ge(fixed, h + 1)
                    pe.wait_ge(done, h)
                    nc.tensor.matmul(ps_b[:], sel[:], rows[:, 1, :], start=True, stop=True)
                    nc.tensor.matmul(ps_e[:], sel[:], rows[:, 2, :], start=True, stop=True).then_inc(bc_ready, 1)
                    for j in range(TN):
                        mm = nc.tensor.transpose(ps_v[:, j * P:(j + 1) * P], kv[:, 1, j * P:(j + 1) * P], c["ident"][:])
                    mm.then_inc(vt_ready, 1)
                    for j in range(TN + 1):
                        if j < TN:
                            n = T2 - j * P
                            pe.wait_ge(pt_ready, h * TN + max(j - 1, 0))
                            nc.tensor.matmul(ps_k[j % 2][:, 0:n], kv[:, 0, j * P:(j + 1) * P], qs[:, j * P:T2],
                                             start=True, stop=True).then_inc(kq_ready, 1)
                        if j > 0:
                            i = j - 1
                            n = T2 - i * P
                            if i == 0:
                                pe.wait_ge(vt_copied, h + 1)
                            pe.wait_ge(pt_ready, h * TN + i + 1)
                            nc.tensor.matmul(ps_o[:, i * P:T2], vt[:, i, :], pt[i % 2][:, 0:n], start=(i == 0), stop=(i == TN - 1))
                            nc.tensor.matmul(ps_d[:, i * P:T2], c["ones"][:], pt[i % 2][:, 0:n], start=(i == 0),
                                             stop=(i == TN - 1)).then_inc(o_ready, 1)

            @block.gpsimd
            def _(pool):
                nc.gpsimd.memset(k_scale[:], K_SCALE).then_inc(scale_set, 1)
                pool.wait_ge(scale_set, 1)
                with pool.Fori(0, 4) as h:
                    pool.wait_ge(o_ready, h * TN)
                    nc.gpsimd.tensor_copy(kv[:, 0, :], z[:, h + 4, :])
                    nc.gpsimd.tensor_copy(kv[:, 1, :], z[:, h + 8, :])
                    nc.gpsimd.tensor_copy(sel[:], c["head_sel"][:, h, :])
                    nc.gpsimd.tensor_tensor(qs[:], z[:, h, :], k_scale[:].broadcast_to([P, T2]), ALU.mult).then_inc(fixed, 1)

            @block.scalar
            def _(act):
                act.wait_ge(col_ready, 1)
                nc.scalar.activation(gcol[:].rearrange("p j h -> p (j h)"), ps_b[:, 0:4 * TN], ACT.Copy).then_inc(col_copied, 1)
                act.wait_ge(col_copied, 1)
                with act.Fori(0, 4) as h:
                    act.wait_ge(bc_ready, h + 1)
                    act.wait_ge(done, h)
                    nc.scalar.activation(em[:], ps_e[:], ACT.Exp).then_inc(em_ready, 1)
                    act.wait_ge(vt_ready, h + 1)
                    nc.scalar.activation(vt[:].rearrange("p j d -> p (j d)"), ps_v[:], ACT.Copy).then_inc(vt_copied, 1)
                    for j in range(TN):
                        n = T2 - j * P
                        act.wait_ge(arg_ready, h * TN + j + 1)
                        nc.scalar.activation(ex[j % 2][:, 0:n], ex[j % 2][:, 0:n], ACT.Exp, bias=gcol[:, j, bass.ds(h, 1)]).then_inc(ex_ready, 1)
                    nc.scalar.activation(sig[:], z[:, h + 12, :], ACT.Sigmoid).then_inc(ex_ready, 1)

            @block.vector
            def _(dve):
                TT, STT = nc.vector.tensor_tensor, nc.vector.scalar_tensor_tensor
                with dve.Fori(0, 4) as h:
                    chain = Chain(dve, order, h, 5)
                    dve.wait_ge(bc_ready, h + 1)
                    chain(nc.vector.tensor_copy(mb[:], ps_b[:]))
                    for j in range(TN + 1):
                        if j < TN:
                            n = T2 - j * P
                            dve.wait_ge(pt_ready, h * TN + max(j - 1, 0))
                            TT(ex[j % 2][:, 0:n], c["mask_st"][:, 0:n], mb[:, j * P:T2], ALU.subtract).then_inc(arg_ready, 1)
                        if j > 0:
                            i = j - 1
                            n = T2 - i * P
                            dve.wait_ge(ex_ready, h * (TN + 1) + i + 1)
                            dve.wait_ge(kq_ready, h * TN + i + 1)
                            dve.wait_ge(o_ready, h * TN + max(i - 1, 0))
                            TT(pt[i % 2][:, 0:n], ps_k[i % 2][:, 0:n], ex[i % 2][:, 0:n], ALU.mult).then_inc(pt_ready, 1)
                    dve.wait_ge(o_ready, h * TN + TN)
                    dve.wait_ge(em_ready, h + 1)
                    dve.wait_ge(ex_ready, h * (TN + 1) + TN + 1)
                    chain(TT(den[:], ps_d[:], em[:], ALU.max))
                    chain(STT(out=den[:], in0=ps_d[:], scalar=-1.0, in1=den[:], op0=ALU.mult, op1=ALU.max))
                    chain(nc.vector.reciprocal(den[:], den[:]))
                    chain(TT(den[:], den[:], sig[:], ALU.mult))
                    TT(o[:, h, :], ps_o[:], den[:], ALU.mult).then_inc(done, 1)
                    chain.close()


def gla_intra(nc, c, z, lr, o, dec, tok_scr):
    NB = 4 * GN
    with stage(nc) as s:
        wl, bl = s.sb("wl", [16, 512]), s.sb("bl", [P, 4])
        cum = s.sb("cum", [P, 4, T2])
        lin, ax = s.sb("lin", [P, 4, T2]), s.sb("ax", [P, 4, T2])
        kd = s.sb("kd", [P, 4, T2])
        ex = [s.sb("ex", [P, 4, T2]) for _ in range(3)]
        tk = [s.sb("tk", [P, 512]) for _ in range(2)]
        ps = s.ps("ps", [P, 4, BANK])
        ps_w = s.ps("ps_w", [P, 4, BANK])
        (loaded, x_ready, lin_ready, ax_ready, ln_ready, cum_ready, order, e_ready, k_ready, a_ready, p_ready,
         tr_ready, tr_copied, eb_ready, lag_ready, lag_exp, kq_ready, sum_ready, av_ready, added) = (s.sem(n) for n in (
             "loaded", "x_ready", "lin_ready", "ax_ready", "ln_ready", "cum_ready", "order", "e_ready", "k_ready", "a_ready", "p_ready",
             "tr_ready", "tr_copied", "eb_ready", "lag_ready", "lag_exp", "kq_ready", "sum_ready", "av_ready", "added"))

        stored = [s.sem("stored") for _ in range(2)]

        def blocks(ap, lo, hi):
            return ap.rearrange("p h (n t) -> p (h n) t", t=GC)[:, :, lo:hi]

        with nc.Block() as block:
            @block.sync
            def _(sp):
                sp.dma_start(wl[:], c["gla_w"]).then_inc(loaded, 16)
                sp.dma_start(bl[:], c["gla_b"]).then_inc(loaded, 16)
                for j in range(TN):
                    for b in range(2):
                        sp.wait_ge(tr_copied, 2 * j + b + 1)
                        sp.dma_start(tok_scr[j * P:(j + 1) * P, b, :], tk[b][:]).then_inc(stored[b], 16)
                for b in range(2):
                    sp.wait_ge(stored[b], 16 * TN)

            @block.tensor
            def _(pe):
                pe.wait_ge(loaded, 32)
                for i in range(4):
                    mm = nc.tensor.matmul(ps[:, i, :], wl[:, i * P:(i + 1) * P], lr, start=True, stop=True)
                mm.then_inc(x_ready, 1)
                pe.wait_ge(k_ready, 1)
                for j in range(TN):
                    for b, src in ((0, kd[:]), (1, z[:, 8:12, :])):
                        pe.wait_ge(tr_copied, max(2 * j + b - 1, 0))
                        for h in range(4):
                            mm = nc.tensor.transpose(ps_w[:, b, h * P:(h + 1) * P], src[:, h, j * P:(j + 1) * P], c["ident"][:])
                        mm.then_inc(tr_ready, 1)
                for d in range(GC):
                    n = GN * (GC - d)
                    pe.wait_ge(kq_ready, d + 1)
                    pe.wait_ge(av_ready, d)
                    for i in range(4):
                        mm = nc.tensor.matmul(ps[:, i, 0:n], c["ones"][:],
                                              ex[d % 3][:].rearrange("p h t -> p (h t)")[:, i * n:(i + 1) * n], start=True, stop=True)
                    mm.then_inc(sum_ready, 1)

            @block.scalar
            def _(act):
                act.wait_ge(lin_ready, 1)
                nc.scalar.activation(ax[:], lin[:], ACT.Abs).then_inc(ax_ready, 1)
                act.wait_ge(ax_ready, 1)
                nc.scalar.activation(ax[:], ax[:], ACT.Exp, scale=-1.0).then_inc(ax_ready, 1)
                act.wait_ge(ax_ready, 2)
                nc.scalar.activation(ax[:], ax[:], ACT.Ln, bias=1.0).then_inc(ln_ready, 1)
                act.wait_ge(cum_ready, 1)
                nc.scalar.activation(lin[:], cum[:], ACT.Exp).then_inc(eb_ready, 1)
                act.wait_ge(e_ready, 1)
                nc.scalar.activation(kd[:], kd[:], ACT.Exp)
                nc.scalar.activation(dec[:], blocks(cum[:], GC - 1, GC).rearrange("p (h n) t -> p h (n t)", h=4), ACT.Exp).then_inc(a_ready, 1)
                for j in range(TN):
                    for b in range(2):
                        act.wait_ge(tr_ready, 2 * j + b + 1)
                        act.wait_ge(stored[b], 16 * j)
                        nc.scalar.activation(tk[b][:], ps_w[:, b, :], ACT.Copy).then_inc(tr_copied, 1)
                for d in range(GC):
                    m = NB * (GC - d)
                    act.wait_ge(lag_ready, d + 1)
                    e = ex[d % 3][:].rearrange("p h t -> p (h t)")[:, 0:m]
                    nc.scalar.activation(e, e, ACT.Exp).then_inc(lag_exp, 1)

            @block.gpsimd
            def _(pool):
                for l in range(1, GC):
                    n = GN * (GC - l)
                    pool.wait_ge(av_ready, l + 1)
                    if l > 1:
                        pool.wait_ge(added, l - 1)
                    for i in range(4):
                        av = ax[:, i, 0:n].rearrange("p (n t) -> p n t", n=GN)
                        ov = o[:, i, :].rearrange("p (n t) -> p n t", t=GC)[:, :, l:GC]
                        r = nc.gpsimd.tensor_tensor(ov, ov, av, ALU.add)
                    r.then_inc(added, 1)

            @block.vector
            def _(dve):
                TT, TS, STT = nc.vector.tensor_tensor, nc.vector.tensor_scalar, nc.vector.scalar_tensor_tensor
                chain = Chain(dve, order)
                dve.wait_ge(x_ready, 1)
                for i in range(4):
                    r = TS(lin[:, i, :], ps[:, i, :], bl[:, i:i + 1], None, ALU.add)
                r.then_inc(lin_ready, 1)
                dve.wait_ge(lin_ready, 1)
                dve.wait_ge(ln_ready, 1)
                chain(STT(out=lin[:], in0=lin[:], scalar=0.0, in1=ax[:], op0=ALU.min, op1=ALU.subtract))
                chain(TS(lin[:], lin[:], 1.0 / 16, None, ALU.mult))
                for i in range(4):
                    r = nc.vector.tensor_tensor_scan(cum[:, i, :], c["chunk_start16"][:], lin[:, i, :], 0.0, ALU.mult, ALU.add)
                r.then_inc(cum_ready, 1)
                dve.wait_ge(cum_ready, 1)
                TT(blocks(kd[:], 0, GC), blocks(cum[:], GC - 1, GC).broadcast_to([P, NB, GC]), blocks(cum[:], 0, GC), ALU.subtract).then_inc(e_ready, 1)
                dve.wait_ge(a_ready, 1)
                TT(kd[:], kd[:], z[:, 4:8, :], ALU.mult).then_inc(k_ready, 1)
                chain(TS(z[:, 0:4, :], z[:, 0:4, :], K_SCALE, None, ALU.mult))
                def lag_view(d):
                    m = NB * (GC - d)
                    return ex[d % 3][:].rearrange("p h t -> p (h t)")[:, 0:m].rearrange("p (n t) -> p n t", n=NB)

                def decay_args(d):
                    if d >= 3:
                        dve.wait_ge(sum_ready, d - 2)
                    TT(lag_view(d), blocks(cum[:], d, GC), blocks(cum[:], 0, GC - d), ALU.subtract).then_inc(lag_ready, 1)

                decay_args(0)
                for d in range(GC + 1):
                    if d + 1 < GC:
                        decay_args(d + 1)
                    if d < GC:
                        e = lag_view(d)
                        dve.wait_ge(lag_exp, d + 1)
                        chain(TT(e, e, blocks(z[:, 4:8, :], 0, GC - d), ALU.mult))
                        TT(e, e, blocks(z[:, 0:4, :], d, GC), ALU.mult).then_inc(kq_ready, 1)
                    if d > 0:
                        l = d - 1
                        dve.wait_ge(sum_ready, l + 1)
                        n = GN * (GC - l)
                        if l > 1:
                            dve.wait_ge(added, l - 1)
                        for i in range(4):
                            pv = ps[:, i, 0:n].rearrange("p (n t) -> p n t", n=GN)
                            vv = z[:, 8 + i, :].rearrange("p (n t) -> p n t", t=GC)[:, :, 0:GC - l]
                            if l == 0:
                                av = o[:, i, :].rearrange("p (n t) -> p n t", t=GC)
                            else:
                                av = ax[:, i, 0:n].rearrange("p (n t) -> p n t", n=GN)
                            r = TT(av, pv, vv, ALU.mult)
                        r.then_inc(av_ready, 1)
                dve.wait_ge(eb_ready, 1)
                TT(z[:, 0:4, :], z[:, 0:4, :], lin[:], ALU.mult).then_inc(p_ready, 1)


def gla_state(nc, c, z, o, dec, tok_scr):
    RING = 4
    with stage(nc) as s:
        tk = [s.sb("tk", [GC, 2, 512]) for _ in range(RING)]
        st = [s.sb("st", [P, 4, P]) for _ in range(2)]
        ps_o = [s.ps("ps_o", [P, BANK]) for _ in range(2)]
        ps_s = [s.ps("ps_s", [P, BANK]) for _ in range(2)]
        tk_in = [s.sem("tk_in") for _ in range(RING)]
        kv_ready, o_ready, st_ready, added = (s.sem(n) for n in ("kv_ready", "o_ready", "st_ready", "added"))
        with nc.Block() as block:
            @block.sync
            def _(sp):
                with sp.Fori(0, GN // RING) as it:
                    for b in range(RING):
                        sp.wait_ge(kv_ready, it * RING)
                        sp.dma_start(tk[b][:], tok_scr[bass.ds((it * RING + b) * GC, GC)]).then_inc(tk_in[b], 16)

            @block.tensor
            def _(pe):
                with pe.Fori(0, GN // RING) as it:
                    for b in range(RING):
                        n = it * RING + b
                        pe.wait_ge(tk_in[b], it * 16 + 16)
                        pe.wait_ge(st_ready, n)
                        for h in range(4):
                            mm = nc.tensor.matmul(ps_s[b % 2][:, h * P:(h + 1) * P], tk[b][:, 0, h * P:(h + 1) * P],
                                                  tk[b][:, 1, h * P:(h + 1) * P], start=True, stop=True)
                        mm.then_inc(kv_ready, 1)
                        pe.wait_ge(st_ready, n + 1)
                        pe.wait_ge(added, it * RING + max(b - 1, 0))
                        for h in range(4):
                            mm = nc.tensor.matmul(ps_o[b % 2][:, h * GC:(h + 1) * GC], st[b % 2][:, h, :],
                                                  z[:, h, bass.ds(n * GC, GC)], start=True, stop=True)
                        mm.then_inc(o_ready, 1)

            @block.vector
            def _(dve):
                nc.vector.memset(st[0][:], 0.0).then_inc(st_ready, 1)
                dve.wait_ge(st_ready, 1)
                def add_sums(it, b):
                    n = it * RING + b
                    dve.wait_ge(o_ready, n + 1)
                    ov = o[:, :, bass.ds(n * GC, GC)]
                    nc.vector.tensor_tensor(ov, ps_o[b % 2][:, 0:4 * GC].rearrange("p (h t) -> p h t", h=4), ov, ALU.add).then_inc(added, 1)

                with dve.Fori(0, GN // RING) as it:
                    for b in range(RING):
                        n = it * RING + b
                        dve.wait_ge(kv_ready, n + 1)
                        dve.wait_ge(o_ready, n)
                        dve.wait_ge(st_ready, n + 1)
                        for h in range(4):
                            r = nc.vector.scalar_tensor_tensor(out=st[(b + 1) % 2][:, h, :], in0=st[b % 2][:, h, :],
                                                               scalar=dec[:, h, bass.ds(n, 1)], in1=ps_s[b % 2][:, h * P:(h + 1) * P],
                                                               op0=ALU.mult, op1=ALU.add)
                        r.then_inc(st_ready, 1)
                        if b > 0:
                            add_sums(it, b - 1)
                    add_sums(it, RING - 1)


def gdn_conv(nc, c, z):
    with stage(nc) as s:
        taps = s.sb("taps", [P, 12, 4])
        cv = [s.sb("cv", [P, T2]) for _ in range(2)]
        loaded, conv_ready, done = s.sem("loaded"), s.sem("conv_ready"), s.sem("done")
        order = [s.sem("order") for _ in range(2)]
        with nc.Block() as block:
            @block.sync
            def _(sp):
                sp.dma_start(taps[:], c["gdn_taps"]).then_inc(loaded, 16)

            @block.vector
            def _(dve):
                dve.wait_ge(loaded, 16)
                with dve.Fori(0, 6) as it:
                    for b in range(2):
                        i = it * 2 + b
                        dve.wait_ge(done, it * 2)
                        nc.vector.tensor_scalar(cv[b][:], z[:, i, 3:3 + T2], taps[:, i, 3:4], None, ALU.mult).then_inc(order[b], 1)
                    for j in range(3):
                        for b in range(2):
                            i = it * 2 + b
                            dve.wait_ge(order[b], it * 3 + j + 1)
                            r = nc.vector.scalar_tensor_tensor(out=cv[b][:], in0=z[:, i, j:j + T2], scalar=taps[:, i, j:j + 1], in1=cv[b][:],
                                                               op0=ALU.mult, op1=ALU.add)
                            r.then_inc(order[b] if j < 2 else conv_ready, 1)

            @block.scalar
            def _(act):
                with act.Fori(0, 6) as it:
                    for b in range(2):
                        act.wait_ge(conv_ready, it * 2 + b + 1)
                        nc.scalar.activation(z[:, it * 2 + b, 3:3 + T2], cv[b][:], ACT.Silu).then_inc(done, 1)


def gdn_matrices(nc, c, z, rows, yall, qk):
    L = LEVELS3
    E = range(2)
    with stage(nc) as s:
        bcol = s.sb("bcol", [DC, DN, 4])
        sel = [s.sb("sel", [4, P]) for _ in E]
        ks, qs = [s.sb("ks", [P, T2]) for _ in E], [s.sb("qs", [P, T2]) for _ in E]
        dec, nn, t1, xi, yi = ([s.sb(n, [DC, T2]) for _ in E] for n in ("dec", "nn", "t1", "xi", "yi"))
        nm = [s.sb("nm", [DC, L, T2]) for _ in E]
        psA, psB, psC = ([s.ps(n, [P, BANK]) for _ in E] for n in ("psA", "psB", "psC"))
        col_ready, col_copied = s.sem("col_ready"), s.sem("col_copied")
        names = ("fixed", "bc_ready", "arg_ready", "bd_read", "dec_ready", "prod_ready", "n_ready", "qk_done", "level_done",
                 "t1_ready", "t1_copied", "xy_ready", "xy_done", "order")
        (fixed, bc_ready, arg_ready, bd_read, dec_ready, prod_ready, n_ready, qk_done, level_done, t1_ready, t1_copied,
         xy_ready, xy_done, order) = ([s.sem(n) for _ in E] for n in names)

        def cols(n):
            return slice(n * DC, (n + 1) * DC)

        def chunked(ap):
            return ap.rearrange("p (n t) -> p n t", t=DC)

        with nc.Block() as block:
            @block.gpsimd
            def _(pool):
                with pool.Fori(0, 2) as it:
                    for e in E:
                        h = it * 2 + e
                        pool.wait_ge(prod_ready[e], it)
                        nc.gpsimd.tensor_copy(ks[e][:], z[:, h + 4, 3:3 + T2])
                        nc.gpsimd.tensor_copy(qs[e][:], z[:, h, 3:3 + T2])
                        nc.gpsimd.tensor_copy(sel[e][:], c["head_sel"][:, h, :]).then_inc(fixed[e], 1)
                    for l in range(L):
                        for e in E:
                            pool.wait_ge(n_ready[e], it + 1)
                            nc.gpsimd.tensor_tensor(nm[e][:, l, :], nn[e][:], c["level64"][:, l, :], ALU.mult).then_inc(level_done[e], 1)

            @block.tensor
            def _(pe):
                for n in range(DN):
                    mm = nc.tensor.transpose(psC[0][0:DC, 4 * n:4 * n + 4], rows[:, 3, cols(n)], c["ident"][0:4, 0:4])
                mm.then_inc(col_ready, 1)
                pe.wait_ge(col_copied, 1)
                with pe.Fori(0, 2) as it:
                    for e in E:
                        pe.wait_ge(fixed[e], it + 1)
                        pe.wait_ge(n_ready[e], it)
                        nc.tensor.matmul(psC[e][:], sel[e][:], rows[:, 3, :], start=True, stop=True).then_inc(bc_ready[e], 1)
                    for e in E:
                        pe.wait_ge(xy_done[e], it * L)
                        for n in range(DN):
                            nc.tensor.matmul(psA[e][0:DC, cols(n)], ks[e][:, cols(n)], ks[e][:, cols(n)], start=True, stop=True)
                            nc.tensor.matmul(psB[e][0:DC, cols(n)], ks[e][:, cols(n)], qs[e][:, cols(n)], start=True, stop=True)
                        pe.wait_ge(bd_read[e], it + 1)
                        nc.tensor.matmul(psC[e][:], sel[e][:], rows[:, 5, :], start=True, stop=True).then_inc(prod_ready[e], 1)
                    for l in range(L):
                        for e in E:
                            count = pe.compute_val(it * L + l + 1)
                            count_2 = pe.compute_val(it + 1)
                            count_3 = pe.compute_val(it * L + l)
                            settle(pe, col_copied)
                            pe.wait_ge(level_done[e], count)
                            pe.wait_ge(qk_done[e], count_2)
                            pe.wait_ge(xy_done[e], count_3)
                            for n in range(DN):
                                rhs = c["ident"][0:DC, 0:DC] if l == 0 else xi[e][:, cols(n)]
                                mm = nc.tensor.matmul(psA[e][0:DC, cols(n)], nm[e][:, l, cols(n)], rhs, start=True, stop=True)
                            mm.then_inc(t1_ready[e], 1)
                        if l == 0:
                            continue
                        for e in E:
                            count = pe.compute_val(it * (L - 1) + l)
                            settle(pe, col_copied)
                            pe.wait_ge(t1_copied[e], count)
                            for n in range(DN):
                                if l < L - 1:
                                    nc.tensor.matmul(psA[e][0:DC, cols(n)], yi[e][:, cols(n)], t1[e][:, cols(n)], start=True, stop=True)
                                mm = nc.tensor.matmul(psB[e][0:DC, cols(n)], t1[e][:, cols(n)], yi[e][:, cols(n)], start=True, stop=True)
                            mm.then_inc(xy_ready[e], 1)

            @block.scalar
            def _(act):
                act.wait_ge(col_ready, 1)
                nc.scalar.activation(bcol[:].rearrange("p n h -> p (n h)"), psC[0][0:DC, 0:4 * DN], ACT.Copy).then_inc(col_copied, 1)
                with act.Fori(0, 2) as it:
                    for e in E:
                        act.wait_ge(arg_ready[e], it + 1)
                        nc.scalar.activation(dec[e][:], dec[e][:], ACT.Exp).then_inc(dec_ready[e], 1)
                    for l in range(1, L):
                        for e in E:
                            act.wait_ge(t1_ready[e], it * L + l + 1)
                            nc.scalar.activation(t1[e][:], psA[e][0:DC, :], ACT.Copy).then_inc(t1_copied[e], 1)

            @block.vector
            def _(dve):
                TT = nc.vector.tensor_tensor
                dve.wait_ge(col_copied, 1)
                with dve.Fori(0, 2) as it:
                    chain = [Chain(dve, order[e], it, 2) for e in E]
                    for e in E:
                        h = it * 2 + e
                        dve.wait_ge(bc_ready[e], it + 1)
                        dve.wait_ge(qk_done[e], it)
                        TT(chunked(dec[e][:]), chunked(psC[e][0:DC, :]), bcol[:, :, bass.ds(h, 1)].broadcast_to([DC, DN, DC]),
                           ALU.subtract).then_inc(bd_read[e], 1)
                    for e in E:
                        dve.wait_ge(bd_read[e], it + 1)
                        TT(dec[e][:], dec[e][:], c["mask64"][:], ALU.add).then_inc(arg_ready[e], 1)
                    for e in E:
                        dve.wait_ge(dec_ready[e], it + 1)
                        dve.wait_ge(level_done[e], it * L)
                        chain[e](TT(nn[e][:], dec[e][:], c["neg_strict64"][:], ALU.mult))
                        dve.wait_ge(prod_ready[e], it + 1)
                        chain[e](TT(nn[e][:], psC[e][0:DC, :], nn[e][:], ALU.mult))
                        TT(nn[e][:], psA[e][0:DC, :], nn[e][:], ALU.mult).then_inc(n_ready[e], 1)
                        TT(qk[:, it * 2 + e, :], psB[e][0:DC, :], dec[e][:], ALU.mult).then_inc(qk_done[e], 1)
                    for l in range(L):
                        for e in E:
                            if l == 0:
                                dve.wait_ge(t1_ready[e], it * L + 1)
                                TT(xi[e][:], psA[e][0:DC, :], c["ident64"][:], ALU.add)
                                TT(yi[e][:], nm[e][:, 0, :], c["ident64"][:], ALU.add).then_inc(xy_done[e], 1)
                                continue
                            dve.wait_ge(xy_ready[e], it * (L - 1) + l)
                            if l < L - 1:
                                TT(xi[e][:], psA[e][0:DC, :], xi[e][:], ALU.add)
                                TT(yi[e][:], psB[e][0:DC, :], yi[e][:], ALU.add).then_inc(xy_done[e], 1)
                            else:
                                TT(yall[:, it * 2 + e, :], psB[e][0:DC, :], yi[e][:], ALU.add).then_inc(xy_done[e], 1)
                    for e in E:
                        chain[e].close()


def gdn_factors(nc, c, z, rows, kh, bv, dec):
    with stage(nc) as s:
        sel = s.sb("sel", [4, P])
        khf, bvf = s.sb("khf", [P, T2]), s.sb("bvf", [P, T2])
        ps_b = [s.ps("ps_b", [P, BANK]) for _ in range(4)]
        ps_t = [s.ps("ps_t", [P, 2, BANK]) for _ in range(2)]
        fixed, bc_ready, kh_ready, bv_ready, tr_ready, copied, done, order = (
            s.sem(n) for n in ("fixed", "bc_ready", "kh_ready", "bv_ready", "tr_ready", "copied", "done", "order"))
        with nc.Block() as block:
            @block.gpsimd
            def _(pool):
                with pool.Fori(0, 4) as h:
                    pool.wait_ge(bc_ready, h)
                    nc.gpsimd.tensor_copy(sel[:], c["head_sel"][:, h, :]).then_inc(fixed, 1)

            @block.tensor
            def _(pe):
                with pe.Fori(0, 4) as h:
                    pe.wait_ge(fixed, h + 1)
                    pe.wait_ge(done, h)
                    for b, r in enumerate((7, 5, 6, 4)):
                        mm = nc.tensor.matmul(ps_b[b][:], sel[:], rows[:, r, :], start=True, stop=True)
                    mm.then_inc(bc_ready, 1)
                    for b, (src, ready) in enumerate(((khf, kh_ready), (bvf, bv_ready))):
                        count = pe.compute_val(h + 1)
                        count_2 = pe.compute_val(h * 2)
                        settle(pe, bc_ready)
                        pe.wait_ge(ready, count)
                        pe.wait_ge(copied, count_2)
                        for n in range(DN):
                            mm = nc.tensor.transpose(ps_t[b][0:DC, n // 4, (n % 4) * P:(n % 4 + 1) * P], src[:, n * DC:(n + 1) * DC], c["ident"][:])
                        mm.then_inc(tr_ready, 1)

            @block.scalar
            def _(act):
                with act.Fori(0, 4) as h:
                    for b, dst in enumerate((kh, bv)):
                        act.wait_ge(tr_ready, h * 2 + b + 1)
                        nc.scalar.activation(dst[:, h, :].rearrange("p (a t) -> p a t", a=2), ps_t[b][0:DC, :, :], ACT.Copy).then_inc(copied, 1)

            @block.vector
            def _(dve):
                TT = nc.vector.tensor_tensor
                with dve.Fori(0, 4) as h:
                    dve.wait_ge(bc_ready, h + 1)
                    dve.wait_ge(tr_ready, h * 2)
                    kz, qz, vz = z[:, h + 4, 3:3 + T2], z[:, h, 3:3 + T2], z[:, h + 8, 3:3 + T2]
                    TT(khf[:], ps_b[0][:], kz, ALU.mult).then_inc(kh_ready, 1)
                    TT(bvf[:], ps_b[1][:], vz, ALU.mult).then_inc(bv_ready, 1)
                    dve.wait_ge(kh_ready, h + 1)
                    TT(kz, ps_b[2][:], kz, ALU.mult)
                    TT(qz, ps_b[3][:], qz, ALU.mult)
                    nc.vector.tensor_copy(dec[:, h, :], ps_b[3][:].rearrange("p (n t) -> p n t", t=DC)[:, :, DC - 1]).then_inc(done, 1)


def gdn_chunks(nc, c, z, yall, qk, kh, bv, dec, o):
    with stage(nc) as s:
        st = s.sb("st", [P, 4, P])
        kb = [s.sb("kb", [P, 4, DC]) for _ in range(2)]
        kt = [s.sb("kt", [DC, 4, P]) for _ in range(2)]
        yt = [s.sb("yt", [DC, 4, DC]) for _ in range(2)]
        rr, vn = s.sb("rr", [DC, 512]), s.sb("vn", [DC, 512])
        ps_r, ps_v, ps_s = (s.ps(n, [P, BANK]) for n in ("ps_r", "ps_v", "ps_s"))
        ps_o = s.ps("ps_o", [P, BANK])
        fixed, r_prod, r_ready, v_prod, v_ready, o_ready, s_prod, o_done, st_ready = (
            s.sem(n) for n in ("fixed", "r_prod", "r_ready", "v_prod", "v_ready", "o_ready", "s_prod", "o_done", "st_ready"))
        with nc.Block() as block:
            @block.gpsimd
            def _(pool):
                with pool.Fori(0, DN // 2) as it:
                    for b in range(2):
                        n = it * 2 + b
                        pool.wait_ge(s_prod, it * 2)
                        nc.gpsimd.tensor_copy(kb[b][:], z[:, 4:8, bass.ds(n * DC + 3, DC)])
                        nc.gpsimd.tensor_copy(kt[b][:], kh[:, :, bass.ds(n * P, P)])
                        nc.gpsimd.tensor_copy(yt[b][:], yall[:, :, bass.ds(n * DC, DC)]).then_inc(fixed, 1)

            @block.tensor
            def _(pe):
                with pe.Fori(0, DN // 2) as it:
                    for b in range(2):
                        n = it * 2 + b
                        pe.wait_ge(fixed, n + 1)
                        pe.wait_ge(st_ready, n + 1)
                        for h in range(4):
                            mm = nc.tensor.matmul(ps_r[0:DC, h * P:(h + 1) * P], kb[b][:, h, :], st[:, h, :], start=True, stop=True)
                        mm.then_inc(r_prod, 1)
                        count = pe.compute_val(n + 1)
                        settle(pe, fixed)
                        pe.wait_ge(r_ready, count)
                        for h in range(4):
                            mm = nc.tensor.matmul(ps_v[0:DC, h * P:(h + 1) * P], yt[b][:, h, :], rr[:, h * P:(h + 1) * P], start=True, stop=True)
                        mm.then_inc(v_prod, 1)
                        pe.wait_ge(v_ready, n + 1)
                        pe.wait_ge(o_done, n)
                        for h in range(4):
                            out = ps_o[:, h * DC:(h + 1) * DC]
                            nc.tensor.matmul(out, st[:, h, :], z[:, h, bass.ds(n * DC + 3, DC)], start=True, stop=False)
                            mm = nc.tensor.matmul(out, vn[:, h * P:(h + 1) * P], qk[:, h, bass.ds(n * DC, DC)], start=False, stop=True)
                        mm.then_inc(o_ready, 1)
                        for h in range(4):
                            mm = nc.tensor.matmul(ps_s[:, h * P:(h + 1) * P], kt[b][:, h, :], vn[:, h * P:(h + 1) * P], start=True, stop=True)
                        mm.then_inc(s_prod, 1)

            @block.scalar
            def _(act):
                with act.Fori(0, DN) as n:
                    act.wait_ge(v_prod, n + 1)
                    nc.scalar.activation(vn[:], ps_v[0:DC, :], ACT.Copy).then_inc(v_ready, 1)
                    act.wait_ge(o_ready, n + 1)
                    nc.scalar.activation(o[:, :, bass.ds(n * DC, DC)], ps_o[:, 0:4 * DC].rearrange("p (h t) -> p h t", h=4), ACT.Copy).then_inc(o_done, 1)

            @block.vector
            def _(dve):
                nc.vector.memset(st[:], 0.0).then_inc(st_ready, 1)
                with dve.Fori(0, DN) as n:
                    dve.wait_ge(r_prod, n + 1)
                    nc.vector.tensor_tensor(rr[:].rearrange("p (h v) -> p h v", h=4), ps_r[0:DC, :].rearrange("p (h v) -> p h v", h=4),
                                            bv[:, :, bass.ds(n * P, P)], ALU.add).then_inc(r_ready, 1)
                    dve.wait_ge(s_prod, n + 1)
                    dve.wait_ge(st_ready, n + 1)
                    for h in range(4):
                        r = nc.vector.scalar_tensor_tensor(out=st[:, h, :], in0=st[:, h, :], scalar=dec[:, h, bass.ds(n, 1)],
                                                           in1=ps_s[:, h * P:(h + 1) * P], op0=ALU.mult, op1=ALU.add)
                    r.then_inc(st_ready, 1)


def silu_tiles(nc, x):
    with stage(nc):
        with nc.Block() as block:
            @block.scalar
            def _(act):
                with act.Fori(0, x.shape[1]) as i:
                    nc.scalar.activation(x[:, i, :], x[:, i, :], ACT.Silu)


def zero(nc, x):
    with stage(nc):
        with nc.Block() as block:
            @block.vector
            def _(dve):
                nc.vector.memset(x, 0.0)


def copy_tile(nc, dst, src):
    with stage(nc):
        with nc.Block() as block:
            @block.vector
            def _(dve):
                nc.vector.tensor_copy(dst, src)



def resident(nc, memory, name, shape):
    return memory.enter_context(nc.sbuf_tensor(f"{name}_{nc.next_id()}", shape, F32))


def resident_pair(nc, memory, name, shape):
    return tuple(memory.enter_context(nc.sbuf_tensor(f"{name}_{part}_{nc.next_id()}", shape, F32R)) for part in ("hi", "lo"))


def with_constants(nc, memory, a, names):
    c = dict(a)
    for name in names:
        c[name] = resident(nc, memory, name, a[name].shape)
    load(nc, [(c[name][:], a[name]) for name in names])
    return c


def first_block(nc, a, x, ones_ident):
    chunks = nc.dram_tensor("rwkv_chunks", (RN, P, 8, 5, RC), F32).ap()
    bonus = nc.dram_tensor("rwkv_bonus", (P, 8, T1), F32).ap()
    gate = nc.dram_tensor("rwkv_gate", (P, 8, T1), F32).ap()

    def act(memory, name, k, t=T1):
        return resident(nc, memory, name, [P, k, t])
    with ExitStack() as m:
        c = with_constants(nc, m, {**a, **ones_ident}, CONSTANTS[1])
        h, y = resident_pair(nc, m, "h", [P, 8, T1]), act(m, "y", 8)
        rmsnorm(nc, c["ones"], x, a["norm_mix_1"], h, T1, 1e-5, src=a["x_1"])
        with ExitStack() as m2:
            decay = resident(nc, m2, "chunk_decay", [P, 8, RN])
            with ExitStack() as m3:
                p = act(m3, "p", 27, T1 + 1)
                zero(nc, p[:, :, 0:1])
                dense(nc, a["w_rwkv_1"], h, p[:, :, 1:T1 + 1], T1, func=ACT.Copy, n_body=3)
                rwkv_lora_inputs(nc, c, p)
                rwkv_prepare(nc, c, p, chunks, decay, bonus, gate)
            rwkv_chunks(nc, c, y, chunks, decay)
        rwkv_finish(nc, c, y, bonus, gate)
        o = act(m, "o", 8)
        with ExitStack() as m2:
            p = act(m2, "p", 24)
            dense(nc, a["w_qkv_1"], h, p, T1, func=ACT.Copy, n_body=4)
            diff_attention(nc, c, p, o)
        head_rms(nc, c["ones"], o, a["subln_1"], T1, 1e-5, factor=1 - LAMBDA_INIT)
        with ExitStack() as m2:
            gates = act(m2, "gates", 16)
            dense(nc, a["w_gates_1"], h, gates, T1, func=ACT.Sigmoid, n_body=4, ring=2)
            dense(nc, a["rwkv_out_1"], y, y, T1, gate=gates[:, 0:8, :], n_body=4, ring=2)
            dense(nc, a["diff_out_1"], o, y, T1, gate=gates[:, 8:16, :], residual=y, n_body=4, ring=2)
        dense(nc, a["w_out_1"], y, x, T1, residual=x, n_body=4, ring=4)
    mlp(nc, ones_ident, x, a["norm_mlp_1"], a["mlp_in_1"], a["mlp_out_1"], T1, 1e-5)
    rmsnorm(nc, ones_ident["ones"], x, a["norm_final_1"], x, T1, 1e-5)


def mlp(nc, c, x, norm, w_in, w_out, T, eps):
    N, KG = w_in.shape[0] // 2, w_out.shape[1] // 2
    with ExitStack() as m:
        h, hidden = resident_pair(nc, m, "h", [P, 8, T]), resident_pair(nc, m, "hidden", [P, N, T])
        rmsnorm(nc, c["ones"], x, norm, h, T, eps)
        for half in range(2):
            dense(nc, w_in[half * N:(half + 1) * N], h, hidden, T, func="relu2", n_body=4, ring=4)
            dense(nc, w_out[:, half * KG:(half + 1) * KG], hidden, x, T, residual=x, n_body=4, ring=4)


def second_block(nc, a, x, ones_ident):
    bias_scr = nc.dram_tensor("bias_by_distance", (8, 640), F32).ap()
    bias_rows = nc.dram_tensor("bias_rows", (8, P, T2), F32).ap()

    def act(memory, name, k, t=T2):
        return resident(nc, memory, name, [P, k, t])
    with ExitStack() as m:
        c = with_constants(nc, m, {**a, **ones_ident}, CONSTANTS[2])
        h, o = resident_pair(nc, m, "h", [P, 8, T2]), act(m, "o", 4)
        rmsnorm(nc, c["ones"], x, a["norm_mix_2"], h, T2, 1e-6)
        glu, taps = resident(nc, m, "glu", [P, 4, CONV_TAPS - 1 + T2]), resident(nc, m, "taps", [P, 4, CONV_TAPS + 3])
        with ExitStack() as m2:
            z = act(m2, "z", 20)
            bias_cmp = resident(nc, m2, "bias_cmp", [P, 55, 8])
            k_cmp, v_cmp = resident(nc, m2, "k_cmp", [P, NC2]), resident(nc, m2, "v_cmp", [NC2, P])
            with ExitStack() as m3:
                cmp_w = {n: [resident(nc, m3, n, shape) for _ in range(2)]
                         for n, shape in (("cmp_pe", [P, 32, NC2]), ("cmp_w1", [P, 32, 256]), ("cmp_w2", [P, 2, 64]))}
                loads = []
                for b in range(2):
                    loads += [(cmp_w["cmp_pe"][b][:], a["cmp_pe"][b]), (cmp_w["cmp_w2"][b][:], a["cmp_w2"][b])]
                    loads += [(cmp_w["cmp_w1"][b][64 * g:64 * g + 64, 8 * i:8 * i + 8, :], a["cmp_w1"][b][:, 8 * i:8 * i + 8, :])
                              for g in range(2) for i in range(4)]
                dense(nc, a["w_in_2"], h, z, T2, func=ACT.Copy, n_body=4, ring=2, loads=loads)
                compress(nc, cmp_w, c["ident"], z[:, 12:18, :], k_cmp, v_cmp)
            conv_inputs(nc, c, z[:, 0:8, :], glu, taps)
            bias_tables(nc, c, bias_scr, bias_rows, bias_cmp)
            nsa_attention(nc, c, z[:, 8:12, :], z[:, 12:18, :], z[:, 18, :], bias_rows, bias_cmp, k_cmp, v_cmp, o)
        mixed, conv = act(m, "mixed", 8), act(m, "conv", 4)
        with ExitStack() as m2:
            gates = act(m2, "gates", 16)
            dense(nc, a["w_gates_2"], h, gates, T2, func=ACT.Sigmoid, n_body=4, side=conv_steps(nc, glu, taps, conv, 4))
            conv_norm(nc, c, taps, conv)
            dense(nc, a["conv_out_2"], conv, mixed, T2, gate=gates[:, 0:8, :], n_body=4)
            dense(nc, a["attn_out_2"], o, mixed, T2, gate=gates[:, 8:16, :], residual=mixed, n_body=4)
        dense(nc, a["w_out_2"], mixed, x, T2, residual=x, n_body=4)
    with ExitStack() as m:
        h, u = resident_pair(nc, m, "h", [P, 8, T2]), resident_pair(nc, m, "u", [P, 22, T2])
        rmsnorm(nc, ones_ident["ones"], x, a["norm_ffn_2"], h, T2, 1e-6)
        ffn_up(nc, a, a["ffn_up_2"], h, u)
        dense(nc, a["ffn_down_2"], u, x, T2, residual=x, n_body=4, ring=4)
    with ExitStack() as m:
        h, gate, p = resident_pair(nc, m, "h", [P, 8, T2]), act(m, "gate", 8), act(m, "p", 2)
        load(nc, [(p[:], a["p_2"])])
        rmsnorm(nc, ones_ident["ones"], x, a["norm_ple_2"], h, T2, 1e-6)
        dense(nc, a["ple_gate_2"], h, gate, T2, func=ACT.Sigmoid, n_body=4)
        dense(nc, a["ple_2"], p, x, T2, gate=gate, residual=x, n_body=4)
        rmsnorm(nc, ones_ident["ones"], x, a["norm_final_2"], x, T2, 1e-6)


def third_block(nc, a, x, ones_ident, out):
    gla_tok = nc.dram_tensor("gla_by_token", (T2, 2, 512), F32).ap()

    def act(memory, name, k, t=T2):
        return resident(nc, memory, name, [P, k, t])
    with ExitStack() as m:
        h = act(m, "h", 8)
        o_m, o_l, o_d = act(m, "o_m", 4), act(m, "o_l", 4), act(m, "o_d", 4)
        rmsnorm(nc, ones_ident["ones"], x, a["norm_mix_3"], h, T2, 1e-6)
        with ExitStack() as mc:
            c = with_constants(nc, mc, {**a, **ones_ident}, CONSTANTS[3])
            low_rank, rows = act(mc, "low_rank", 1), resident(nc, mc, "rows", [4, 8, T2])
            with ExitStack() as m2:
                z = act(m2, "z", 18)
                dense(nc, a["w_mlstm_3"], h, z, T2, func=ACT.Copy, n_body=3)
                copy_tile(nc, low_rank[:, 0, :], z[:, 17, :])
                gate_rows(nc, c, z[:, 16, :], rows)
                mlstm(nc, c, z, rows, o_m)
            head_rms(nc, c["ones"], o_m, a["norm_mlstm_3"], T2, 1e-6)
            with ExitStack() as m2:
                z, decay = act(m2, "z", 16), resident(nc, m2, "decay", [P, 4, GN])
                dense(nc, a["w_gla_in_3"], h, z, T2, func=ACT.Copy, n_body=4, ring=2)
                gla_intra(nc, c, z[:], low_rank[0:16, 0, :], o_l, decay, gla_tok)
                gla_state(nc, c, z, o_l, decay, gla_tok)
                silu_tiles(nc, z[:, 12:16, :])
                head_rms(nc, c["ones"], o_l, a["norm_gla_3"], T2, 1e-6, gate=z[:, 12:16, :])
            with ExitStack() as m2:
                z, decay = act(m2, "z", 16, T2 + 3), resident(nc, m2, "decay", [P, 4, DN])
                zero(nc, z[:, :, 0:3])
                dense(nc, a["w_gdn_3"], h, z[:, :, 3:T2 + 3], T2, func=ACT.Copy, n_body=4, ring=2)
                gdn_conv(nc, c, z)
                head_rms(nc, c["ones"], z[:, 0:8, 3:T2 + 3], a["l2_weight"], T2, 1e-6, mean=1.0)
                inverse, qk = resident(nc, m2, "inverse", [DC, 4, T2]), resident(nc, m2, "qk", [DC, 4, T2])
                gdn_matrices(nc, c, z, rows, inverse, qk)
                kh, bv = resident(nc, m2, "kh", [DC, 4, DN * P]), resident(nc, m2, "bv", [DC, 4, DN * P])
                gdn_factors(nc, c, z, rows, kh, bv, decay)
                gdn_chunks(nc, c, z, inverse, qk, kh, bv, decay, o_d)
                silu_tiles(nc, z[:, 12:16, 3:T2 + 3])
                head_rms(nc, c["ones"], o_d, a["norm_gdn_3"], T2, 1e-6, gate=z[:, 12:16, 3:T2 + 3])
        with ExitStack() as m2:
            gates = act(m2, "gates", 24)
            dense(nc, a["w_gates_3"], h, gates, T2, func=ACT.Sigmoid, n_body=4, ring=2)
            for n, o in enumerate((o_m, o_l, o_d)):
                dense(nc, a["up_3"][n], o, h, T2, gate=gates[:, 8 * n:8 * n + 8, :], residual=h if n > 0 else None, n_body=4)
        dense(nc, a["w_out_3"], h, x, T2, residual=x, n_body=4)
    mlp(nc, ones_ident, x, a["norm_mlp_3"], a["mlp_in_3"], a["mlp_out_3"], T2, 1e-6)
    rmsnorm(nc, ones_ident["ones"], x, a["norm_final_3"], x, T2, 1e-6, dst=out)


def program(nc, a, out):
    with ExitStack() as memory:
        common = {n: resident(nc, memory, n, a[n].shape) for n in CONSTANTS[0]}
        load(nc, [(common[n][:], a[n]) for n in CONSTANTS[0]])
        x = resident(nc, memory, "x", [P, 8, T1])
        first_block(nc, a, x, common)
        x = x[:, :, T1 - T2:T1]
        second_block(nc, a, x, common)
        third_block(nc, a, x, common, out)



CONSTANTS = {
    0: ["ones", "ident"],
    1: ["blk64", "mean64", "chunk_start66", "causal66", "level66", "ident66", "mask88", "rope_cos", "rope_sin", "rope_swap"],
    2: ["row_valid", "upside_down"],
    3: ["mask_st", "head_sel", "chunk_start64", "chunk_start16", "mask64", "neg_strict64", "ident64", "level64"],
}


def bucket_one_hot(distance):
    n = np.maximum(distance, 0)
    large = 16 + (np.log(np.maximum(n, 16).astype(np.float32) / np.float32(16)) / np.float32(math.log(8))
                  * np.float32(16)).astype(np.int32)
    bucket = np.where(distance < 0, 32, np.where(n < 16, n, np.minimum(large, 31)))
    return (np.arange(33)[:, None] == bucket[None, :]).astype(np.float32)


def level_masks(size, levels):
    s_, t_ = np.mgrid[0:size, 0:size]
    out = np.zeros((size, levels, size), np.float32)
    for l in range(levels):
        w = 1 << l
        out[:, l] = (s_ // (2 * w) == t_ // (2 * w)) & ((s_ // w) % 2 == 0) & ((t_ // w) % 2 == 1)
    return out


def constants():
    f = np.float32
    eye = np.eye(P, dtype=f)
    heads2 = np.kron(np.eye(2), np.ones((64, 64))).astype(f)
    out = {"ones": np.ones((P, P), f), "ident": eye, "blk64": heads2, "mean64": heads2 / f(64)}
    for name, t, n in (("chunk_start66", T1, RC), ("chunk_start64", T2, DC), ("chunk_start16", T2, GC)):
        out[name] = np.ones((P, t), f)
        out[name][:, ::n] = 0
    s_, t_ = np.mgrid[0:RC, 0:RC]
    out["causal66"] = np.tile(np.concatenate([s_ < t_, s_ <= t_], 1).astype(f), (1, 2))
    out["level66"] = np.repeat(level_masks(RC, LEVELS1)[:, :, None, :], 4, 2)
    out["ident66"] = np.tile(np.eye(RC, dtype=f)[:, None, :], (1, 4, 1))
    off = T1 - QT
    out["mask88"] = np.where(np.arange(T1 + off)[None, :] - off <= np.arange(QT)[:, None], 0, NEG).astype(f)
    inv = (500000.0 ** (-np.arange(0, 16, 2, dtype=f) / f(16))).astype(f)
    angle = (np.arange(T1, dtype=f)[:, None] * inv[None, :]).T
    cos, sin, swap = np.ones((P, T1), f), np.zeros((P, T1), f), np.zeros((P, P), f)
    for b in (0, 64):
        for half in (0, 8):
            cos[b + half:b + half + 8], sin[b + half:b + half + 8] = np.cos(angle), np.sin(angle)
        for j in range(8):
            swap[b + 8 + j, b + j], swap[b + j, b + 8 + j] = -1, 1
    out["rope_cos"], out["rope_sin"], out["rope_swap"] = cos, sin, swap
    out["buckets_rev"] = bucket_one_hot(511 - np.arange(640))
    out["buckets_fwd"] = bucket_one_hot(np.arange(1024) - 511)
    out["upside_down"] = eye[::-1]
    out["row_valid"] = (np.arange(P)[:, None] >= 31).astype(f)
    s_, t_ = np.mgrid[0:P, 0:T2]
    out["mask_st"] = np.where(s_ <= t_, 0, NEG).astype(f)
    out["head_sel"] = np.repeat(np.eye(4, dtype=f)[:, :, None], P, 2)
    s_, t_ = np.mgrid[0:DC, 0:DC]
    out["mask64"] = np.tile(np.where(s_ <= t_, 0, NEG).astype(f), (1, DN))
    out["neg_strict64"] = np.tile(-(s_ < t_).astype(f), (1, DN))
    out["ident64"] = np.tile(np.eye(DC, dtype=f), (1, DN))
    out["level64"] = np.tile(level_masks(DC, LEVELS3), (1, 1, DN))
    out["l2_weight"] = np.repeat(np.array([[K_SCALE] * 4 + [1.0] * 4], f), P, 0)
    return out


def tiles(w, kp=8):
    k, n = w.shape
    return w.reshape(k // (P * kp), kp, P, n // P, P).transpose(3, 0, 2, 1, 4)


def by_feature(x):
    return x.T.reshape(-1, P, x.shape[0]).transpose(1, 0, 2)


def column(v):
    return v.reshape(-1, P).T


def blank(rows, cols):
    return np.zeros((rows, cols), np.float32)


def arguments(i):
    cat = np.concatenate
    a = constants()
    w, mu = i["w_in"][0], i["rwkv_mu"][0]
    a["x_1"] = by_feature(cat([i["meta_tokens"], i["x"][0]], 0))
    a["norm_mix_1"], a["norm_mlp_1"], a["norm_final_1"] = column(i["norm_mix_w"][0]), column(i["norm_mlp_w"][0]), column(i["final_norm_w"])
    a["w_rwkv_1"] = tiles(cat([w[:, :3360], blank(1024, 96)], 1))
    a["w_qkv_1"], a["w_gates_1"] = tiles(w[:, 3360:6432]), tiles(w[:, 6432:])
    a["lora_mu"] = column(cat([mu[3072:], np.zeros(96, np.float32)]))
    vectors = [mu[:1024], mu[1024:2048], mu[2048:3072]] + [
        i[n][0].reshape(-1) for n in ("rwkv_w0", "rwkv_a0", "rwkv_k_k", "rwkv_k_a", "rwkv_r_k")]
    a["rwkv_vec"] = np.stack(vectors).reshape(8, 8, P).transpose(1, 2, 0)
    up = cat([i["rwkv_w2"][0], i["rwkv_a2"][0], i["rwkv_g2"][0], blank(96, 1024)], 0)
    a["lora_up"] = up.reshape(3, P, 8, P).transpose(2, 1, 0, 3)
    a["rwkv_ln"] = np.stack([i["rwkv_ln_w"][0], i["rwkv_ln_b"][0]]).reshape(2, 8, P).transpose(2, 0, 1)
    a["lambda_qk"] = np.stack([i[n][0] for n in ("diff_lq1", "diff_lq2", "diff_lk1", "diff_lk2")], 1)
    a["subln_1"] = np.tile(column(i["diff_subln_w"][0]), (1, 8))
    for name, key in (("rwkv_out_1", "rwkv_w_o"), ("diff_out_1", "diff_w_o"), ("w_out_1", "w_out"), ("mlp_in_1", "mlp_w1"),
                      ("mlp_out_1", "mlp_w2")):
        a[name] = tiles(i[key][0])
    w = i["w_in_2"][0]
    heads = [j + 4 * e for j in range(4) for e in range(2)]
    q_cols = [64 * h + d for h in heads for d in range(64)]
    gate_cols = [2304 + 3 * h + b for h in heads for b in range(3)]
    a["w_in_2"] = tiles(cat([w[:, :1024], w[:, [1024 + q for q in q_cols]], w[:, 1536:2304], w[:, gate_cols], blank(1024, 232)], 1))
    a["w_gates_2"] = tiles(w[:, 2328:])
    vectors = cat([i["conv_dw_w_2"][0], i["conv_dw_b_2"], i["conv_ln_g_2"], i["conv_ln_b_2"]], 0)
    a["conv_taps"] = vectors.reshape(-1, 4, P).transpose(2, 1, 0)
    a["conv_out_2"], a["attn_out_2"] = tiles(i["w_conv_out_2"][0], 4), tiles(i["w_attn_out_2"][0][q_cols], 4)
    a["rel_bias"] = i["rel_bias_2"]
    pe = np.stack([i["cmp_pe_k_2"][0].T, i["cmp_pe_v_2"][0].T])
    a["cmp_pe"] = np.repeat(cat([pe, pe], 1)[..., None], NC2, -1)
    a["cmp_w1"] = np.stack([i["w_ck1_2"][0], i["w_cv1_2"][0]]).reshape(2, 32, 64, 256).transpose(0, 2, 1, 3)
    a["cmp_w2"] = np.stack([i["w_ck2_2"][0], i["w_cv2_2"][0]]).reshape(2, 2, P, 64).transpose(0, 2, 1, 3)
    a["w_out_2"], a["ple_gate_2"], a["ple_2"] = tiles(i["w_out_2"][0]), tiles(i["w_ple_gate_2"][0]), tiles(i["w_ple_2"][0], 2)
    up = tiles(i["w_up_2"][0])[:, 0]
    a["ffn_up_2"] = np.stack([up[:22], up[22:]], 1)
    a["ffn_taps"] = cat([i["ffn_dw_w_2"][0], i["ffn_dw_b_2"]], 0).reshape(4, 44, P).transpose(2, 1, 0)
    a["ffn_down_2"] = tiles(i["w_down_2"][0], 11)
    a["p_2"] = by_feature(i["p_2"][0, 0])
    for name, key in (("norm_mix_2", "norm_mix_2"), ("norm_ffn_2", "norm_ffn_2"), ("norm_ple_2", "norm_ple_2"), ("norm_final_2", "norm_final_2")):
        a[name] = column(i[key])
    w = i["w_in_3"][0]
    small = [part for at in (2048, 2052, 6168, 6172) for part in (w[:, at:at + 4], blank(1024, 28))]
    a["w_mlstm_3"] = tiles(cat([w[:, :2048]] + small + [w[:, 4104:4120], blank(1024, 112)], 1))
    a["w_gla_in_3"], a["w_gdn_3"], a["w_gates_3"] = tiles(w[:, 2056:4104]), tiles(w[:, 4120:6168]), tiles(w[:, 6176:])
    a["gate_bias"] = np.stack([i["b_if_3"][0, :4], i["b_if_3"][0, 4:], i["dt_bias_3"][0], i["a_log_3"][0]], 1)
    a["gla_w"], a["gla_b"] = i["w_gla_lr_3"][0], column(i["b_gla_3"])
    a["gdn_taps"] = i["conv_gdn_3"][0].reshape(4, 12, P).transpose(2, 1, 0)
    for name, key in (("norm_mix_3", "g_norm_mix_3"), ("norm_mlp_3", "g_norm_mlp_3"), ("norm_mlstm_3", "g_head_mlstm_3"),
                      ("norm_gla_3", "g_head_gla_3"), ("norm_gdn_3", "g_head_gdn_3"), ("norm_final_3", "g_final_3")):
        a[name] = column(i[key])
    a["up_3"] = np.stack([tiles(i["w_up_3"][0, n], 4) for n in range(3)])
    a["w_out_3"], a["mlp_in_3"], a["mlp_out_3"] = tiles(i["w_out_3"][0]), tiles(i["w_mlp_in_3"][0]), tiles(i["w_mlp_out_3"][0])
    return a


def kernel(**inputs):
    import concourse.bacc as bacc
    from concourse.bass_utils import run_bass_kernel_spmd

    nc = bacc.Bacc("TRN2", target_bir_lowering=False, num_devices=1)
    arrays, args = {}, {}
    for name, value in arguments({n: np.asarray(v) for n, v in inputs.items()}).items():
        value = np.ascontiguousarray(value)
        arrays[f"in_{name}"] = value
        args[name] = nc.dram_tensor(f"in_{name}", value.shape, mybir.dt.from_np(value.dtype), kind="ExternalInput").ap()
    out = nc.dram_tensor("out_features", (P, 8, T2), F32, kind="ExternalOutput").ap()
    program(nc, args, out)
    result = run_bass_kernel_spmd(nc, [arrays], core_ids=[0]).results[0]["out_features"]
    return result.transpose(2, 1, 0).reshape(1, T2, 8 * P)
```
